# Optimizing a Trainium2 kernel written in Bass

```python
import jax
import jax.numpy as jnp
from jax import lax
import numpy as np

D_MODEL = 1024
BATCH = 1
SEQ = 512
DEPTH = 2

MEM_LEN = 256
EPS = 1e-6
F32 = jnp.float32

GLA_HEADS = 6
GLA_DK = 32
GLA_DV = 64
GLA_RANK = 16
GLA_TAU = 16.0
GLA_CHUNK = 64

RET_HEADS = 6
RET_DK = 32
RET_DV = 64
RET_CHUNK = 128
ROPE_BASE = 10000.0

ML_HEADS = 4
ML_DK = 64
ML_DV = 64
ML_CHUNK = 64
ML_CONV = 4
ML_FBIAS_LO = 3.0
ML_FBIAS_HI = 6.0

D_MIX = GLA_HEADS * GLA_DV + RET_HEADS * RET_DV + ML_HEADS * ML_DV
IN_SIZES = (
    GLA_HEADS * GLA_DK, GLA_HEADS * GLA_DK, GLA_HEADS * GLA_DV, GLA_RANK, GLA_HEADS * GLA_DV,
    RET_HEADS * RET_DK, RET_HEADS * RET_DK, RET_HEADS * RET_DV, RET_HEADS * RET_DV,
    ML_HEADS * ML_DK, ML_HEADS * ML_DK, ML_HEADS * ML_DV, ML_HEADS * ML_DV, ML_HEADS, ML_HEADS,
)
D_IN = sum(IN_SIZES)

XA_HEADS = 4
XA_DH = D_MODEL // XA_HEADS
D_FF = ((8 * D_MODEL // 3 + 127) // 128) * 128
MAX_POS_OFFSET = 1024

kernel_name = "hybrid_gla_retnet_mlstm_macaron"

def rmsnorm(x, g):
    xf = x.astype(F32)
    y = xf * lax.rsqrt(jnp.mean(xf * xf, axis=-1, keepdims=True) + EPS)
    return (y * g.astype(F32)).astype(x.dtype)

def head_rmsnorm(x, g):
    b, s, h, d = x.shape
    xf = x.astype(F32)
    y = xf * lax.rsqrt(jnp.mean(xf * xf, axis=-1, keepdims=True) + EPS)
    return y.reshape(b, s, h * d) * g.astype(F32)

def head_groupnorm(x, g):
    b, s, h, d = x.shape
    xf = x.astype(F32)
    mu = jnp.mean(xf, axis=-1, keepdims=True)
    xc = xf - mu
    y = xc * lax.rsqrt(jnp.mean(xc * xc, axis=-1, keepdims=True) + EPS)
    return y.reshape(b, s, h * d) * g.astype(F32)

def swiglu_ffn(x, w_gu, w_down):
    a, g = jnp.split(x @ w_gu, 2, axis=-1)
    return (jax.nn.silu(a) * g) @ w_down

def _to_chunks(t, c):
    b, s, h, d = t.shape
    return t.reshape(b, s // c, c, h, d).transpose(1, 0, 3, 2, 4)

def _from_chunks(t):
    n, b, h, c, d = t.shape
    return t.transpose(1, 0, 3, 2, 4).reshape(b, n * c, h, d)

def rotary(x, positions):
    half = x.shape[-1] // 2
    inv_freq = 1.0 / (ROPE_BASE ** jnp.linspace(0.0, 1.0, half, dtype=F32))
    ang = positions.astype(F32)[..., None] * inv_freq
    cos = jnp.cos(ang)[:, :, None, :]
    sin = jnp.sin(ang)[:, :, None, :]
    x1 = x[..., :half].astype(F32)
    x2 = x[..., half:].astype(F32)
    return jnp.concatenate([x1 * cos - x2 * sin, x1 * sin + x2 * cos], axis=-1).astype(x.dtype)

def causal_dwconv(x, w):
    k = w.shape[0]
    return lax.conv_general_dilated(
        x, w[:, None, :].astype(x.dtype), window_strides=(1,), padding=[(k - 1, 0)],
        dimension_numbers=("NWC", "WIO", "NWC"), feature_group_count=x.shape[-1])

def gla_chunked(q, k, v, log_a):
    b, s, h, dk = q.shape
    dv = v.shape[-1]
    c = GLA_CHUNK
    qc = _to_chunks(q * dk ** -0.5, c)
    kc = _to_chunks(k, c)
    vc = _to_chunks(v, c)
    ac = _to_chunks(log_a.astype(F32), c)
    causal = jnp.tril(jnp.ones((c, c), bool))[:, :, None]

    def step(state, inp):
        qi, ki, vi, ai = inp
        bcum = jnp.cumsum(ai, axis=2)
        b_last = bcum[:, :, -1:, :]
        diff = bcum[:, :, :, None, :] - bcum[:, :, None, :, :]
        decay = jnp.exp(jnp.where(causal, diff, -jnp.inf))
        scores = jnp.einsum("bhid,bhjd,bhijd->bhij", qi, ki, decay)
        o = (jnp.einsum("bhij,bhjv->bhiv", scores, vi)
             + jnp.einsum("bhid,bhdv->bhiv", qi * jnp.exp(bcum), state))
        state = (jnp.exp(b_last)[:, :, 0, :, None] * state
                 + jnp.einsum("bhjd,bhjv->bhdv", ki * jnp.exp(b_last - bcum), vi))
        return state, o

    s0 = jnp.zeros((b, h, dk, dv), F32)
    _, out = lax.scan(step, s0, (qc, kc, vc, ac))
    return _from_chunks(out)

def retention_chunked(q, k, v):
    b, s, h, dk = q.shape
    dv = v.shape[-1]
    c = RET_CHUNK
    log_g = jnp.log(1.0 - 2.0 ** (-5.0 - jnp.arange(h, dtype=F32)))
    idx = jnp.arange(c, dtype=F32)
    rel = idx[:, None] - idx[None, :]
    decay = jnp.where(rel >= 0, jnp.exp(log_g[:, None, None] * jnp.maximum(rel, 0.0)), 0.0)
    q_dec = jnp.exp(log_g[:, None] * (idx + 1.0))[:, :, None]
    k_dec = jnp.exp(log_g[:, None] * (c - 1.0 - idx))[:, :, None]
    chunk_dec = jnp.exp(log_g * c)[:, None, None]
    qc = _to_chunks(q, c)
    kc = _to_chunks(k * dk ** -0.5, c)
    vc = _to_chunks(v, c)

    def step(r, inp):
        qi, ki, vi = inp
        scores = jnp.einsum("bhid,bhjd->bhij", qi, ki) * decay
        o = jnp.einsum("bhij,bhjv->bhiv", scores, vi) + q_dec * jnp.einsum("bhid,bhdv->bhiv", qi, r)
        r = chunk_dec * r + jnp.einsum("bhjd,bhjv->bhdv", ki * k_dec, vi)
        return r, o

    r0 = jnp.zeros((b, h, dk, dv), F32)
    _, out = lax.scan(step, r0, (qc, kc, vc))
    return _from_chunks(out)

def mlstm_chunked(q, k, v, i_pre, f_pre):
    b, s, h, dk = q.shape
    dv = v.shape[-1]
    c = ML_CHUNK
    qc = _to_chunks(q, c)
    kc = _to_chunks(k * dk ** -0.5, c)
    vc = _to_chunks(v, c)
    ic = _to_chunks(i_pre.astype(F32)[..., None], c)[..., 0]
    fc = _to_chunks(jax.nn.log_sigmoid(f_pre.astype(F32))[..., None], c)[..., 0]
    causal = jnp.tril(jnp.ones((c, c), bool))

    def step(carry, inp):
        c_st, n_st, m_st = carry
        qi, ki, vi, ii, lfi = inp
        bcum = jnp.cumsum(lfi, axis=-1)
        d_log = jnp.where(causal, bcum[..., :, None] - bcum[..., None, :] + ii[..., None, :], -jnp.inf)
        inter_log = bcum + m_st[..., None]
        m_t = jnp.maximum(inter_log, jnp.max(d_log, axis=-1))
        w_inter = jnp.exp(inter_log - m_t)
        s_qk = jnp.einsum("bhid,bhjd->bhij", qi, ki) * jnp.exp(d_log - m_t[..., None])
        num = (jnp.einsum("bhij,bhjv->bhiv", s_qk, vi)
               + w_inter[..., None] * jnp.einsum("bhid,bhdv->bhiv", qi, c_st))
        den = jnp.sum(s_qk, axis=-1) + w_inter * jnp.einsum("bhid,bhd->bhi", qi, n_st)
        h_t = num / jnp.maximum(jnp.abs(den), jnp.exp(-m_t))[..., None]
        b_last = bcum[..., -1]
        log_w = b_last[..., None] - bcum + ii
        m_new = jnp.maximum(b_last + m_st, jnp.max(log_w, axis=-1))
        g_prev = jnp.exp(b_last + m_st - m_new)
        wk = jnp.exp(log_w - m_new[..., None])[..., None] * ki
        c_new = g_prev[..., None, None] * c_st + jnp.einsum("bhjd,bhjv->bhdv", wk, vi)
        n_new = g_prev[..., None] * n_st + jnp.sum(wk, axis=2)
        return (c_new, n_new, m_new), h_t

    carry0 = (jnp.zeros((b, h, dk, dv), F32), jnp.zeros((b, h, dk), F32), jnp.zeros((b, h), F32))
    _, out = lax.scan(step, carry0, (qc, kc, vc, ic, fc))
    return _from_chunks(out)

def hybrid_mix(hn, positions, w_in, gla_w_a2, gla_b_a, gla_g_norm, ret_g_norm,
               ml_conv, ml_b_i, ml_b_f, w_out):
    b, s, _ = hn.shape
    split_points = np.cumsum(IN_SIZES)[:-1].tolist()
    (gq, gk, gv, ga, gr, rq, rk, rv, rg, mq, mk, mv, mo, mi, mf) = jnp.split(hn @ w_in, split_points, axis=-1)

    def heads(t, nh):
        return t.reshape(b, s, nh, -1)

    log_a = jax.nn.log_sigmoid((ga @ gla_w_a2 + gla_b_a).astype(F32)) / GLA_TAU
    o_gla = gla_chunked(heads(gq, GLA_HEADS), heads(gk, GLA_HEADS), heads(gv, GLA_HEADS), heads(log_a, GLA_HEADS))
    o_gla = (head_rmsnorm(o_gla, gla_g_norm) * jax.nn.silu(gr.astype(F32))).astype(hn.dtype)

    rq = rotary(heads(rq, RET_HEADS), positions)
    rk = rotary(heads(rk, RET_HEADS), positions)
    o_ret = retention_chunked(rq, rk, heads(rv, RET_HEADS))
    o_ret = (head_groupnorm(o_ret, ret_g_norm) * jax.nn.silu(rg.astype(F32))).astype(hn.dtype)

    mqk = jax.nn.silu(causal_dwconv(jnp.concatenate([mq, mk], axis=-1), ml_conv))
    mq, mk = jnp.split(mqk, 2, axis=-1)
    o_ml = mlstm_chunked(heads(mq, ML_HEADS), heads(mk, ML_HEADS), heads(mv, ML_HEADS), mi + ml_b_i, mf + ml_b_f)
    o_ml = (jax.nn.sigmoid(mo.astype(F32)) * o_ml.reshape(b, s, -1)).astype(hn.dtype)

    return jnp.concatenate([o_gla, o_ret, o_ml], axis=-1) @ w_out

def mem_cross_attn(hn, memn, w_q, w_kv, w_o):
    b, s, d = hn.shape
    m = memn.shape[1]
    q = (hn @ w_q).reshape(b, s, XA_HEADS, XA_DH)
    k, v = jnp.split(memn @ w_kv, 2, axis=-1)
    k = k.reshape(b, m, XA_HEADS, XA_DH)
    v = v.reshape(b, m, XA_HEADS, XA_DH)
    scores = jnp.einsum("bshd,bmhd->bhsm", q, k).astype(F32) * XA_DH ** -0.5
    p = jax.nn.softmax(scores, axis=-1).astype(v.dtype)
    o = jnp.einsum("bhsm,bmhd->bshd", p, v).reshape(b, s, d)
    return o @ w_o

def setup_inputs(seed: int = 0) -> dict:
    key = jax.random.key(seed)
    ks = jax.random.split(key, 32)
    L, D = DEPTH, D_MODEL

    def w(k, shape, fan_in):
        return jax.random.normal(k, shape, F32) * fan_in ** -0.5

    def gain(k, shape):
        return 1.0 + 0.02 * jax.random.normal(k, shape, F32)

    x = jax.random.normal(ks[0], (BATCH, SEQ, D), F32)
    mem = jax.random.normal(ks[1], (BATCH, MEM_LEN, D), F32)
    positions = (jnp.arange(SEQ, dtype=jnp.int32)[None, :]
                 + jax.random.randint(ks[2], (BATCH, 1), 0, MAX_POS_OFFSET, dtype=jnp.int32))
    ml_b_f = (jnp.linspace(ML_FBIAS_LO, ML_FBIAS_HI, ML_HEADS, dtype=F32)[None, :]
              + 0.1 * jax.random.normal(ks[14], (L, ML_HEADS), F32))
    return {
        "x": x,
        "mem": mem,
        "positions": positions,
        "g_ffa": gain(ks[3], (L, D)),
        "w_ffa_gu": w(ks[4], (L, D, 2 * D_FF), D),
        "w_ffa_down": w(ks[5], (L, D_FF, D), D_FF),
        "g_mix": gain(ks[6], (L, D)),
        "w_in": w(ks[7], (L, D, D_IN), D),
        "gla_w_a2": w(ks[8], (L, GLA_RANK, GLA_HEADS * GLA_DK), GLA_RANK),
        "gla_b_a": 0.1 * jax.random.normal(ks[9], (L, GLA_HEADS * GLA_DK), F32),
        "gla_g_norm": gain(ks[10], (L, GLA_HEADS * GLA_DV)),
        "ret_g_norm": gain(ks[11], (L, RET_HEADS * RET_DV)),
        "ml_conv": w(ks[12], (L, ML_CONV, 2 * ML_HEADS * ML_DK), ML_CONV),
        "ml_b_i": 0.1 * jax.random.normal(ks[13], (L, ML_HEADS), F32),
        "ml_b_f": ml_b_f,
        "w_out": w(ks[15], (L, D_MIX, D), D_MIX),
        "g_xa": gain(ks[16], (L, D)),
        "g_mem": gain(ks[17], (L, D)),
        "w_xa_q": w(ks[18], (L, D, D), D),
        "w_xa_kv": w(ks[19], (L, D, 2 * D), D),
        "w_xa_o": w(ks[20], (L, D, D), D),
        "g_ffb": gain(ks[21], (L, D)),
        "w_ffb_gu": w(ks[22], (L, D, 2 * D_FF), D),
        "w_ffb_down": w(ks[23], (L, D_FF, D), D_FF),
        "g_final": gain(ks[24], (D,)),
    }

def reference(x, mem, positions, g_ffa, w_ffa_gu, w_ffa_down, g_mix, w_in, gla_w_a2, gla_b_a,
              gla_g_norm, ret_g_norm, ml_conv, ml_b_i, ml_b_f, w_out, g_xa, g_mem, w_xa_q,
              w_xa_kv, w_xa_o, g_ffb, w_ffb_gu, w_ffb_down, g_final):
    for l in range(DEPTH):
        x = x + 0.5 * swiglu_ffn(rmsnorm(x, g_ffa[l]), w_ffa_gu[l], w_ffa_down[l])
        x = x + hybrid_mix(rmsnorm(x, g_mix[l]), positions, w_in[l], gla_w_a2[l], gla_b_a[l],
                           gla_g_norm[l], ret_g_norm[l], ml_conv[l], ml_b_i[l], ml_b_f[l], w_out[l])
        x = x + mem_cross_attn(rmsnorm(x, g_xa[l]), rmsnorm(mem, g_mem[l]), w_xa_q[l], w_xa_kv[l], w_xa_o[l])
        x = x + 0.5 * swiglu_ffn(rmsnorm(x, g_ffb[l]), w_ffb_gu[l], w_ffb_down[l])
    return rmsnorm(x, g_final)


_drawn_inputs = setup_inputs


def setup_inputs(seed=0):
    import zlib

    import numpy as np

    out = dict(_drawn_inputs(seed))
    spreads = {}
    factors = {'gla_g_norm': 5.596,
     'ret_g_norm': 5.529,
     'ml_b_i': 8.0,
     'g_xa': 8.0,
     'g_mem': 8.0,
     'g_ffb': 4.976,
     'g_final': 2.858}
    for name, (base, spread) in spreads.items():
        noise = np.random.default_rng([zlib.crc32(name.encode()), seed]).standard_normal(out[name].shape)
        drawn = base * np.exp(spread * noise) if base else spread * noise
        out[name] = jnp.asarray(drawn.astype(out[name].dtype))
    for name, factor in factors.items():
        out[name] = (out[name] * factor).astype(out[name].dtype)
    return out
```

```python
import numpy as np
import concourse.bass as bass
from concourse import mybir
from contextlib import ExitStack

F32 = mybir.dt.float32
F32R = mybir.dt.float32r
U8 = mybir.dt.uint8
I32 = mybir.dt.int32
ALU = mybir.AluOpType
ACT = mybir.ActivationFunctionType
AX = mybir.AxisListType

P = 128
D, S, DEPTH, MEM = 1024, 512, 2, 256
KT = D // P
TB = S // P
DFF = 2816
NJ = DFF // P
EPS = 1e-6
GH, GDK, DV = 6, 32, 64
MH, MDK = 4, 64
XH, XDH = 4, 256
GT = 96
SIZES = [192, 192, 384, 16, 384, 192, 192, 384, 384, 256, 256, 256, 256, 4, 4]
(GQ0, GK0, GV0, GA0, GR0, RQ0, RK0, RV0, RG0, MQ0, MK0, MV0, MO0, MI0, MF0) = (
    int(v) for v in np.cumsum([0] + SIZES[:-1]))
D_IN = sum(SIZES)

FFN_UP, FFN_DOWN = 2 * NJ, 3 * KT
DOWN_PARTS = [(0, 8), (8, 15), (15, 22)]
C_FFA = 0
MIX_COLS = ([(GA0, 16), (MI0, 4), (MF0, 4)]
            + [(GQ0 + GT * i, GT) for i in range(2)] + [(GK0 + GT * i, GT) for i in range(2)]
            + [(GV0 + GT * i, GT) for i in range(4)]
            + [(RQ0 + GT * i, GT) for i in range(2)] + [(RK0 + GT * i, GT) for i in range(2)]
            + [(RV0 + P * i, P) for i in range(3)]
            + [(MQ0 + P * i, P) for i in range(2)] + [(MK0 + P * i, P) for i in range(2)]
            + [(MV0 + P * i, P) for i in range(2)]
            + [(GR0 + P * i, P) for i in range(3)] + [(RG0 + P * i, P) for i in range(3)]
            + [(MO0 + P * i, P) for i in range(2)])
C_MIX = FFN_UP + FFN_DOWN
(C_GA, C_MI, C_MF, C_GQ, C_GK, C_GV, C_RQ, C_RK, C_RV, C_MQK, C_MV, C_GATE) = (
    C_MIX + i for i in (0, 1, 2, 3, 5, 7, 11, 13, 15, 18, 22, 24))
C_K = C_MIX + len(MIX_COLS)
C_V, C_OUT, C_Q, C_O = C_K + 8, C_K + 16, C_K + 24, C_K + 32
C_FFB = C_K + 40
CHUNKS = C_FFB + FFN_UP + FFN_DOWN

J_FFA, J_HA, J_MIX, J_MEM, J_FEAT, J_XA, J_ATT, J_FFB, J_HB = (
    0, 8, 30, 38, 46, 54, 62, 70, 78)

R_FFA, R_MIX, R_XA, R_MEM, R_FFB, R_GG, R_RG, R_CONV, R_BA = 0, 8, 16, 24, 32, 40, 43, 46, 62
N_ROWS = 64

K_ID, K_CAUSAL, K_HEAD, K_MEAN, K_ONE, K_SWAP, K_PAIR, K_FREQ, K_EPS = (
    0, 128, 256, 384, 385, 386, 482, 738, 739)
K_N = 740

HEAVY_LEVELS = [64, 32]
LEVELS = [16, 8, 4, 2, 1]
X_ORDER = [64, 32, 16, 8, 4, 2, 1, 256, 128]
X_SLOTS = 3
U_OFF = GH * (2 + len(LEVELS))
U_ML, U_RET, U_XA = U_OFF + 2 * GH, U_OFF + 2 * GH + MH * TB, U_OFF + 2 * GH + (MH + GH) * TB
POST = [(0, 1), (1, 1), (2, 1), (3, 0), (3, 1), (4, 0), (4, 1), (5, 0), (5, 1)]


def constants():
    c = np.zeros((P, K_N), np.float32)
    j, i = np.arange(P)[:, None], np.arange(P)[None, :]
    c[:, K_ID:K_ID + P] = np.eye(P)
    c[:, K_CAUSAL:K_CAUSAL + P] = j <= i
    c[:, K_HEAD:K_HEAD + P] = (j // DV == i // DV) / DV
    c[:, K_MEAN] = 1.0 / D
    c[:, K_ONE] = 1.0
    for h in range(MH):
        c[h, K_PAIR + DV * h:K_PAIR + DV * (h + 1)] = 1.0
    half = GDK // 2
    for h in range(3):
        for r in range(half):
            c[GDK * h + half + r, K_SWAP + GDK * h + r] = -1.0
            c[GDK * h + r, K_SWAP + GDK * h + half + r] = 1.0
    freq = (np.float32(1.0) / (np.float32(10000.0) ** np.linspace(0, 1, half, dtype=np.float32)))
    c[:, K_FREQ] = np.tile(freq.astype(np.float32), P // half)
    c[:, K_EPS] = EPS
    lg = np.log(1.0 - 2.0 ** (-5.0 - np.arange(GH)))
    rel = np.arange(S)[None, :] - np.arange(P)[:, None]
    dec = np.where(rel >= 0, np.exp(lg[:, None, None] * np.maximum(rel, 0)), 0.0) * GDK ** -0.5
    decay = np.ascontiguousarray(dec.transpose(1, 0, 2)).astype(np.float32)
    masks = np.zeros((P, 6, P), bool)
    for n, low in enumerate([HEAVY_LEVELS] + [[v] for v in LEVELS]):
        for v in low:
            masks[:, n] |= ((j // (2 * v) == i // (2 * v)) & (j % (2 * v) < v) & (i % (2 * v) >= v))
    return c, decay, masks.astype(np.float32)


class Banks:

    def __init__(self, engine, banks):
        self.engine, self.banks, self.n = engine, banks, 0
        self.freed, self.of, self.full = [None] * len(banks), {}, {}

    def next(self, name, sem, value):
        b = self.n % len(self.banks)
        if self.freed[b] is not None:
            self.engine.wait_ge(*self.freed[b])
        self.freed[b] = (sem, value)
        self.n += 1
        assert name not in self.of, name
        self.of[name] = self.banks[b]
        return self.banks[b]

    def there(self, name):
        self.full[name] = len(self.full) + 1


def build(nc, A, out):
    ctx = ExitStack()
    with ctx:
        at = [-(-nc.sbuf_base // 32) * 32]

        def place(name, shape, dt=F32, offset=None):
            size = int(np.prod(shape[1:])) * (1 if dt == U8 else 4)
            o = at[0] if offset is None else offset
            if offset is None:
                at[0] += -(-size // 32) * 32
                assert at[0] <= nc.sbuf_usable_end, (name, at[0])
            return nc.alloc_sbuf_tensor_at(name, shape, dt, offset=o)

        UNIT = S * 4
        x = place("x", [P, KT, S])
        xh = place("xh", [P, KT, S], F32R)
        xl = place("xl", [P, KT, S], F32R)
        raw = [place(f"w_raw{i}", [P, 8, P]) for i in range(4)]
        whi = [place(f"w_hi{i}", [P, 8, P], F32R) for i in range(2)]
        wlo = [place(f"w_lo{i}", [P, 8, P], F32R) for i in range(2)]
        region = at[0]
        hh = place("h_hi", [P, NJ, S], F32R)
        hl = place("h_lo", [P, NJ, S], F32R)

        def unit(name, first, shape, dt=F32):
            assert first * UNIT + int(np.prod(shape[1:])) * 4 <= 2 * NJ * UNIT
            return place(name, shape, dt, region + first * UNIT)

        gq = unit("gq", 0, [P, 2, S])
        gk = unit("gk", 2, [P, 2, S])
        p64 = unit("p64", 4, [P, 2, S])
        p128 = unit("p128", 6, [P, 2, S])
        p256 = unit("p256", 8, [P, 2, S])
        xs = [unit(f"xs{i}", 10 + 2 * i, [P, 2, S]) for i in range(X_SLOTS)]
        sdiag = unit("sdiag", 16, [P, GH, TB, P])
        gv = unit("gv", 22, [P, TB, GH * DV])
        rqk = unit("rqk", 25, [P, 4, S])
        rv = unit("rv", 29, [P, TB, GH * DV])
        mqk = unit("mqk", 32, [P, 4, S])
        mv = unit("mv", 36, [P, TB, MH * DV])
        row_u = unit("row_u", 38, [P, S])
        row_b = unit("row_b", 39, [P, S])
        row_m = unit("row_m", 40, [P, S])
        row_e = unit("row_e", 41, [P, S])
        sm = [unit(f"sm{i}", 42 + i, [P, S]) for i in range(2)]
        ga_t = unit("ga_t", 10, [P, S])
        gates = unit("gates", 0, [P, 8, S])
        o_ret = unit("o_ret", 8, [P, 3, S])
        o_ml = unit("o_ml", 11, [P, 2, S])
        memraw = unit("memraw", 13, [P, 2, D])
        memhi = unit("memhi", 17, [P, KT, MEM], F32R)
        memlo = unit("memlo", 21, [P, KT, MEM], F32R)
        psq = [unit(f"psq{i}", 40 + i, [P, S]) for i in range(2)]
        kx = unit("kx", 32, [P, KT, MEM])
        vx = unit("vx", 36, [P, 2, D])
        memsq = unit("memsq", 40, [P, D])
        qx = unit("qx", 0, [P, KT, S])
        prob = [unit(f"prob{i}", 8 + i, [P, 2, MEM]) for i in range(2)]
        pt = [unit(f"pt{i}", 10 + 2 * i, [P, 2, S]) for i in range(2)]
        xin = unit("xin", 0, [P, TB, D])
        prow = unit("prow", 43, [N_ROWS, P])
        posi = unit("posi", 16, [P, S], I32)
        ang = unit("ang", 17, [P, S])
        turns_i = unit("turns_i", 18, [P, S], I32)
        turns = unit("turns", 19, [P, S])
        masks_in = unit("masks_in", 20, [P, 6, P])
        yout = unit("yout", 0, [P, TB, D])
        yk = [unit(f"yk{i}", 16 + i, [P, S]) for i in range(2)]

        T = [place(f"tmp{i}", [P, S]) for i in range(4)]
        stat = place("stat", [P, S])
        o_gla = place("o_gla", [P, 3, S])
        rtmp = place("rtmp", [P, S])
        sincos = place("sincos", [P, 2, S])
        decay = place("decay", [P, GH, S])
        const = place("const", [P, K_N])
        masks = place("masks", [P, 6, P], U8)
        pcol = place("pcol", [P, N_ROWS])
        w_a2 = place("w_a2", [16, 2 * GT])
        b_if = place("b_if", [MH, 2])
        ucol = place("ucol", [P, TB, MH])
        memst = place("memst", [P, 4])
        smx = place("smx", [P, 2, 4])
        ident = const[:, K_ID:K_ID + P]
        eps = const[:, K_EPS:K_EPS + 1]

        psum = [ctx.enter_context(nc.psum_tensor(f"bank{i}", [P, S], F32)) for i in range(8)]
        RB, SB, OB = psum[0:4], psum[4:6], psum[6:8]

        loop_sems = []
        rings = []

        def sem(name):
            s = ctx.enter_context(nc.semaphore(name))
            loop_sems.append(s)
            return s

        w_loaded = [sem(f"w_loaded{i}") for i in range(4)]
        w_hi, w_lo, chunk_done = sem("w_hi"), sem("w_lo"), sem("chunk_done")
        val_ready, hi_ready, lo_ready = sem("val_ready"), sem("hi_ready"), sem("lo_ready")
        tile_full = sem("tile_full")
        sq_added, rms_ready, x_ready, sq_ready = (
            sem("sq_added"), sem("rms_ready"), sem("x_ready"), sem("sq_ready"))
        silu_ready, params_in, params_up = sem("silu_ready"), sem("params_in"), sem("params_up")
        ga_ready, row_in, z_in, ln_ready = sem("ga_ready"), sem("row_in"), sem("z_in"), sem("ln_ready")
        act_link, dve_link = sem("act_link"), sem("dve_link")
        rows_ready, em_ready = sem("rows_ready"), sem("em_ready")
        gqk_ready, stage_ready, vtok_ready = sem("gqk_ready"), sem("stage_ready"), sem("vtok_ready")
        rot_copied, rot_ready = sem("rot_copied"), sem("rot_ready")
        conv_ready, mqk_ready = sem("conv_ready"), sem("mqk_ready")
        gate_copied, gate_ready = sem("gate_copied"), sem("gate_ready")
        e_ready, exp_ready, xs_ready = sem("e_ready"), sem("exp_ready"), sem("xs_ready")
        s_full, s_done = sem("s_full"), sem("s_done")
        o_full, o_taken, den_abs = sem("o_full"), sem("o_taken"), sem("den_abs")
        ucol_ready, dlog_ready, dexp_ready = sem("ucol_ready"), sem("dlog_ready"), sem("dexp_ready")
        xc_ready, post_sq, post_rms = sem("xc_ready"), sem("post_sq"), sem("post_rms")
        mem_in, mem_rms, memn_ready = sem("mem_in"), sem("mem_rms"), sem("memn_ready")
        kx_ready, qx_ready, pt_ready = sem("kx_ready"), sem("qx_ready"), sem("pt_ready")
        max_ready, prob_exp, prob_ready = sem("max_ready"), sem("prob_exp"), sem("prob_ready")

        once_in, once_pe, once_dve, once_act, x_in = (
            ctx.enter_context(nc.semaphore(n))
            for n in ("once_in", "once_pe", "once_dve", "once_act", "x_in"))
        y_pe, y_ready, y_out, y_act, y_in = (
            ctx.enter_context(nc.semaphore(n)) for n in ("y_pe", "y_ready", "y_out", "y_act", "y_in"))

        x_tok = A["x"].rearrange("b (t p) d -> p (b t) d", p=P)
        mem_tok = A["mem"].rearrange("b (t p) d -> p (b t) d", p=P)
        out_tok = out.rearrange("b (t p) d -> p (b t) d", p=P)

        with nc.Block() as block:
            @block.sync
            def _(sp):
                for t in range(TB):
                    sp.dma_start(xin[:, t, :], x_tok[:, t, :]).then_inc(x_in, 16)
                sp.dma_start(decay[:], A["c_decay"]).then_inc(once_in, 16)

            @block.scalar
            def _(act):
                act.dma_start(const[:], A["c_const"]).then_inc(once_in, 16)
                act.dma_start(masks_in[:], A["c_masks"]).then_inc(once_in, 16)
                act.dma_start(posi[0:GT, :], A["positions"].to_broadcast([GT, S])).then_inc(once_in, 16)
                for k in range(KT):
                    act.wait_ge(once_dve, k + 1)
                    if k >= 2:
                        act.wait_ge(once_dve, KT + k - 1)
                    act.activation(T[k % 2][:], x[:, k, :], ACT.Square).then_inc(once_act, 1)
                act.wait_ge(once_dve, 2 * KT + 1)
                act.activation(sincos[0:GT, 1, :], ang[0:GT, :], ACT.Sin).then_inc(once_act, 1)
                act.activation(turns[0:GT, :], ang[0:GT, :], ACT.Abs).then_inc(once_act, 1)
                act.wait_ge(once_dve, 2 * KT + 2)
                act.activation(sincos[0:GT, 0, :], turns[0:GT, :], ACT.Sin)

            @block.tensor
            def _(pe):
                pe.wait_ge(once_in, 64)
                pe.wait_ge(x_in, 16 * TB)
                for k in range(KT):
                    if k >= 8:
                        pe.wait_ge(once_dve, k - 7)
                    for t in range(TB):
                        m = pe.transpose(psum[k % 8][:, t * P:(t + 1) * P],
                                         xin[:, t, k * P:(k + 1) * P], ident)
                    m.then_inc(once_pe, 1)

            @block.vector
            def _(dve):
                for k in range(KT):
                    dve.wait_ge(once_pe, k + 1)
                    dve.tensor_copy(x[:, k, :], psum[k % 8][:]).then_inc(once_dve, 1)
                for k in range(KT):
                    dve.wait_ge(once_act, k + 1)
                    if k == 0:
                        dve.tensor_copy(stat[:], T[0][:]).then_inc(once_dve, 1)
                    else:
                        dve.wait_ge(once_dve, KT + k)
                        dve.tensor_tensor(stat[:], stat[:], T[k % 2][:], ALU.add).then_inc(once_dve, 1)
                dve.memset(prow[:], 0.0)
                two_pi = 2.0 * np.pi
                c1 = 6.28125
                c2 = float(np.float32(np.floor((two_pi - c1) * 2 ** 21) / 2 ** 21))
                c3 = float(two_pi - c1 - c2)
                link = [0]
                angle_step = x_in

                def step(ins):
                    link[0] += 1
                    ins.then_inc(angle_step, 1)
                    dve.wait_ge(angle_step, 16 * TB + link[0])

                dve.wait_ge(x_in, 16 * TB)
                dve.wait_ge(once_in, 64)
                dve.tensor_copy(masks[:], masks_in[:])
                step(dve.tensor_copy(turns[0:GT, :], posi[0:GT, :]))
                step(dve.tensor_scalar(ang[0:GT, :], turns[0:GT, :], const[0:GT, K_FREQ:K_FREQ + 1],
                                       None, ALU.mult))
                step(dve.tensor_scalar(turns[0:GT, :], ang[0:GT, :], 1.0 / two_pi, None, ALU.mult))
                step(dve.tensor_copy(turns_i[0:GT, :], turns[0:GT, :]))
                step(dve.tensor_copy(turns[0:GT, :], turns_i[0:GT, :]))
                for c in (c1, c2, c3):
                    step(dve.scalar_tensor_tensor(ang[0:GT, :], turns[0:GT, :], -c, ang[0:GT, :],
                                                  ALU.mult, ALU.add))
                dve.tensor_scalar(ang[0:GT, :], ang[0:GT, :], 3.1415925, -3.1415925,
                                  ALU.min, ALU.max).then_inc(once_dve, 1)
                dve.wait_ge(once_act, KT + 2)
                dve.tensor_scalar(turns[0:GT, :], turns[0:GT, :], -1.0, float(np.pi / 2),
                                  ALU.mult, ALU.add).then_inc(once_dve, 1)

        gu = [A[n].rearrange("l (k p) (h j c) -> l h j p k c", p=P, h=2, c=P)
              for n in ("w_ffa_gu", "w_ffb_gu")]
        down = [A[n].rearrange("l (k p) (m c) -> l m p k c", p=P, c=P)
                for n in ("w_ffa_down", "w_ffb_down")]
        w_in = A["w_in"].rearrange("l (k p) c -> l p k c", p=P)
        w_kv = A["w_xa_kv"].rearrange("l (k p) c -> l p k c", p=P)
        square = {n: A[n].rearrange("l (k p) c -> l p k c", p=P) for n in ("w_out", "w_xa_q", "w_xa_o")}

        with nc.Fori(0, DEPTH) as lay:
            with nc.Block() as block:

                @block.sync
                def _(sp):
                    def slot_free(c, first=False):
                        if not first:
                            sp.wait_ge(w_hi, c - 3)
                            sp.wait_ge(w_lo, c - 3)

                    def load(c, src):
                        slot_free(c, c < 4)
                        n, w = src.shape[-2], src.shape[-1]
                        sp.dma_start(raw[c % 4][:, 0:n, 0:w], src).then_inc(w_loaded[c % 4], 16)

                    def ffn(base, w_up, w_down):
                        for c in range(4):
                            load(base + c, w_up[lay, c % 2, c // 2])
                        with sp.Fori(1, NJ // 2) as it:
                            for s in range(4):
                                slot_free(it * 4 + (base + s))
                                sp.dma_start(raw[(base + s) % 4][:], w_up[lay, s % 2, it * 2 + s // 2])\
                                  .then_inc(w_loaded[(base + s) % 4], 16)
                        for m in range(KT):
                            for i, (k0, k1) in enumerate(DOWN_PARTS):
                                load(base + FFN_UP + 3 * m + i, w_down[lay, m, :, k0:k1, :])

                    ffn(C_FFA, gu[0], down[0])
                    for i, (c0, w) in enumerate(MIX_COLS):
                        load(C_MIX + i, w_in[lay, :, :, c0:c0 + w])
                    for m in range(16):
                        load(C_K + m, w_kv[lay, :, :, m * P:(m + 1) * P])
                    for c0, n in ((C_OUT, "w_out"), (C_Q, "w_xa_q"), (C_O, "w_xa_o")):
                        for m in range(KT):
                            load(c0 + m, square[n][lay, :, :, m * P:(m + 1) * P])
                    ffn(C_FFB, gu[1], down[1])

                @block.gpsimd
                def _(pool):
                    def lo(c, parity, n=8):
                        pool.wait_ge(w_hi, c + 1)
                        r = raw[parity % 4]
                        pool.tensor_tensor(wlo[parity % 2][:, 0:n], r[:, 0:n],
                                           whi[parity % 2][:, 0:n].bitcast(F32),
                                           ALU.subtract).then_inc(w_lo, 1)

                    def ffn(base):
                        with pool.Fori(0, NJ // 2) as it:
                            for s in range(4):
                                lo(it * 4 + (base + s), base + s)
                        for m in range(KT):
                            for i, (k0, k1) in enumerate(DOWN_PARTS):
                                c = base + FFN_UP + 3 * m + i
                                lo(c, c, k1 - k0)

                    ffn(C_FFA)
                    for c in range(C_MIX, C_FFB):
                        lo(c, c)
                    ffn(C_FFB)

                @block.tensor
                def _(pe):
                    ring = Banks(pe, RB)
                    rings.append(ring)

                    def signal_tile(name, m):
                        ring.there(name)
                        m.then_inc(tile_full, 1)

                    def chunk(c, bank, rhs_hi, rhs_lo, k0=0, k1=8, w=P, jobs=None, start=True,
                              stop=True, parity=None, cols=S):
                        q = c if parity is None else parity
                        pe.wait_ge(w_lo, c + 1)
                        o, wh, wl = bank[0:w, 0:cols], whi[q % 2], wlo[q % 2]
                        for k in range(k0, k1):
                            if jobs is not None:
                                pe.wait_ge(lo_ready, jobs + k - k0 + 1)
                            pe.matmul(o, wl[:, k - k0, 0:w], rhs_hi[:, k, :],
                                      start=start and k == k0, stop=False)
                            pe.matmul(o, wh[:, k - k0, 0:w], rhs_lo[:, k, :], start=False, stop=False)
                        for k in range(k0, k1):
                            m = pe.matmul(o, wh[:, k - k0, 0:w], rhs_hi[:, k, :], start=False,
                                          stop=stop and k == k1 - 1)
                        m.then_inc(chunk_done, 1)

                    def norm_stat(i):
                        if i > 0:
                            pe.wait_ge(sq_added, KT * i)
                        b = ring.next(("stat", i), rms_ready, i + 1)
                        signal_tile(("stat", i), pe.matmul(b[:], const[:, K_MEAN:K_MEAN + 1].to_broadcast([P, P]), stat[:],
                                              start=True, stop=True))

                    def ffn(base, job, hjob, i):
                        norm_stat(i)
                        n0 = ring.n

                        def up(it, first):
                            for s in range(4):
                                j = it * 2 + s // 2
                                b = RB[(n0 + s) % 4]
                                if first:
                                    b = ring.next(("up", i, s), val_ready, hjob + s // 2 + 1)
                                else:
                                    pe.wait_ge(val_ready, j + (hjob - 1))
                                chunk(it * 4 + (base + s), b, xh, xl, parity=base + s,
                                      jobs=job if first and s == 0 else None)

                        up(0, True)
                        with pe.Fori(1, NJ // 2) as it:
                            up(it, False)
                        for s in range(4):
                            ring.freed[(n0 + s) % 4] = (val_ready, hjob + NJ - 1 + s // 2)
                        for m in range(KT):
                            b = ring.next(("down", i, m), x_ready, (0 if i == 0 else 24) + m + 1)
                            for q, (k0, k1) in enumerate(DOWN_PARTS):
                                chunk(base + FFN_UP + 3 * m + q, b, hh, hl, k0, k1,
                                      jobs=hjob + k0 if m == 0 else None, start=q == 0, stop=q == 2)

                    pe.wait_ge(params_in, 16 * 12)
                    b = ring.next("params", params_up, 1)
                    signal_tile("params", pe.transpose(b[:, 0:N_ROWS], prow[:], ident[0:N_ROWS, 0:N_ROWS]))
                    ffn(C_FFA, J_FFA, J_HA, 0)

                    def turn(n, w, cols=S):
                        pe.wait_ge(stage_ready, n + 1)
                        b = ring.next(("turn", n), vtok_ready, n + 1)
                        for t in range(cols // P):
                            m = pe.transpose(b[:, t * w:(t + 1) * w], T[2 + n % 2][0:w, t * P:(t + 1) * P],
                                             ident[0:w, 0:w])
                        signal_tile(("turn", n), m)

                    norm_stat(1)
                    chunk(C_GA, ring.next("ga", ga_ready, 1), xh, xl, jobs=J_MIX)
                    for n, c in enumerate((C_MI, C_MF)):
                        chunk(c, ring.next(("row", n), row_in, n + 1), xh, xl)
                    pe.wait_ge(ga_ready, 1)
                    for t in range(2):
                        b = ring.next(("z", t), z_in, t + 1)
                        signal_tile(("z", t), pe.matmul(b[0:GT, :], w_a2[:, t * GT:(t + 1) * GT], ga_t[0:16, :],
                                              start=True, stop=True))
                    for n in range(4):
                        chunk(C_GQ + n, ring.next(("gqk", n), gqk_ready, n + 1), xh, xl, w=GT)
                    for n in range(5):
                        if n < 4:
                            chunk(C_GV + n, ring.next(("v", n), stage_ready, n + 1), xh, xl, w=GT)
                        if n >= 1:
                            turn(n - 1, GT)

                    unit_n = [0]

                    def scores():
                        u = unit_n[0]
                        if u >= 2:
                            pe.wait_ge(s_done, u - 1)
                        unit_n[0] += 1
                        return SB[u % 2]

                    def rot(n):
                        chunk(C_RQ + n, ring.next(("rot", n), rot_copied, n + 1), xh, xl, w=GT)

                    def swap(n):
                        pe.wait_ge(rot_copied, n + 1)
                        b = ring.next(("swap", n), rot_ready, 2 * n + 1)
                        signal_tile(("swap", n), pe.matmul(b[0:GT, :], const[0:GT, K_SWAP:K_SWAP + GT],
                                              rqk[0:GT, n, :], start=True, stop=True))

                    def vchunk(c, n):
                        chunk(c, ring.next(("v", n), stage_ready, n + 1), xh, xl)

                    def qk_chunk(n):
                        chunk(C_MQK + n, ring.next(("mqk", n), conv_ready, 4 * n + 4), xh, xl)

                    fill = [
                        lambda: (rot(0), rot(1), swap(0)),
                        lambda: (rot(2), swap(1), rot(3), swap(2)),
                        lambda: (vchunk(C_RV, 4), swap(3), vchunk(C_RV + 1, 5), turn(4, P)),
                        lambda: (vchunk(C_RV + 2, 6), turn(5, P), qk_chunk(0), turn(6, P)),
                        lambda: (qk_chunk(1), qk_chunk(2)),
                        lambda: (qk_chunk(3), vchunk(C_MV, 7)),
                        lambda: (vchunk(C_MV + 1, 8), turn(7, P), turn(8, P)),
                    ]

                    def head_rows(t3, h):
                        return t3[GDK * (h % 3):GDK * (h % 3) + GDK, h // 3, :]

                    pe.wait_ge(gqk_ready, 4)
                    for h in range(GH):
                        b = scores()
                        for t in range(TB):
                            c = slice(t * P, (t + 1) * P)
                            m = pe.matmul(b[:, c], head_rows(gk, h)[:, c], head_rows(gq, h)[:, c],
                                          start=True, stop=True)
                        m.then_inc(s_full, 1)
                    fill[0]()
                    pe.wait_ge(xs_ready, 2)
                    for h in range(GH):
                        b = scores()
                        for t in range(TB):
                            for n, v in enumerate(HEAVY_LEVELS):
                                r = head_rows(xs[n], h)
                                for g in range(P // (2 * v)):
                                    k0 = 2 * v * g
                                    m = pe.matmul(b[k0:k0 + v, t * P + k0 + v:t * P + k0 + 2 * v],
                                                  r[:, t * P + k0:t * P + k0 + v],
                                                  r[:, t * P + k0 + v:t * P + k0 + 2 * v],
                                                  start=True, stop=True)
                        m.then_inc(s_full, 1)
                    fill[1]()
                    for n, v in enumerate(LEVELS):
                        pe.wait_ge(xs_ready, 3 + n)
                        for h in range(GH):
                            b = scores()
                            r = head_rows(xs[(2 + n) % X_SLOTS], h)
                            for t in range(TB):
                                c = slice(t * P, (t + 1) * P)
                                m = pe.matmul(b[:, c], r[:, c], r[:, c], start=True, stop=True)
                            m.then_inc(s_full, 1)
                        fill[2 + n]()

                    o_n = [0]

                    def o_bank():
                        q = o_n[0]
                        if q >= 2:
                            pe.wait_ge(o_taken, q - 1)
                        o_n[0] += 1
                        return OB[q % 2]

                    def gate(n):
                        chunk(C_GATE + n, ring.next(("gate", n), gate_copied, n + 1), xh, xl)

                    pe.wait_ge(xs_ready, 9)
                    x256, x128 = xs[7 % X_SLOTS], xs[8 % X_SLOTS]
                    pe.wait_ge(vtok_ready, 4)

                    def gla_off(h):
                        b = scores()
                        r = head_rows(x256, h)
                        for jt in range(2):
                            m = pe.matmul(b[:, jt * 256:(jt + 1) * 256], r[:, jt * P:(jt + 1) * P],
                                          r[:, 256:512], start=True, stop=True)
                        m.then_inc(s_full, 1)
                        b = scores()
                        r = head_rows(x128, h)
                        for n in range(2):
                            m = pe.matmul(b[:, n * P:(n + 1) * P], r[:, n * 256:n * 256 + P],
                                          r[:, n * 256 + P:n * 256 + 256], start=True, stop=True)
                        m.then_inc(s_full, 1)

                    def gla_pv(h, ob):
                        pe.wait_ge(s_done, U_OFF + 2 * h + 2)
                        o = ob[DV * (h % 2):DV * (h % 2) + DV, :]
                        v = gv[:, :, h * DV:(h + 1) * DV]
                        pieces = [(jt, sdiag[:, h, jt, :], jt * P) for jt in range(TB)]
                        pieces += [(jt, sm[0][:, jt * 256:(jt + 1) * 256], 256) for jt in range(2)]
                        pieces += [(2 * n, sm[1][:, n * P:(n + 1) * P], n * 256 + P) for n in range(2)]
                        for n, (jt, s, i0) in enumerate(pieces):
                            m = pe.matmul(o[:, i0:i0 + s.shape[-1]], v[:, jt, :], s, start=n == 0,
                                          stop=n == len(pieces) - 1, skip_group_check=True)
                        m.then_inc(o_full, 1)

                    gla_off(0)
                    for h in range(GH):
                        if h % 2 == 0:
                            ob = o_bank()
                        gla_pv(h, ob)
                        if h + 1 < GH:
                            gla_off(h + 1)

                    pe.wait_ge(rows_ready, 4)
                    b = ring.next("ucol", ucol_ready, 1)
                    for t in range(TB):
                        m = pe.transpose(b[:, t * MH:(t + 1) * MH], row_u[0:MH, t * P:(t + 1) * P],
                                         ident[0:MH, 0:MH])
                    signal_tile("ucol", m)
                    pe.wait_ge(mqk_ready, 4)
                    pe.wait_ge(vtok_ready, 9)
                    pe.wait_ge(em_ready, 1)

                    def ml_scores(h, jt):
                        b = scores()
                        q = mqk[MDK * (h % 2):MDK * (h % 2) + MDK, h // 2, :]
                        k = mqk[MDK * (h % 2):MDK * (h % 2) + MDK, 2 + h // 2, :]
                        pe.matmul(b[:, 0:S - jt * P], k[:, jt * P:(jt + 1) * P], q[:, jt * P:],
                                  start=True, stop=True).then_inc(s_full, 1)

                    def ml_out(h, jt, num, den):
                        n = U_ML + h * TB + jt
                        pe.wait_ge(s_done, n + 1)
                        s = sm[n % 2][:, 0:S - jt * P]
                        part = slice(DV * (h % 2), DV * (h % 2) + DV)
                        pe.matmul(num[part, jt * P:], mv[:, jt, h * DV:(h + 1) * DV], s,
                                  start=jt == 0, stop=jt == TB - 1, skip_group_check=True)
                        pe.matmul(den[part, jt * P:], const[:, K_ONE:K_ONE + 1].to_broadcast([P, DV]), s,
                                  start=jt == 0, stop=jt == TB - 1,
                                  skip_group_check=True).then_inc(o_full, 1)

                    for h in range(MH):
                        b = ring.next(("negm", h), dlog_ready, TB * (h + 1))
                        signal_tile(("negm", h), pe.matmul(b[:], ident[0:MH, h:h + 1].to_broadcast([MH, P]),
                                              row_m[0:MH, :], start=True, stop=True))
                        if h % 2 == 0:
                            den, num = o_bank(), o_bank()
                        ml_scores(h, 0)
                        for jt in range(TB):
                            if jt + 1 < TB:
                                ml_scores(h, jt + 1)
                            if jt in (0, 2):
                                gate(2 * h + jt // 2)
                            ml_out(h, jt, num, den)
                        if h % 2 == 1:
                            b = ring.next(("em", h // 2), o_taken, 4 + 2 * (h // 2))
                            sel = const[0:MH, K_PAIR + P * (h // 2):K_PAIR + P * (h // 2 + 1)]
                            signal_tile(("em", h // 2), pe.matmul(b[:], sel, row_e[0:MH, :], start=True, stop=True))

                    def ret_scores(h, jt):
                        b = scores()
                        q = rqk[GDK * (h % 3):GDK * (h % 3) + GDK, h // 3, :]
                        k = rqk[GDK * (h % 3):GDK * (h % 3) + GDK, 2 + h // 3, :]
                        pe.matmul(b[:, 0:S - jt * P], k[:, jt * P:(jt + 1) * P], q[:, jt * P:],
                                  start=True, stop=True).then_inc(s_full, 1)

                    def ret_out(h, jt, ob):
                        n = U_RET + h * TB + jt
                        pe.wait_ge(s_done, n + 1)
                        pe.matmul(ob[DV * (h % 2):DV * (h % 2) + DV, jt * P:],
                                  rv[:, jt, h * DV:(h + 1) * DV], sm[n % 2][:, 0:S - jt * P],
                                  start=jt == 0, stop=jt == TB - 1,
                                  skip_group_check=True).then_inc(o_full, 1)

                    pe.wait_ge(rot_ready, 8)
                    steps = [(h, jt) for h in range(GH) for jt in range(TB)]
                    ret_scores(0, 0)
                    for n, (h, jt) in enumerate(steps):
                        if n + 1 < len(steps):
                            ret_scores(*steps[n + 1])
                        if h % 2 == 0 and jt == 0:
                            ob = o_bank()
                        ret_out(h, jt, ob)

                    def mem_turn(k):
                        if k == 0:
                            pe.wait_ge(memn_ready, 2)
                        b = ring.next(("mem", k), val_ready, J_MEM + k + 1)
                        for t in range(2):
                            m = pe.transpose(b[:, t * P:(t + 1) * P], memraw[:, t, k * P:(k + 1) * P],
                                             ident)
                        signal_tile(("mem", k), m)

                    for k in range(KT):
                        mem_turn(k)

                    def stat_of(p, step):
                        if step == 0:
                            pe.wait_ge(o_taken, 7 + p - 3 + 1)
                            b, src = ring.next(("mean", p), xc_ready, p - 3 + 1), o_ret[:, p - 3, :]
                        else:
                            pe.wait_ge(post_sq, p + 1)
                            b, src = ring.next(("post", p), post_rms, p + 1), psq[p % 2][:]
                        signal_tile(("post" if step else "mean", p),
                                    pe.matmul(b[:], const[:, K_HEAD:K_HEAD + P], src,
                                              start=True, stop=True))

                    for m in range(17):
                        if m < 8:
                            chunk(C_K + m, ring.next(("kx", m), kx_ready, m + 1), memhi, memlo, cols=MEM,
                                  jobs=J_MEM if m == 0 else None)
                        elif m < 16:
                            chunk(C_K + m, ring.next(("v", m + 1), stage_ready, m + 2), memhi, memlo, cols=MEM)
                        if m > 8:
                            turn(9 + m - 9, P, MEM)
                        if m < len(POST):
                            stat_of(*POST[m])

                    def project(c0, job, sem_, v0):
                        for m in range(KT):
                            chunk(c0 + m, ring.next(("proj", c0 + m), sem_, v0 + m + 1), xh, xl,
                                  jobs=job if m == 0 else None)

                    project(C_OUT, J_FEAT, x_ready, 8)
                    norm_stat(2)
                    project(C_Q, J_XA, qx_ready, 0)
                    pe.wait_ge(kx_ready, KT)
                    pe.wait_ge(vtok_ready, 17)
                    assert unit_n[0] == U_XA

                    def xa_scores(n):
                        h, pair = divmod(n, 2)
                        pe.wait_ge(qx_ready, KT)
                        b = scores()
                        for s in range(2):
                            st = 2 * pair + s
                            for dt in range(2):
                                m = pe.matmul(b[:, s * MEM:(s + 1) * MEM],
                                              qx[:, 2 * h + dt, st * P:(st + 1) * P],
                                              kx[:, 2 * h + dt, :], start=dt == 0, stop=dt == 1)
                        m.then_inc(s_full, 1)

                    def xa_turn(n):
                        pe.wait_ge(prob_ready, 2 * n + 2)
                        b = ring.next(("pt", n), pt_ready, n + 1)
                        for mt in range(2):
                            for s in range(2):
                                m = pe.transpose(b[:, (2 * mt + s) * P:(2 * mt + s + 1) * P],
                                                 prob[n % 2][:, s, mt * P:(mt + 1) * P], ident)
                        signal_tile(("pt", n), m)

                    def xa_out(h):
                        pe.wait_ge(pt_ready, 2 * h + 2)
                        for dt in range(2):
                            b = ring.next(("att", 2 * h + dt), val_ready, J_ATT + 2 * h + dt + 1)
                            for mt in range(2):
                                m = pe.matmul(b[:], vx[:, mt, (2 * h + dt) * P:(2 * h + dt + 1) * P],
                                              pt[h % 2][:, mt, :], start=mt == 0, stop=mt == 1)
                            signal_tile(("att", 2 * h + dt), m)

                    N = 2 * XH
                    for n in range(N + 2):
                        if n < N:
                            xa_scores(n)
                        if n >= 1 and n - 1 < N:
                            xa_turn(n - 1)
                        if n >= 3 and n % 2 == 1:
                            xa_out((n - 3) // 2)
                    project(C_O, J_ATT, x_ready, 16)
                    ffn(C_FFB, J_FFB, J_HB, 3)

                @block.scalar
                def _(act):
                    bank, full = rings[-1].of, rings[-1].full
                    spare = act.alloc_register("act_spare")

                    def settle():
                        act.reg_mov(spare, 0)

                    def rows(r, src, n, w=P):
                        act.dma_start(prow[r:r + n, 0:w], src).then_inc(params_in, 16)

                    for r, n in ((R_FFA, "g_ffa"), (R_MIX, "g_mix"), (R_XA, "g_xa"), (R_MEM, "g_mem"),
                                 (R_FFB, "g_ffb")):
                        rows(r, A[n][lay].rearrange("(k p) -> k p", p=P), KT)
                    rows(R_GG, A["gla_g_norm"][lay].rearrange("(k p) -> k p", p=P), 3)
                    rows(R_RG, A["ret_g_norm"][lay].rearrange("(k p) -> k p", p=P), 3)
                    rows(R_CONV, A["ml_conv"][lay].rearrange("j (t p) -> (j t) p", p=P), 16)
                    rows(R_BA, A["gla_b_a"][lay].rearrange("(k p) -> k p", p=GT), 2, GT)
                    act.dma_start(w_a2[:], A["gla_w_a2"][lay]).then_inc(params_in, 16)
                    for n, name in enumerate(("ml_b_i", "ml_b_f")):
                        act.dma_start(b_if[:, n:n + 1], A[name][lay].rearrange("(h o) -> h o", o=1))\
                           .then_inc(params_in, 16)

                    head = [0]

                    def ahead(count=1, n=8):
                        for _ in range(count):
                            c = head[0]
                            act.wait_ge(w_loaded[c % 4], 16 * (c // 4 + 1))
                            if c >= 2:
                                act.wait_ge(chunk_done, c - 1)
                            act.activation(whi[c % 2][:, 0:n], raw[c % 4][:, 0:n], ACT.Copy)\
                               .then_inc(w_hi, 1)
                            head[0] += 1

                    def hi(job, dst, cols=S):
                        act.wait_ge(val_ready, job + 1)
                        act.activation(dst, T[job % 2][:, 0:cols], ACT.Copy).then_inc(hi_ready, 1)

                    def norm(i, job):
                        act.wait_ge(tile_full, full["stat", i])
                        act.activation(stat[:], bank["stat", i][:], ACT.Sqrt, bias=eps)\
                           .then_inc(rms_ready, 1)
                        for k in range(KT):
                            hi(job + k, xh[:, k, :])

                    added = [0]

                    def square_of(m, v0):
                        act.wait_ge(x_ready, v0 + m + 1)
                        if m >= 2:
                            act.wait_ge(sq_added, added[0] + m - 1)
                        act.activation(T[2 + m % 2][:], x[:, m, :], ACT.Square).then_inc(sq_ready, 1)
                        if m == KT - 1:
                            added[0] += KT

                    def ffn(base, job, hjob, i, v0):
                        norm(i, job)

                        def silu(c, s):
                            act.wait_ge(chunk_done, c + 1)
                            if not isinstance(c, int):
                                settle()
                            act.activation(T[2 + s][:], bank["up", i, 2 * s][:], ACT.Silu)\
                               .then_inc(silu_ready, 1)

                        def cut(it, s):
                            q = base + s
                            act.wait_ge(w_loaded[q % 4], it * 16 + 16 * (q // 4 + 1))
                            act.wait_ge(chunk_done, it * 4 + (q - 1))
                            settle()
                            act.activation(whi[q % 2][:], raw[q % 4][:], ACT.Copy).then_inc(w_hi, 1)

                        def hidden(it, s):
                            act.wait_ge(val_ready, it * 2 + (hjob + s + 1))
                            settle()
                            act.activation(hh[:, it * 2 + s, :], T[(hjob + s) % 2][:], ACT.Copy)\
                               .then_inc(hi_ready, 1)

                        ahead()
                        silu(base, 0)
                        ahead()
                        hi(hjob, hh[:, 0, :])
                        with act.Fori(1, NJ // 2) as it:
                            cut(it, 0)
                            silu(it * 4 + (base - 2), 1)
                            cut(it, 1)
                            hidden(it, -1)
                            cut(it, 2)
                            silu(it * 4 + base, 0)
                            cut(it, 3)
                            hidden(it, 0)
                        d = base + FFN_UP
                        head[0] = d
                        ahead()
                        silu(d - 2, 1)
                        ahead(n=7)
                        hi(hjob + NJ - 1, hh[:, NJ - 1, :])
                        for m in range(KT):
                            for q in range(3):
                                if head[0] < CHUNKS:
                                    e = head[0] - d
                                    ahead(n=7 if e < FFN_DOWN and e % 3 else 8)
                            square_of(m, v0)

                    ahead(2)
                    ffn(C_FFA, J_FFA, J_HA, 0, 0)

                    norm(1, J_MIX)
                    ahead(3)
                    links = [0]

                    def link(ins):
                        links[0] += 1
                        ins.then_inc(act_link, 1)
                        act.wait_ge(act_link, links[0])

                    def softplus(buf, src):
                        link(act.activation(buf, src, ACT.Abs))
                        link(act.activation(buf, buf, ACT.Exp, scale=-1.0))
                        act.activation(buf, buf, ACT.Ln, bias=1.0).then_inc(ln_ready, 1)

                    act.wait_ge(row_in, 2)
                    softplus(row_m[0:MH, :], row_b[0:MH, :])
                    act.wait_ge(z_in, 2)
                    softplus(p128[0:GT], p64[0:GT])
                    ahead()
                    act.wait_ge(rows_ready, 3)
                    act.activation(row_e[0:MH, :], row_e[0:MH, :], ACT.Exp, scale=-1.0)\
                       .then_inc(em_ready, 1)

                    def exps(n):
                        v, slot = X_ORDER[n], xs[n % X_SLOTS]
                        act.wait_ge(e_ready, n + 1)
                        if v <= 32:
                            act.activation(slot[0:GT], slot[0:GT], ACT.Exp, scale=1 / 16.0)\
                               .then_inc(exp_ready, 1)
                        else:
                            src = {64: p64, 128: p128, 256: p256}[v]
                            s = slot[0:GT].rearrange("p t (n h v) -> p (t n) h v", h=2, v=v)
                            q = src[0:GT].rearrange("p t (n h v) -> p (t n) h v", h=2, v=v)
                            act.activation(s[:, :, 0, :], s[:, :, 0, :], ACT.Exp, scale=1 / 16.0)
                            act.activation(s[:, :, 1, :], q[:, :, 1, :], ACT.Exp, scale=1 / 16.0)\
                               .then_inc(exp_ready, 1)

                    def conv_silu(n):
                        act.wait_ge(conv_ready, 4 * n + 4)
                        act.activation(mqk[:, n, :], mqk[:, n, :], ACT.Silu).then_inc(mqk_ready, 1)

                    for n in range(3):
                        exps(n)
                    ahead(7)
                    ahead(2)
                    exps(3)
                    exps(4)
                    ahead(2)
                    exps(5)
                    ahead(2)
                    exps(6)
                    ahead(2)
                    exps(7)
                    conv_silu(0)
                    ahead(2)
                    exps(8)
                    conv_silu(1)
                    conv_silu(2)
                    ahead(2)
                    conv_silu(3)
                    ahead()
                    assert head[0] == C_GATE + 2

                    act.wait_ge(o_full, GH)
                    act.dma_start(memraw[:], mem_tok).then_inc(mem_in, 16)

                    for h in range(MH):
                        for jt in range(TB):
                            n = h * TB + jt
                            act.wait_ge(dlog_ready, n + 1)
                            b = T[2 + n % 2][:, 0:S - jt * P]
                            act.activation(b, b, ACT.Exp).then_inc(dexp_ready, 1)
                            if jt % 2 == 1:
                                ahead()
                        if h % 2 == 1:
                            act.wait_ge(o_full, GH + (h + 1) * TB)
                            act.activation(rtmp[:], OB[1][:], ACT.Abs).then_inc(den_abs, 1)
                    for n in range(8):
                        act.wait_ge(gate_copied, n + 1)
                        act.activation(gates[:, n, :], gates[:, n, :],
                                       ACT.Silu if n < 6 else ACT.Sigmoid).then_inc(gate_ready, 1)
                    act.wait_ge(mem_in, 16)
                    act.wait_ge(o_taken, 7)
                    for t in range(2):
                        link(act.activation(memsq[:], memraw[:, t, :], ACT.Square,
                                            accum_out=memst[:, t:t + 1]))
                    act.activation(memst[:, 2:4], memst[:, 0:2], ACT.Sqrt, bias=eps,
                                   scale=1.0 / D).then_inc(mem_rms, 1)
                    for k in range(KT):
                        hi(J_MEM + k, memhi[:, k, :], MEM)

                    for m in range(16):
                        p, step = POST[m] if m < len(POST) else (0, 0)
                        if step:
                            if p < 3:
                                act.wait_ge(o_taken, p + 1)
                            else:
                                act.wait_ge(xc_ready, p - 2)
                            src = o_gla[:, p, :] if p < 3 else o_ret[:, p - 3, :]
                            act.activation(psq[p % 2][:], src, ACT.Square).then_inc(post_sq, 1)
                        ahead()
                        if step:
                            act.wait_ge(tile_full, full["post", p])
                            act.activation(rtmp[:], bank["post", p][:], ACT.Sqrt, bias=eps)\
                               .then_inc(post_rms, 1)
                            hi(J_FEAT + p, xh[:, p, :])
                        if m == len(POST):
                            hi(J_FEAT + 6, xh[:, 6, :])
                            hi(J_FEAT + 7, xh[:, 7, :])

                    for m in range(KT):
                        ahead()
                        square_of(m, 8)
                    norm(2, J_XA)
                    ahead(8)
                    for n in range(2 * XH):
                        act.wait_ge(max_ready, n + 1)
                        if n >= 2:
                            act.wait_ge(pt_ready, n - 1)
                        for s in range(2):
                            act.activation(prob[n % 2][:, s, :],
                                           SB[(U_XA + n) % 2][:, s * MEM:(s + 1) * MEM], ACT.Exp,
                                           bias=smx[:, n % 2, s:s + 1], scale=XDH ** -0.5,
                                           accum_out=smx[:, n % 2, 2 + s:3 + s]).then_inc(prob_exp, 1)
                        if n >= 3 and n % 2 == 1:
                            for dt in range(2):
                                hi(J_ATT + n - 3 + dt, xh[:, n - 3 + dt, :])
                    for dt in range(2):
                        hi(J_ATT + 6 + dt, xh[:, 6 + dt, :])
                    for m in range(KT):
                        ahead()
                        square_of(m, 16)
                    assert head[0] == C_FFB + 2
                    ffn(C_FFB, J_FFB, J_HB, 3, 24)

                @block.vector
                def _(dve):
                    bank, full = rings[-1].of, rings[-1].full
                    links = [0]

                    def link(ins):
                        links[0] += 1
                        ins.then_inc(dve_link, 1)
                        dve.wait_ge(dve_link, links[0])

                    def lo(job, dst, hi_part, cols=S):
                        dve.wait_ge(hi_ready, job + 1)
                        dve.tensor_tensor(dst, T[job % 2][:, 0:cols], hi_part.bitcast(F32),
                                          ALU.subtract).then_inc(lo_ready, 1)

                    def free(job):
                        if job >= 2:
                            dve.wait_ge(lo_ready, job - 1)

                    def norm(i, job, gain):
                        dve.wait_ge(rms_ready, i + 1)
                        link(dve.reciprocal(stat[:], stat[:]))
                        for k in range(KT + 1):
                            if k < KT:
                                free(job + k)
                                dve.scalar_tensor_tensor(T[(job + k) % 2][:], x[:, k, :],
                                                         pcol[:, gain + k:gain + k + 1], stat[:],
                                                         ALU.mult, ALU.mult).then_inc(val_ready, 1)
                            if k >= 1:
                                lo(job + k - 1, xl[:, k - 1, :], xh[:, k - 1, :])

                    added = [0]

                    def add_square(m):
                        dve.wait_ge(sq_ready, added[0] + 1)
                        if m == 0:
                            ins = dve.tensor_copy(stat[:], T[2][:])
                        else:
                            dve.wait_ge(sq_added, added[0])
                            ins = dve.tensor_tensor(stat[:], stat[:], T[2 + m % 2][:], ALU.add)
                        ins.then_inc(sq_added, 1)
                        added[0] += 1

                    def update_x(chunk_of, name_of, factor):
                        for m in range(KT):
                            dve.wait_ge(chunk_done, chunk_of(m) + 1)
                            dve.scalar_tensor_tensor(x[:, m, :], bank[name_of(m)][:], factor,
                                                     x[:, m, :], ALU.mult, ALU.add)\
                               .then_inc(x_ready, 1)
                            if m >= 1:
                                add_square(m - 1)
                        add_square(KT - 1)

                    def ffn(base, job, hjob, i, gain, silus):
                        norm(i, job, gain)
                        with dve.Fori(0, NJ // 2) as it:
                            for s in range(2):
                                dve.wait_ge(chunk_done, it * 4 + (base + 2 * s + 2))
                                dve.wait_ge(silu_ready, it * 2 + (silus + s + 1))
                                dve.wait_ge(lo_ready, it * 2 + (hjob + s - 1))
                                dve.tensor_tensor(T[s][:], T[2 + s][:], bank["up", i, 2 * s + 1][:],
                                                  ALU.mult).then_inc(val_ready, 1)
                                dve.wait_ge(hi_ready, it * 2 + (hjob + s + 1))
                                dve.tensor_tensor(hl[:, it * 2 + s, :], T[s][:],
                                                  hh[:, it * 2 + s, :].bitcast(F32),
                                                  ALU.subtract).then_inc(lo_ready, 1)
                        update_x(lambda m: base + FFN_UP + 3 * m + 2, lambda m: ("down", i, m), 0.5)

                    dve.wait_ge(tile_full, full["params"])
                    dve.tensor_copy(pcol[:], bank["params"][:, 0:N_ROWS]).then_inc(params_up, 1)
                    dve.wait_ge(params_up, 1)
                    ffn(C_FFA, J_FFA, J_HA, 0, R_FFA, 0)

                    norm(1, J_MIX, R_MIX)
                    dve.wait_ge(chunk_done, C_GA + 1)
                    dve.tensor_copy(ga_t[0:16, :], bank["ga"][0:16, :]).then_inc(ga_ready, 1)
                    for n, row in enumerate((row_u, row_b)):
                        dve.wait_ge(chunk_done, C_MI + n + 1)
                        dve.tensor_scalar(row[0:MH, :], bank["row", n][0:MH, :], b_if[:, n:n + 1],
                                          None, ALU.add).then_inc(row_in, 1)
                    for t in range(2):
                        dve.wait_ge(tile_full, full["z", t])
                        dve.tensor_scalar(p64[0:GT, t, :], bank["z", t][0:GT, :],
                                          pcol[0:GT, R_BA + t:R_BA + t + 1], None, ALU.add)\
                           .then_inc(z_in, 1)
                    u, b, mm, em = (r[0:MH, :] for r in (row_u, row_b, row_m, row_e))
                    dve.wait_ge(ln_ready, 1)
                    link(dve.scalar_tensor_tensor(b, b, 0.0, mm, ALU.min, ALU.subtract))
                    link(dve.tensor_tensor_scan(b, b, b, 0.0, ALU.add, ALU.bypass))
                    dve.tensor_tensor(u, u, b, ALU.subtract).then_inc(rows_ready, 1)
                    dve.wait_ge(rows_ready, 1)
                    dve.tensor_tensor_scan(mm, u, u, 0.0, ALU.max, ALU.bypass).then_inc(rows_ready, 1)
                    dve.wait_ge(rows_ready, 2)
                    dve.tensor_tensor(em, b, mm, ALU.add).then_inc(rows_ready, 1)
                    dve.tensor_scalar(mm, mm, -1.0, None, ALU.mult).then_inc(rows_ready, 1)
                    dve.wait_ge(ln_ready, 2)
                    z = p64[0:GT].rearrange("p t s -> p (t s)")
                    link(dve.scalar_tensor_tensor(z, z, 0.0, p128[0:GT].rearrange("p t s -> p (t s)"),
                                                  ALU.min, ALU.subtract))
                    for n in range(16):
                        c = z[:, n * 64:(n + 1) * 64]
                        ins = dve.tensor_tensor_scan(c, c, c, 0.0, ALU.add, ALU.bypass)
                    link(ins)
                    for src, dst, v in ((p64, p128, 64), (p128, p256, 128)):
                        q = src[0:GT].rearrange("p t (n h v) -> p (t n) h v", h=2, v=v)
                        d = dst[0:GT].rearrange("p t (n h v) -> p (t n) h v", h=2, v=v)
                        dve.tensor_copy(d[:, :, 0, :], q[:, :, 0, :])
                        link(dve.tensor_tensor(d[:, :, 1, :], q[:, :, 1, :],
                                               q[:, :, 0, v - 1:v].to_broadcast([GT, S // v, v]),
                                               ALU.add))

                    def halves(t3, v):
                        return t3[0:GT].rearrange("p t (n h v) -> p (t n) h v", h=2, v=v)

                    def exponents(n):
                        v = X_ORDER[n]
                        q = halves({128: p128, 256: p256}.get(v, p64), v)
                        d = halves(xs[n % X_SLOTS], v)
                        mid = q[:, :, 0, v - 1:v].to_broadcast([GT, S // v, v])
                        ins = dve.tensor_tensor(d[:, :, 0, :], mid, q[:, :, 0, :], ALU.subtract)
                        if v <= 32:
                            ins = dve.tensor_tensor(d[:, :, 1, :], q[:, :, 1, :], mid, ALU.subtract)
                        ins.then_inc(e_ready, 1)

                    def factors(n):
                        v = X_ORDER[n]
                        d = halves(xs[n % X_SLOTS], v)
                        dve.wait_ge(exp_ready, n + 1)
                        dve.tensor_tensor(d[:, :, 0, :], d[:, :, 0, :], halves(gk, v)[:, :, 0, :],
                                          ALU.mult)
                        dve.tensor_tensor(d[:, :, 1, :], d[:, :, 1, :], halves(gq, v)[:, :, 1, :],
                                          ALU.mult).then_inc(xs_ready, 1)

                    for n in range(3):
                        exponents(n)
                    for n in range(4):
                        dve.wait_ge(chunk_done, C_GQ + n + 1)
                        if n < 2:
                            ins = dve.tensor_scalar(gq[0:GT, n, :], bank["gqk", n][0:GT, :],
                                                    GDK ** -0.5, None, ALU.mult)
                        else:
                            ins = dve.tensor_copy(gk[0:GT, n - 2, :], bank["gqk", n][0:GT, :])
                        ins.then_inc(gqk_ready, 1)
                    dve.wait_ge(gqk_ready, 4)
                    for n in range(3):
                        factors(n)

                    def stage(n, c, w=P, cols=S):
                        dve.wait_ge(chunk_done, c + 1)
                        dve.tensor_copy(T[2 + n % 2][0:w, 0:cols], bank["v", n][0:w, 0:cols])\
                           .then_inc(stage_ready, 1)

                    def turned(n, dst, w, cols=S):
                        dve.wait_ge(tile_full, full["turn", n])
                        src = bank["turn", n][:, 0:w * (cols // P)].rearrange("p (t c) -> p t c", c=w)
                        dve.tensor_copy(dst, src).then_inc(vtok_ready, 1)

                    for n in range(5):
                        if n < 4:
                            stage(n, C_GV + n, GT)
                        if n >= 1:
                            turned(n - 1, gv[:, :, (n - 1) * GT:n * GT], GT)

                    def rot(n):
                        dve.wait_ge(chunk_done, C_RQ + n + 1)
                        dve.tensor_copy(rqk[0:GT, n, :], bank["rot", n][0:GT, :])\
                           .then_inc(rot_copied, 1)

                    def swap(n):
                        dve.wait_ge(tile_full, full["swap", n])
                        r = rqk[0:GT, n, :]
                        if n >= 1:
                            dve.wait_ge(rot_ready, 2 * n)
                        dve.tensor_tensor(rtmp[0:GT, :], sincos[0:GT, 1, :], bank["swap", n][0:GT, :],
                                          ALU.mult).then_inc(rot_ready, 1)
                        link(dve.tensor_tensor(r, r, sincos[0:GT, 0, :], ALU.mult))
                        dve.tensor_tensor(r, r, rtmp[0:GT, :], ALU.add).then_inc(rot_ready, 1)

                    def conv(n):
                        dve.wait_ge(chunk_done, C_MQK + n + 1)
                        src, dst = bank["mqk", n], mqk[:, n, :]

                        def tap(j):
                            return pcol[:, R_CONV + 4 * j + n:R_CONV + 4 * j + n + 1]

                        dve.tensor_scalar(dst, src[:], tap(3), None, ALU.mult).then_inc(conv_ready, 1)
                        for e in range(1, 4):
                            dve.wait_ge(conv_ready, 4 * n + e)
                            dve.scalar_tensor_tensor(dst[:, e:], src[:, 0:S - e], tap(3 - e),
                                                     dst[:, e:], ALU.mult, ALU.add)\
                               .then_inc(conv_ready, 1)

                    def rv_of(n):
                        turned(n, rv[:, :, (n - 4) * P:(n - 3) * P], P)

                    def mv_of(n):
                        turned(n, mv[:, :, (n - 7) * P:(n - 6) * P], P)

                    fill = [
                        lambda: (rot(0), rot(1), swap(0)),
                        lambda: (rot(2), swap(1), rot(3), swap(2)),
                        lambda: (stage(4, C_RV), swap(3), stage(5, C_RV + 1), rv_of(4)),
                        lambda: (stage(6, C_RV + 2), rv_of(5), conv(0), rv_of(6)),
                        lambda: (conv(1), conv(2)),
                        lambda: (conv(3), stage(7, C_MV)),
                        lambda: (stage(8, C_MV + 1), mv_of(7), mv_of(8)),
                    ]
                    for g in range(7):
                        for h in range(GH):
                            u_ = g * GH + h
                            dve.wait_ge(s_full, u_ + 1)
                            src = SB[u_ % 2][:].rearrange("p (t c) -> p t c", c=P)
                            if g == 0:
                                sel = ident.unsqueeze(1).to_broadcast([P, TB, P])
                                ins = dve.tensor_tensor(sdiag[:, h], src, sel, ALU.mult)
                            else:
                                dve.wait_ge(s_done, u_ - GH + 1)
                                sel = masks[:, g - 1, :].unsqueeze(1).to_broadcast([P, TB, P])
                                ins = dve.copy_predicated(sdiag[:, h], sel, src)
                            ins.then_inc(s_done, 1)
                        nxt = {1: (3, 4), 2: (5,), 3: (6,), 4: (7,), 5: (8,)}.get(g, ())
                        for n in nxt:
                            exponents(n)
                        fill[g]()
                        for n in nxt:
                            factors(n)
                    for h in range(GH):
                        for n in range(2):
                            u_ = U_OFF + 2 * h + n
                            w = S if n == 0 else 256
                            dve.wait_ge(s_full, u_ + 1)
                            if h >= 1:
                                dve.wait_ge(o_full, h)
                            dve.tensor_copy(sm[n][:, 0:w], SB[n][:, 0:w]).then_inc(s_done, 1)
                        if h % 2 == 0 and h >= 2:
                            p = h // 2 - 1
                            dve.tensor_copy(o_gla[:, p, :], OB[p % 2][:]).then_inc(o_taken, 1)
                    dve.wait_ge(o_full, GH)
                    dve.tensor_copy(o_gla[:, 2, :], OB[0][:]).then_inc(o_taken, 1)

                    dve.wait_ge(tile_full, full["ucol"])
                    dve.tensor_copy(ucol[:].rearrange("p t h -> p (t h)"), bank["ucol"][:, 0:TB * MH])\
                       .then_inc(ucol_ready, 1)
                    dve.wait_ge(ucol_ready, 1)

                    def weight_log(n):
                        h, jt = divmod(n, TB)
                        if jt == 0:
                            dve.wait_ge(tile_full, full["negm", h])
                        dve.tensor_scalar(T[2 + n % 2][:, 0:S - jt * P], bank["negm", h][:, jt * P:],
                                          ucol[:, jt, h:h + 1], 0.0, ALU.add, ALU.min)\
                           .then_inc(dlog_ready, 1)

                    def gate(n):
                        dve.wait_ge(chunk_done, C_GATE + n + 1)
                        dve.tensor_copy(gates[:, n, :], bank["gate", n][:]).then_inc(gate_copied, 1)

                    for n in range(MH * TB):
                        h, jt = divmod(n, TB)
                        if jt == 0:
                            weight_log(n)
                        if jt + 1 < TB:
                            weight_log(n + 1)
                        u_, w = U_ML + n, S - jt * P
                        s = sm[u_ % 2]
                        dve.wait_ge(s_full, u_ + 1)
                        dve.wait_ge(dexp_ready, n + 1)
                        dve.wait_ge(o_full, GH + max(n - 1, 0))
                        link(dve.scalar_tensor_tensor(s[:, 0:w], SB[u_ % 2][:, 0:w], MDK ** -0.5,
                                                      T[2 + n % 2][:, 0:w], ALU.mult, ALU.mult))
                        dve.tensor_tensor(s[:, 0:P], s[:, 0:P], const[:, K_CAUSAL:K_CAUSAL + P],
                                          ALU.mult).then_inc(s_done, 1)
                        if jt in (0, 2):
                            gate(2 * h + jt // 2)
                        if h % 2 == 1 and jt == TB - 1:
                            p = h // 2
                            dve.wait_ge(den_abs, p + 1)
                            dve.wait_ge(tile_full, full["em", p])
                            dve.tensor_tensor(rtmp[:], rtmp[:], bank["em", p][:], ALU.max)\
                               .then_inc(o_taken, 1)
                            dve.wait_ge(o_taken, 4 + 2 * p)
                            link(dve.reciprocal(rtmp[:], rtmp[:]))
                            dve.tensor_tensor(o_ml[:, p, :], rtmp[:], OB[0][:], ALU.mult)\
                               .then_inc(o_taken, 1)

                    for n in range(GH * TB):
                        h, jt = divmod(n, TB)
                        u_, w = U_RET + n, S - jt * P
                        dve.wait_ge(s_full, u_ + 1)
                        dve.wait_ge(o_full, GH + MH * TB + n - 1)
                        dve.tensor_tensor(sm[u_ % 2][:, 0:w], SB[u_ % 2][:, 0:w], decay[:, h, 0:w],
                                          ALU.mult).then_inc(s_done, 1)
                        if n >= 8 and n % 8 == 1:
                            p = n // 8 - 1
                            dve.tensor_copy(o_ret[:, p, :], OB[(7 + p) % 2][:]).then_inc(o_taken, 1)
                    dve.wait_ge(o_full, GH + (MH + GH) * TB)
                    dve.tensor_copy(o_ret[:, 2, :], OB[1][:]).then_inc(o_taken, 1)

                    dve.wait_ge(mem_rms, 1)
                    link(dve.reciprocal(memst[:, 2:4], memst[:, 2:4]))
                    for t in range(2):
                        dve.tensor_scalar(memraw[:, t, :], memraw[:, t, :], memst[:, 2 + t:3 + t],
                                          None, ALU.mult).then_inc(memn_ready, 1)
                    for k in range(KT + 1):
                        if k < KT:
                            dve.wait_ge(tile_full, full["mem", k])
                            free(J_MEM + k)
                            dve.tensor_scalar(T[(J_MEM + k) % 2][:, 0:MEM], bank["mem", k][:, 0:MEM],
                                              pcol[:, R_MEM + k:R_MEM + k + 1], None, ALU.mult)\
                               .then_inc(val_ready, 1)
                        if k >= 1:
                            lo(J_MEM + k - 1, memlo[:, k - 1, :], memhi[:, k - 1, :], MEM)

                    def post(p, step):
                        o = o_gla[:, p, :] if p < 3 else o_ret[:, p - 3, :]
                        gain = R_GG + p if p < 3 else R_RG + p - 3
                        if step == 0:
                            dve.wait_ge(tile_full, full["mean", p])
                            dve.tensor_tensor(o, o, bank["mean", p][:], ALU.subtract)\
                               .then_inc(xc_ready, 1)
                            return
                        dve.wait_ge(post_rms, p + 1)
                        link(dve.reciprocal(rtmp[:], rtmp[:]))
                        link(dve.scalar_tensor_tensor(o, o, pcol[:, gain:gain + 1], rtmp[:],
                                                      ALU.mult, ALU.mult))
                        gated(p, o)

                    def gated(p, o):
                        dve.wait_ge(gate_ready, p + 1)
                        free(J_FEAT + p)
                        dve.tensor_tensor(T[(J_FEAT + p) % 2][:], o, gates[:, p, :], ALU.mult)\
                           .then_inc(val_ready, 1)
                        lo(J_FEAT + p, xl[:, p, :], xh[:, p, :])

                    for m in range(17):
                        if m < 8:
                            dve.wait_ge(chunk_done, C_K + m + 1)
                            dve.tensor_copy(kx[:, m, :], bank["kx", m][:, 0:MEM]).then_inc(kx_ready, 1)
                        elif m < 16:
                            stage(m + 1, C_K + m, P, MEM)
                        if m > 8:
                            turned(m, vx[:, :, (m - 9) * P:(m - 8) * P], P, MEM)
                        if m < len(POST):
                            post(*POST[m])
                        if m == len(POST):
                            gated(6, o_ml[:, 0, :])
                            gated(7, o_ml[:, 1, :])

                    update_x(lambda m: C_OUT + m, lambda m: ("proj", C_OUT + m), 1.0)

                    norm(2, J_XA, R_XA)
                    for m in range(KT):
                        dve.wait_ge(chunk_done, C_Q + m + 1)
                        dve.tensor_copy(qx[:, m, :], bank["proj", C_Q + m][:]).then_inc(qx_ready, 1)
                    N = 2 * XH
                    for n in range(N + 2):
                        if n < N:
                            st = smx[:, n % 2, :]
                            dve.wait_ge(s_full, U_XA + n + 1)
                            link(dve.tensor_reduce(
                                st[:, 0:2], SB[(U_XA + n) % 2][:].rearrange("p (s m) -> p s m", s=2),
                                AX.X, ALU.max))
                            dve.tensor_scalar(st[:, 0:2], st[:, 0:2], -XDH ** -0.5, None, ALU.mult)\
                               .then_inc(max_ready, 1)
                            dve.wait_ge(prob_exp, 2 * n + 2)
                            dve.reciprocal(st[:, 2:4], st[:, 2:4]).then_inc(s_done, 1)
                            dve.wait_ge(s_done, U_XA + n + 1)
                            for s in range(2):
                                dve.tensor_scalar(prob[n % 2][:, s, :], prob[n % 2][:, s, :],
                                                  st[:, 2 + s:3 + s], None, ALU.mult)\
                                   .then_inc(prob_ready, 1)
                        if 1 <= n <= N:
                            h, pair = divmod(n - 1, 2)
                            dve.wait_ge(tile_full, full["pt", n - 1])
                            dve.tensor_copy(pt[h % 2][:, :, pair * 256:(pair + 1) * 256],
                                            bank["pt", n - 1][:].rearrange("p (m c) -> p m c", m=2))\
                               .then_inc(pt_ready, 1)
                        if n >= 3 and n % 2 == 1:
                            for k in (n - 3, n - 2):
                                dve.wait_ge(tile_full, full["att", k])
                                free(J_ATT + k)
                                dve.tensor_copy(T[(J_ATT + k) % 2][:], bank["att", k][:])\
                                   .then_inc(val_ready, 1)
                                lo(J_ATT + k, xl[:, k, :], xh[:, k, :])
                    update_x(lambda m: C_O + m, lambda m: ("proj", C_O + m), 1.0)
                    ffn(C_FFB, J_FFB, J_HB, 3, R_FFB, NJ)

            for s in loop_sems:
                nc.gpsimd.sem_clear(s)
            nc.all_engine_barrier()

        with nc.Block() as block:
            @block.sync
            def _(sp):
                sp.dma_start(prow[0:KT, :], A["g_final"].rearrange("(k p) -> k p", p=P))\
                  .then_inc(y_in, 16)
                for t in range(TB):
                    sp.wait_ge(y_ready, 2 * KT + 1)
                    sp.dma_start(out_tok[:, t, :], yout[:, t, :]).then_inc(y_out, 16)
                sp.wait_ge(y_out, 16 * TB)

            @block.scalar
            def _(act):
                act.wait_ge(y_pe, 1)
                act.activation(stat[:], psum[0][:], ACT.Sqrt, bias=eps).then_inc(y_act, 1)

            @block.tensor
            def _(pe):
                pe.matmul(psum[0][:], const[:, K_MEAN:K_MEAN + 1].to_broadcast([P, P]), stat[:], start=True, stop=True)\
                  .then_inc(y_pe, 1)
                pe.wait_ge(y_in, 16)
                pe.transpose(psum[1][:, 0:KT], prow[0:KT, :], ident[0:KT, 0:KT]).then_inc(y_pe, 1)
                for k in range(KT):
                    pe.wait_ge(y_ready, 1 + (2 * k + 1 if k < 2 else 2 * k))
                    for t in range(TB):
                        m = pe.transpose(psum[2 + k % 6][:, t * P:(t + 1) * P],
                                         yk[k % 2][:, t * P:(t + 1) * P], ident)
                    m.then_inc(y_pe, 1)

            @block.vector
            def _(dve):
                dve.wait_ge(y_pe, 2)
                dve.tensor_copy(pcol[:, 0:KT], psum[1][:, 0:KT]).then_inc(y_ready, 1)
                dve.wait_ge(y_ready, 1)
                dve.wait_ge(y_act, 1)
                dve.reciprocal(stat[:], stat[:]).then_inc(y_act, 1)
                dve.wait_ge(y_act, 2)

                def value(k):
                    dve.scalar_tensor_tensor(yk[k % 2][:], x[:, k, :], pcol[:, k:k + 1], stat[:],
                                             ALU.mult, ALU.mult).then_inc(y_ready, 1)

                value(0)
                value(1)
                for k in range(KT):
                    dve.wait_ge(y_pe, 3 + k)
                    dve.tensor_copy(yout[:, :, k * P:(k + 1) * P],
                                    psum[2 + k % 6][:].rearrange("p (t c) -> p t c", c=P))\
                       .then_inc(y_ready, 1)
                    if k + 2 < KT:
                        value(k + 2)


_INS = ["x", "mem", "positions", "g_ffa", "w_ffa_gu", "w_ffa_down", "g_mix", "w_in", "gla_w_a2",
        "gla_b_a", "gla_g_norm", "ret_g_norm", "ml_conv", "ml_b_i", "ml_b_f", "w_out", "g_xa",
        "g_mem", "w_xa_q", "w_xa_kv", "w_xa_o", "g_ffb", "w_ffb_gu", "w_ffb_down", "g_final"]


def kernel(**inputs):
    import numpy as _np
    import concourse.bacc as _bacc
    from concourse import mybir as _mybir
    from concourse.bass_utils import run_bass_kernel_spmd as _run

    nc = _bacc.Bacc("TRN2", target_bir_lowering=False, num_devices=1)
    c, decay, masks = constants()
    given = {n: _np.ascontiguousarray(inputs[n]) for n in _INS}
    given |= {"c_const": c, "c_decay": decay, "c_masks": masks}
    arrays, args = {}, {}
    for name, a in given.items():
        arrays[f"in_{name}_dram"] = a
        args[name] = nc.dram_tensor(f"in_{name}_dram", a.shape, _mybir.dt.from_np(a.dtype),
                                    kind="ExternalInput").ap()
    out = nc.dram_tensor("out_0_dram", (1, S, D), _mybir.dt.float32, kind="ExternalOutput").ap()
    build(nc, args, out)
    r = _run(nc, [arrays], core_ids=[0])
    return r.results[0]["out_0_dram"]
```

```python
import numpy as np
import concourse.bass as bass
from concourse import mybir
from contextlib import ExitStack

F32 = mybir.dt.float32
F32R = mybir.dt.float32r
U8 = mybir.dt.uint8
I32 = mybir.dt.int32
ALU = mybir.AluOpType
ACT = mybir.ActivationFunctionType
AX = mybir.AxisListType

P = 128
D, S, DEPTH, MEM = 1024, 512, 2, 256
KT = D // P
TB = S // P
DFF = 2816
NJ = DFF // P
EPS = 1e-6
GH, GDK, DV = 6, 32, 64
MH, MDK = 4, 64
XH, XDH = 4, 256
SIZES = [192, 192, 384, 16, 384, 192, 192, 384, 384, 256, 256, 256, 256, 4, 4]
(GQ0, GK0, GV0, GA0, GR0, RQ0, RK0, RV0, RG0, MQ0, MK0, MV0, MO0, MI0, MF0) = (
    int(v) for v in np.cumsum([0] + SIZES[:-1]))
D_IN = sum(SIZES)

FFN_UP, FFN_DOWN = 2 * NJ, 3 * KT
DOWN_PARTS = [(0, 8), (8, 15), (15, 22)]
C_FFA = 0
HALF = P // 2
MIX = ([[(0, GA0, 16), (32, MI0, 4), (64, MF0, 4)]]
       + [[(0, GQ0, P)], [(0, GK0, P)], [(0, GK0 + P, HALF), (HALF, GQ0 + P, HALF)]]
       + [[(0, GV0 + P * i, P)] for i in range(3)]
       + [[(0, RQ0, P)], [(0, RK0 + P, HALF), (HALF, RQ0 + P, HALF)], [(0, RK0, P)]]
       + [[(0, c + P * i, P)] for c, n in ((RV0, 3), (MQ0, 2), (MK0, 2), (MV0, 2), (GR0, 3), (RG0, 3),
                                           (MO0, 2)) for i in range(n)])
C_MIX = FFN_UP + FFN_DOWN
(C_GA, C_GQK, C_GV, C_ROT, C_RV, C_MQK, C_MV, C_GATE) = (
    C_MIX + i for i in (0, 1, 4, 7, 10, 13, 17, 19))
C_K = C_MIX + len(MIX)
C_V, C_OUT, C_Q, C_O = C_K + 8, C_K + 16, C_K + 24, C_K + 32
C_FFB = C_K + 40
assert DEPTH == 2
CHUNKS = C_FFB + FFN_UP + FFN_DOWN

J_FFA, J_HA, J_MIX, J_MEM, J_FEAT, J_XA, J_ATT, J_FFB, J_HB, J_END = (
    -8, 0, 22, 30, 38, 46, 54, 62, 70, 92)


def head_at(h):
    return (0, GDK * h) if h < 4 else (1, HALF + GDK * (h - 4))


def cut(job):
    return job + 1 + KT



R_FFA, R_MIX, R_XA, R_MEM, R_FFB, R_GG, R_RG, R_CONV, R_BA = 0, 8, 16, 24, 32, 40, 43, 46, 62
N_ROWS = 64
LAYER_DMAS = 10

K_ID, K_CAUSAL, K_HEAD, K_MEAN, K_ONE, K_SWAP, K_FREQ, K_EPS = (
    0, 128, 256, 384, 385, 386, 514, 515)
K_N = 516

HEAVY_LEVELS = [64, 32]
LEVELS = [16, 8, 4, 2, 1]
X_ORDER = [64, 32, 16, 8, 4, 2, 1, 256, 128]
X_SLOTS = 3
U_OFF = GH * (2 + len(LEVELS))
U_XA = U_OFF + 2 * GH
ML_STEPS, RET_STEPS = MH // 2 * TB, GH // 2 * TB
MEM_TURNS = {2: (0,), 3: (1,), 4: (2,), 5: (3,), 6: (4, 5), 7: (6, 7)}
GLA_NORMS = {1: 0, 4: 1, 5: 2}
POST = {0: (0, 2), 1: (6, 2), 2: (1, 2), 3: (7, 2), 4: (2, 2), 5: (3, 0), 6: (3, 1), 9: (4, 0),
        10: (4, 1), 13: (5, 0), 14: (5, 1)}
FEAT_ORDER = [0, 6, 1, 7, 2, 3, 4, 5]


XA_STEPS = [("query", 0), ("query", 1), ("scores", 0), ("query", 2), ("scores", 1), ("query", 3),
            ("turn", 0), ("scores", 2), ("query", 4), ("turn", 1), ("scores", 3), ("query", 5),
            ("turn", 2), ("scores", 4), ("query", 6), ("turn", 3), ("scores", 5), ("query", 7),
            ("turn", 4), ("scores", 6), ("turn", 5), ("scores", 7), ("out", 0), ("turn", 6),
            ("out", 1), ("turn", 7), ("out", 2), ("out", 3)]


def constants():
    c = np.zeros((P, K_N), np.float32)
    j, i = np.arange(P)[:, None], np.arange(P)[None, :]
    c[:, K_ID:K_ID + P] = np.eye(P)
    c[:, K_CAUSAL:K_CAUSAL + P] = j <= i
    c[:, K_HEAD:K_HEAD + P] = (j // DV == i // DV) / DV
    c[:, K_MEAN] = 1.0 / D
    c[:, K_ONE] = 1.0
    half = GDK // 2
    for h in range(P // GDK):
        for r in range(half):
            c[GDK * h + half + r, K_SWAP + GDK * h + r] = -1.0
            c[GDK * h + r, K_SWAP + GDK * h + half + r] = 1.0
    freq = (np.float32(1.0) / (np.float32(10000.0) ** np.linspace(0, 1, half, dtype=np.float32)))
    c[:, K_FREQ] = np.tile(freq.astype(np.float32), P // half)
    c[:, K_EPS] = EPS
    lg = np.log(1.0 - 2.0 ** (-5.0 - np.arange(GH)))
    rel = np.arange(S)[None, :] - np.arange(P)[:, None]
    dec = np.where(rel >= 0, np.exp(lg[:, None, None] * np.maximum(rel, 0)), 0.0) * GDK ** -0.5
    decay = np.ascontiguousarray(dec.transpose(1, 0, 2)).astype(np.float32)
    masks = np.zeros((P, 6, P), bool)
    for n, low in enumerate([HEAVY_LEVELS] + [[v] for v in LEVELS]):
        for v in low:
            masks[:, n] |= ((j // (2 * v) == i // (2 * v)) & (j % (2 * v) < v) & (i % (2 * v) >= v))
    return c, decay, masks.astype(np.float32)


class Banks:

    def __init__(self, engine, banks):
        self.engine, self.banks, self.n = engine, banks, 0
        self.freed, self.of, self.full = [None] * len(banks), {}, {}

    def next(self, name, sem, value):
        b = self.n % len(self.banks)
        if self.freed[b] is not None:
            self.engine.wait_ge(*self.freed[b])
        self.freed[b] = (sem, value)
        self.n += 1
        assert name not in self.of, name
        self.of[name] = self.banks[b]
        return self.banks[b]

    def there(self, name):
        self.full[name] = len(self.full) + 1


def build(nc, A, out):
    ctx = ExitStack()
    with ctx:
        at = [-(-nc.sbuf_base // 32) * 32]

        def place(name, shape, dt=F32, offset=None):
            size = int(np.prod(shape[1:])) * (1 if dt == U8 else 4)
            o = at[0] if offset is None else offset
            if offset is None:
                at[0] += -(-size // 32) * 32
                assert at[0] <= nc.sbuf_usable_end, (name, at[0])
            return nc.alloc_sbuf_tensor_at(name, shape, dt, offset=o)

        UNIT = S * 4
        x = place("x", [P, KT, S])
        xh = place("xh", [P, KT, S], F32R)
        xl = place("xl", [P, KT, S], F32R)
        raw = [place(f"w_raw{i}", [P, 8, P]) for i in range(4)]
        whi = [place(f"w_hi{i}", [P, 8, P], F32R) for i in range(2)]
        wlo = [place(f"w_lo{i}", [P, 8, P], F32R) for i in range(2)]
        region = at[0]
        hh = place("h_hi", [P, NJ, S], F32R)
        hl = place("h_lo", [P, NJ, S], F32R)

        def unit(name, first, shape, dt=F32):
            assert first * UNIT + int(np.prod(shape[1:])) * 4 <= 2 * NJ * UNIT
            return place(name, shape, dt, region + first * UNIT)

        gq = unit("gq", 0, [P, 2, S])
        gk = unit("gk", 2, [P, 2, S])
        p64 = unit("p64", 4, [P, 2, S])
        p128 = unit("p128", 6, [P, 2, S])
        p256 = unit("p256", 8, [P, 2, S])
        xs = [unit(f"xs{i}", 10 + 2 * i, [P, 2, S]) for i in range(X_SLOTS)]
        sdiag = unit("sdiag", 16, [P, GH, TB, P])
        gv = unit("gv", 22, [P, TB, GH * DV])
        rqk = unit("rqk", 25, [P, 4, S])
        rv = unit("rv", 29, [P, TB, GH * DV])
        mqk = unit("mqk", 32, [P, 4, S])
        mv = unit("mv", 36, [P, TB, MH * DV])
        row_u = unit("row_u", 38, [P, S])
        row_b = unit("row_b", 39, [P, S])
        row_m = unit("row_m", 40, [P, S])
        row_e = unit("row_e", 41, [P, S])
        sm = [unit(f"sm{i}", 42 + i, [P, S]) for i in range(2)]
        ga_t = unit("ga_t", 10, [P, S])
        gates = unit("gates", 0, [P, 8, S])
        negm = [unit(f"negm{i}", 8 + i, [P, S]) for i in range(2)]
        gsq0 = unit("gsq0", 10, [P, S])
        sm += [unit(f"sm{i}", 11 + i, [P, S]) for i in range(2, 4)]
        o_ret = unit("o_ret", 8, [P, 3, S])
        o_ml = unit("o_ml", 11, [P, 2, S])
        memraw = unit("memraw", 13, [P, 2, D])
        memhi = unit("memhi", 17, [P, KT, MEM], F32R)
        memlo = unit("memlo", 21, [P, KT, MEM], F32R)
        psq = [unit(f"psq{i}", 40 + i, [P, S]) for i in range(2)]
        kx = unit("kx", 32, [P, KT, MEM])
        vx = unit("vx", 36, [P, 2, D])
        memsq = unit("memsq", 17, [P, D])
        ah = unit("a_hi", 0, [P, KT, S], F32R)
        al = unit("a_lo", 8, [P, KT, S], F32R)
        qx = unit("qx", 16, [P, KT, S])
        prob = [unit(f"prob{i}", 24 + i, [P, 2, MEM]) for i in range(2)]
        pt = [unit(f"pt{i}", 40 if i == 3 else 26 + 2 * i, [P, 2, S]) for i in range(XH)]
        xin = unit("xin", 0, [P, TB, D])
        prow = unit("prow", 22, [P, P])
        pfin = unit("pfin", 23, [P, P])
        posi = unit("posi", 16, [P, S], I32)
        ang = unit("ang", 17, [P, S])
        turns_i = unit("turns_i", 18, [P, S], I32)
        turns = unit("turns", 19, [P, S])
        masks_in = unit("masks_in", 20, [P, 6, P])
        yout = unit("yout", 0, [P, TB, D])
        yk = [unit(f"yk{i}", 16 + i, [P, S]) for i in range(2)]

        T = [place(f"tmp{i}", [P, S]) for i in range(4)]
        stat = place("stat", [P, S])
        o_gla = place("o_gla", [P, 3, S])
        rtmp = place("rtmp", [P, S])
        gsq = [gsq0, rtmp]
        sincos = place("sincos", [P, 2, S])
        decay = place("decay", [P, GH, S])
        const = place("const", [P, K_N])
        masks = place("masks", [P, 6, P], U8)
        pcols = place("pcols", [P, DEPTH * N_ROWS + KT])
        pcol = place("pcol", [P, N_ROWS])
        w_a2 = place("w_a2", [16, GH * GDK])
        b_if = place("b_if", [MH, 2])
        ucol = place("ucol", [P, TB, MH])
        memst = place("memst", [P, 4])
        smx = place("smx", [P, 2, 4])
        ident = const[:, K_ID:K_ID + P]
        eps = const[:, K_EPS:K_EPS + 1]

        psum = [ctx.enter_context(nc.psum_tensor(f"bank{i}", [P, S], F32)) for i in range(8)]
        RB, SB, OB = psum[0:4], psum[4:6], psum[6:8]
        LB = psum[4:8]

        loop_sems = []
        rings = []

        def sem(name):
            s = ctx.enter_context(nc.semaphore(name))
            loop_sems.append(s)
            return s

        w_loaded = [sem(f"w_loaded{i}") for i in range(4)]
        w_pieces = [sem(f"w_pieces{i}") for i in range(4)]
        w_hi, w_lo, chunk_done = sem("w_hi"), sem("w_lo"), sem("chunk_done")
        val_ready, hi_ready, lo_ready = sem("val_ready"), sem("hi_ready"), sem("lo_ready")
        tile_full = sem("tile_full")
        sq_added, rms_ready, sq_ready = sem("sq_added"), sem("rms_ready"), sem("sq_ready")
        a_scaled, g_scaled = sem("a_scaled"), sem("g_scaled")
        silu_ready, params_in, params_up = sem("silu_ready"), sem("params_in"), sem("params_up")
        biases_in = sem("biases_in")
        ga_ready, row_in, z_in, ln_ready = sem("ga_ready"), sem("row_in"), sem("z_in"), sem("ln_ready")
        act_link, dve_link = sem("act_link"), sem("dve_link")
        rows_ready, em_ready = sem("rows_ready"), sem("em_ready")
        gqk_ready, stage_ready, vtok_ready = sem("gqk_ready"), sem("stage_ready"), sem("vtok_ready")
        rot_copied, rot_ready = sem("rot_copied"), sem("rot_ready")
        conv_ready, mqk_ready = sem("conv_ready"), sem("mqk_ready")
        gate_copied, gate_ready = sem("gate_copied"), sem("gate_ready")
        e_ready, exp_ready, xs_ready = sem("e_ready"), sem("exp_ready"), sem("xs_ready")
        s_full, s_done = sem("s_full"), sem("s_done")
        normed = sem("normed")
        ml_full, ml_done, negm_ready = sem("ml_full"), sem("ml_done"), sem("negm_ready")
        ret_full, ret_done = sem("ret_full"), sem("ret_done")
        o_full, o_taken, den_abs = sem("o_full"), sem("o_taken"), sem("den_abs")
        ucol_ready, dlog_ready, dexp_ready = sem("ucol_ready"), sem("dlog_ready"), sem("dexp_ready")
        xc_ready, post_sq, post_rms = sem("xc_ready"), sem("post_sq"), sem("post_rms")
        mem_in, mem_rms, memn_ready = sem("mem_in"), sem("mem_rms"), sem("memn_ready")
        kx_ready, qx_ready, pt_ready = sem("kx_ready"), sem("qx_ready"), sem("pt_ready")
        max_ready, prob_exp, prob_ready = sem("max_ready"), sem("prob_exp"), sem("prob_ready")

        w_first = [ctx.enter_context(nc.semaphore(f"w_first{i}")) for i in range(4)]
        once_in, angle_in, decay_in, masks_in_, params_all, once_pe, once_dve, once_act, x_in = (
            ctx.enter_context(nc.semaphore(n))
            for n in ("once_in", "angle_in", "decay_in", "masks_in", "params_all", "once_pe",
                      "once_dve", "once_act", "x_in"))
        angle_step = ctx.enter_context(nc.semaphore("angle_step"))
        y_pe, y_ready, y_out, y_act = (
            ctx.enter_context(nc.semaphore(n)) for n in ("y_pe", "y_ready", "y_out", "y_act"))

        x_tok = A["x"].rearrange("b (t p) d -> p (b t) d", p=P)
        mem_tok = A["mem"].rearrange("b (t p) d -> p (b t) d", p=P)
        out_tok = out.rearrange("b (t p) d -> p (b t) d", p=P)

        gu = [A[n].rearrange("l (k p) (h j c) -> l h j p k c", p=P, h=2, c=P)
              for n in ("w_ffa_gu", "w_ffb_gu")]

        def load_first(sp, layer):
            for c in range(4):
                if layer > 0:
                    last = CHUNKS - 1 - (CHUNKS - 1 - c) % 4
                    sp.wait_ge(w_hi, last + 1)
                    sp.wait_ge(w_lo, last + 1)
                sp.dma_start(raw[c][:], gu[0][layer, c % 2, c // 2]).then_inc(w_first[c], 16)

        with nc.Block() as block:
            def layer_params(engine, l):
                def rows(r, src, n):
                    r += l * N_ROWS
                    engine.dma_start(prow[r:r + n, :], src).then_inc(params_all, 16)

                for r, n in ((R_FFA, "g_ffa"), (R_MIX, "g_mix"), (R_XA, "g_xa"), (R_MEM, "g_mem"),
                             (R_FFB, "g_ffb")):
                    rows(r, A[n][l].rearrange("(k p) -> k p", p=P), KT)
                rows(R_GG, A["gla_g_norm"][l].rearrange("(k p) -> k p", p=P), 3)
                rows(R_RG, A["ret_g_norm"][l].rearrange("(k p) -> k p", p=P), 3)
                rows(R_CONV, A["ml_conv"][l].rearrange("j (t p) -> (j t) p", p=P), 16)
                b_a = A["gla_b_a"].rearrange("l (o c) -> l o c", o=1)
                for t in range(2):
                    rows(R_BA + t, b_a[l, :, t * HALF:t * HALF + P], 1)

            @block.sync
            def _(sp):
                for t in range(TB):
                    sp.dma_start(xin[:, t, :], x_tok[:, t, :]).then_inc(x_in, 16)
                load_first(sp, 0)
                layer_params(sp, 1)
                sp.dma_start(decay[:], A["c_decay"]).then_inc(decay_in, 16)
                sp.wait_ge(decay_in, 16)

            @block.scalar
            def _(act):
                act.dma_start(posi[:], A["positions"].to_broadcast([P, S])).then_inc(angle_in, 16)
                act.dma_start(const[:], A["c_const"]).then_inc(once_in, 16)
                layer_params(act, 0)
                act.dma_start(pfin[0:KT, :], A["g_final"].rearrange("(k p) -> k p", p=P))\
                   .then_inc(params_all, 16)
                act.dma_start(masks_in[:], A["c_masks"]).then_inc(masks_in_, 16)
                act.wait_ge(once_dve, 1)
                act.activation(sincos[:, 1, :], ang[:], ACT.Sin).then_inc(once_act, 1)
                act.activation(turns[:], ang[:], ACT.Abs).then_inc(once_act, 1)
                act.wait_ge(once_dve, 2)
                act.activation(sincos[:, 0, :], turns[:], ACT.Sin)
                for k in range(KT):
                    act.wait_ge(once_dve, 3 + k)
                    if k >= 2:
                        act.wait_ge(once_dve, 3 + KT + k - 2)
                    act.activation(T[k % 2][:], x[:, k, :], ACT.Square).then_inc(once_act, 1)

            @block.tensor
            def _(pe):
                pe.wait_ge(once_in, 16)
                pe.wait_ge(x_in, 16 * TB)
                for k in range(KT):
                    for t in range(TB):
                        m = pe.transpose(psum[k][:, t * P:(t + 1) * P],
                                         xin[:, t, k * P:(k + 1) * P], ident)
                    m.then_inc(once_pe, 1)
                pe.wait_ge(params_all, 16 * (2 * LAYER_DMAS + 1))
                pe.wait_ge(once_dve, 3)
                pe.transpose(psum[0][:, 0:P], prow[:], ident)
                pe.transpose(psum[0][:, P:P + KT], pfin[0:KT, :], ident[0:KT, 0:KT])\
                  .then_inc(once_pe, 1)

            @block.vector
            def _(dve):
                two_pi = 2.0 * np.pi
                c1 = 6.28125
                c2 = float(np.float32(np.floor((two_pi - c1) * 2 ** 21) / 2 ** 21))
                c3 = float(two_pi - c1 - c2)
                steps = [0]

                def step(ins):
                    steps[0] += 1
                    ins.then_inc(angle_step, 1)
                    dve.wait_ge(angle_step, steps[0])

                dve.wait_ge(angle_in, 16)
                step(dve.tensor_copy(turns[:], posi[:]))
                dve.wait_ge(once_in, 16)
                step(dve.tensor_scalar(ang[:], turns[:], const[:, K_FREQ:K_FREQ + 1],
                                       None, ALU.mult))
                step(dve.tensor_scalar(turns[:], ang[:], 1.0 / two_pi, None, ALU.mult))
                step(dve.tensor_copy(turns_i[:], turns[:]))
                step(dve.tensor_copy(turns[:], turns_i[:]))
                for c in (c1, c2, c3):
                    step(dve.scalar_tensor_tensor(ang[:], turns[:], -c, ang[:],
                                                  ALU.mult, ALU.add))
                dve.tensor_scalar(ang[:], ang[:], 3.1415925, -3.1415925,
                                  ALU.min, ALU.max).then_inc(once_dve, 1)
                dve.wait_ge(once_act, 2)
                dve.tensor_scalar(turns[:], turns[:], -1.0, float(np.pi / 2),
                                  ALU.mult, ALU.add).then_inc(once_dve, 1)
                for k in range(KT):
                    dve.wait_ge(once_pe, k + 1)
                    dve.tensor_copy(x[:, k, :], psum[k][:]).then_inc(once_dve, 1)
                for k in range(KT):
                    dve.wait_ge(once_act, 3 + k)
                    if k == 0:
                        dve.tensor_copy(stat[:], T[0][:]).then_inc(once_dve, 1)
                    else:
                        dve.wait_ge(once_dve, 2 + KT + k)
                        dve.tensor_tensor(stat[:], stat[:], T[k % 2][:], ALU.add).then_inc(once_dve, 1)
                dve.wait_ge(once_pe, KT + 1)
                dve.tensor_copy(pcols[:], psum[0][:, 0:DEPTH * N_ROWS + KT])
                dve.wait_ge(masks_in_, 16)
                dve.tensor_copy(masks[:], masks_in[:])

        w_in = A["w_in"].rearrange("l (k p) c -> l p k c", p=P)
        down = [A[n].rearrange("l (k p) (m c) -> l m p k c", p=P, c=P)
                for n in ("w_ffa_down", "w_ffb_down")]
        w_kv = A["w_xa_kv"].rearrange("l (k p) c -> l p k c", p=P)
        square = {n: A[n].rearrange("l (k p) c -> l p k c", p=P) for n in ("w_out", "w_xa_q", "w_xa_o")}

        with nc.Fori(0, DEPTH) as lay:
            with nc.Block() as block:

                @block.sync
                def _(sp):
                    def slot_free(c):
                        sp.wait_ge(w_hi, c - 3)
                        sp.wait_ge(w_lo, c - 3)

                    def load(c, src):
                        slot_free(c)
                        n, w = src.shape[-2], src.shape[-1]
                        sp.dma_start(raw[c % 4][:, 0:n, 0:w], src).then_inc(w_loaded[c % 4], 16)

                    def ffn(base, w_up, w_down):
                        for c in range(4 if base > 0 else 0):
                            load(base + c, w_up[lay, c % 2, c // 2])
                        with sp.Fori(1, NJ // 2) as it:
                            for s in range(4):
                                slot_free(it * 4 + (base + s))
                                sp.dma_start(raw[(base + s) % 4][:], w_up[lay, s % 2, it * 2 + s // 2])\
                                  .then_inc(w_loaded[(base + s) % 4], 16)
                        for m in range(KT):
                            for i, (k0, k1) in enumerate(DOWN_PARTS):
                                load(base + FFN_UP + 3 * m + i, w_down[lay, m, :, k0:k1, :])

                    ffn(C_FFA, gu[0], down[0])
                    for i, pieces in enumerate(MIX):
                        c = C_MIX + i
                        slot_free(c)
                        for n, (at_, c0, w) in enumerate(pieces):
                            sp.dma_start(raw[c % 4][:, :, at_:at_ + w], w_in[lay, :, :, c0:c0 + w])\
                              .then_inc(w_loaded[c % 4] if n == 0 else w_pieces[c % 4], 16)
                    for m in range(16):
                        load(C_K + m, w_kv[lay, :, :, m * P:(m + 1) * P])
                    for c0, n in ((C_OUT, "w_out"), (C_Q, "w_xa_q"), (C_O, "w_xa_o")):
                        for m in range(KT):
                            load(c0 + m, square[n][lay, :, :, m * P:(m + 1) * P])
                    ffn(C_FFB, gu[1], down[1])
                    load_first(sp, DEPTH - 1)

                @block.gpsimd
                def _(pool):
                    def lo(c, parity, n=8):
                        pool.wait_ge(w_hi, c + 1)
                        r = raw[parity % 4]
                        pool.tensor_tensor(wlo[parity % 2][:, 0:n], r[:, 0:n],
                                           whi[parity % 2][:, 0:n].bitcast(F32),
                                           ALU.subtract).then_inc(w_lo, 1)

                    def ffn(base):
                        with pool.Fori(0, NJ // 2) as it:
                            for s in range(4):
                                lo(it * 4 + (base + s), base + s)
                        for m in range(KT):
                            for i, (k0, k1) in enumerate(DOWN_PARTS):
                                c = base + FFN_UP + 3 * m + i
                                lo(c, c, k1 - k0)

                    ffn(C_FFA)
                    for c in range(C_MIX, C_FFB):
                        lo(c, c)
                    ffn(C_FFB)

                @block.tensor
                def _(pe):
                    ring = Banks(pe, RB)
                    rings.append(ring)

                    def signal_tile(name, m):
                        ring.there(name)
                        m.then_inc(tile_full, 1)

                    def chunk(c, bank, rhs_hi, rhs_lo, k0=0, k1=8, w=P, jobs=None, start=True,
                              stop=True, parity=None, cols=S, order=None):
                        q = c if parity is None else parity
                        pe.wait_ge(w_lo, c + 1)
                        o, wh, wl = bank[0:w, 0:cols], whi[q % 2], wlo[q % 2]
                        for n, k in enumerate(order or range(k0, k1)):
                            if jobs is not None:
                                pe.wait_ge(lo_ready, cut(jobs + n))
                            pe.matmul(o, wl[:, k - k0, 0:w], rhs_hi[:, k, :],
                                      start=start and n == 0, stop=False)
                            pe.matmul(o, wh[:, k - k0, 0:w], rhs_lo[:, k, :], start=False, stop=False)
                        for k in range(k0, k1):
                            m = pe.matmul(o, wh[:, k - k0, 0:w], rhs_hi[:, k, :], start=False,
                                          stop=stop and k == k1 - 1)
                        m.then_inc(chunk_done, 1)

                    def norm_stat(i):
                        if i > 0:
                            pe.wait_ge(sq_added, KT * i)
                        ring.of["stat", i] = SB[0]
                        signal_tile(("stat", i), pe.matmul(
                            SB[0][:], const[:, K_MEAN:K_MEAN + 1].to_broadcast([P, P]), stat[:],
                            start=True, stop=True))

                    def ffn(base, job, hjob, i, nxt):
                        n0 = ring.n

                        def up(it, first):
                            for s in range(4):
                                j = it * 2 + s // 2
                                b = RB[(n0 + s) % 4]
                                if first:
                                    b = ring.next(("up", i, s), val_ready, hjob + s // 2 + 1)
                                else:
                                    pe.wait_ge(val_ready, j + (hjob - 1))
                                chunk(it * 4 + (base + s), b, xh, xl, parity=base + s,
                                      jobs=job if first and s == 0 else None)
                                if first and s == 0:
                                    norm_stat(i)

                        up(0, True)
                        with pe.Fori(1, NJ // 2) as it:
                            up(it, False)
                        for s in range(4):
                            ring.freed[(n0 + s) % 4] = (val_ready, hjob + NJ - 1 + s // 2)
                        for m in range(KT):
                            b = ring.next(("down", i, m), val_ready, nxt + m + 1)
                            for q, (k0, k1) in enumerate(DOWN_PARTS):
                                chunk(base + FFN_UP + 3 * m + q, b, hh, hl, k0, k1,
                                      jobs=hjob + k0 if m == 0 else None, start=q == 0, stop=q == 2)

                    ffn(C_FFA, J_FFA, J_HA, 0, J_MIX)

                    def turn(n, cols=S):
                        pe.wait_ge(stage_ready, n + 1)
                        b = ring.next(("turn", n), vtok_ready, n + 1)
                        for t in range(cols // P):
                            m = pe.transpose(b[:, t * P:(t + 1) * P], T[2 + n % 2][:, t * P:(t + 1) * P],
                                             ident)
                        signal_tile(("turn", n), m)

                    chunk(C_GA, ring.next("ga", row_in, 2), xh, xl, jobs=J_MIX)
                    norm_stat(1)
                    for n in range(3):
                        chunk(C_GQK + n, ring.next(("gqk", n), gqk_ready, n + 1), xh, xl)
                        if n == 0:
                            pe.wait_ge(ga_ready, 1)
                            pe.wait_ge(params_in, 16)
                            for t in range(2):
                                b = ring.next(("z", t), z_in, t + 1)
                                signal_tile(("z", t), pe.matmul(b[:], w_a2[:, t * HALF:t * HALF + P],
                                                                ga_t[0:16, :], start=True, stop=True))
                    for n in range(4):
                        if n < 3:
                            chunk(C_GV + n, ring.next(("v", n), stage_ready, n + 1), xh, xl)
                        if n >= 1:
                            turn(n - 1)

                    unit_n = [0]

                    def scores():
                        u = unit_n[0]
                        unit_n[0] += 1
                        if u < U_OFF:
                            if u >= 4:
                                pe.wait_ge(s_done, u - 3)
                            return LB[u % 4]
                        pe.wait_ge(s_done, u - 1)
                        return SB[u % 2]

                    def rot(n):
                        chunk(C_ROT + n, ring.next(("rot", n), rot_copied, n + 1), xh, xl)

                    def swap(n):
                        pe.wait_ge(rot_copied, n + 1)
                        b = ring.next(("swap", n), rot_ready, 2 * n + 1)
                        signal_tile(("swap", n), pe.matmul(b[:], const[:, K_SWAP:K_SWAP + P],
                                                           rqk[:, n, :], start=True, stop=True))

                    def vchunk(c, n):
                        chunk(c, ring.next(("v", n), stage_ready, n + 1), xh, xl)

                    def qk_chunk(n):
                        chunk(C_MQK + n, ring.next(("mqk", n), conv_ready, 5 * n + 5), xh, xl)

                    fill = [
                        lambda: (rot(0), rot(1), swap(0)),
                        lambda: (rot(2), swap(1)),
                        lambda: (vchunk(C_RV, 3), swap(2), vchunk(C_RV + 1, 4), turn(3)),
                        lambda: (vchunk(C_RV + 2, 5), turn(4), qk_chunk(0), turn(5)),
                        lambda: (qk_chunk(1), qk_chunk(2)),
                        lambda: (qk_chunk(3), vchunk(C_MV, 6)),
                        lambda: (vchunk(C_MV + 1, 7), turn(6), turn(7)),
                    ]

                    def head_rows(t3, h):
                        t, r = head_at(h)
                        return t3[r:r + GDK, t, :]

                    pe.wait_ge(gqk_ready, 3)
                    for h in range(GH):
                        b = scores()
                        for t in range(TB):
                            c = slice(t * P, (t + 1) * P)
                            m = pe.matmul(b[:, c], head_rows(gk, h)[:, c], head_rows(gq, h)[:, c],
                                          start=True, stop=True)
                        m.then_inc(s_full, 1)
                    fill[0]()
                    pe.wait_ge(xs_ready, 2)
                    for h in range(GH):
                        b = scores()
                        for t in range(TB):
                            for n, v in enumerate(HEAVY_LEVELS):
                                r = head_rows(xs[n], h)
                                for g in range(P // (2 * v)):
                                    k0 = 2 * v * g
                                    m = pe.matmul(b[k0:k0 + v, t * P + k0 + v:t * P + k0 + 2 * v],
                                                  r[:, t * P + k0:t * P + k0 + v],
                                                  r[:, t * P + k0 + v:t * P + k0 + 2 * v],
                                                  start=True, stop=True)
                        m.then_inc(s_full, 1)
                    fill[1]()
                    for n, v in enumerate(LEVELS):
                        pe.wait_ge(xs_ready, 3 + n)
                        for h in range(GH):
                            b = scores()
                            r = head_rows(xs[(2 + n) % X_SLOTS], h)
                            for t in range(TB):
                                c = slice(t * P, (t + 1) * P)
                                m = pe.matmul(b[:, c], r[:, c], r[:, c], start=True, stop=True)
                            m.then_inc(s_full, 1)
                        fill[2 + n]()

                    o_n = [0]

                    def o_bank():
                        q = o_n[0]
                        if q >= 2:
                            pe.wait_ge(o_taken, q - 1)
                        o_n[0] += 1
                        return OB[q % 2]

                    def gate(n):
                        chunk(C_GATE + n, ring.next(("gate", n), gate_copied, n + 1), xh, xl)

                    pe.wait_ge(xs_ready, 9)
                    x256, x128 = xs[7 % X_SLOTS], xs[8 % X_SLOTS]
                    pe.wait_ge(vtok_ready, 3)

                    def gla_off(h):
                        b = scores()
                        r = head_rows(x256, h)
                        for jt in range(2):
                            m = pe.matmul(b[:, jt * 256:(jt + 1) * 256], r[:, jt * P:(jt + 1) * P],
                                          r[:, 256:512], start=True, stop=True)
                        m.then_inc(s_full, 1)
                        b = scores()
                        r = head_rows(x128, h)
                        for n in range(2):
                            m = pe.matmul(b[:, n * P:(n + 1) * P], r[:, n * 256:n * 256 + P],
                                          r[:, n * 256 + P:n * 256 + 256], start=True, stop=True)
                        m.then_inc(s_full, 1)

                    def gla_pv(h, ob):
                        pe.wait_ge(s_done, U_OFF + 2 * h + 2)
                        o = ob[DV * (h % 2):DV * (h % 2) + DV, :]
                        v = gv[:, :, h * DV:(h + 1) * DV]
                        pieces = [(jt, sdiag[:, h, jt, :], jt * P) for jt in range(TB)]
                        pieces += [(jt, sm[0][:, jt * 256:(jt + 1) * 256], 256) for jt in range(2)]
                        pieces += [(2 * n, sm[1][:, n * P:(n + 1) * P], n * 256 + P) for n in range(2)]
                        for n, (jt, s, i0) in enumerate(pieces):
                            m = pe.matmul(o[:, i0:i0 + s.shape[-1]], v[:, jt, :], s, start=n == 0,
                                          stop=n == len(pieces) - 1, skip_group_check=True)
                        m.then_inc(o_full, 1)

                    gla_off(0)
                    for h in range(GH):
                        if h % 2 == 0:
                            ob = o_bank()
                        gla_pv(h, ob)
                        if h + 1 < GH:
                            gla_off(h + 1)

                    pe.wait_ge(rows_ready, 4)
                    b = ring.next("ucol", ucol_ready, 1)
                    for t in range(TB):
                        m = pe.transpose(b[:, t * MH:(t + 1) * MH], row_u[0:MH, t * P:(t + 1) * P],
                                         ident[0:MH, 0:MH])
                    signal_tile("ucol", m)
                    pe.wait_ge(mqk_ready, 4)
                    pe.wait_ge(vtok_ready, 8)
                    pe.wait_ge(em_ready, 1)

                    def mem_turn(k):
                        if k == 0:
                            pe.wait_ge(memn_ready, 2)
                        b = ring.next(("mem", k), val_ready, J_MEM + k + 1)
                        for t in range(2):
                            m = pe.transpose(b[:, t * P:(t + 1) * P], memraw[:, t, k * P:(k + 1) * P],
                                             ident)
                        signal_tile(("mem", k), m)

                    def stat_of(p, step):
                        if step == 0:
                            pe.wait_ge(o_taken, 7 + p - 3 + 1)
                            b, src = ring.next(("mean", p), xc_ready, p - 3 + 1), o_ret[:, p - 3, :]
                        else:
                            pe.wait_ge(post_sq, p + 1)
                            b, src = ring.next(("post", p), post_rms, p + 1), (gsq if p < 3 else psq)[p % 2][:]
                        signal_tile(("post" if step else "mean", p),
                                    pe.matmul(b[:], const[:, K_HEAD:K_HEAD + P], src,
                                              start=True, stop=True))

                    for n in range(ML_STEPS):
                        p, jt = divmod(n, TB)
                        w = S - jt * P
                        if jt == 0:
                            for h in (2 * p, 2 * p + 1):
                                b = ring.next(("negm", h), negm_ready, h + 1)
                                signal_tile(("negm", h), pe.matmul(
                                    b[:], ident[0:MH, h:h + 1].to_broadcast([MH, P]),
                                    row_m[0:MH, :], start=True, stop=True))
                        for e in range(2):
                            r = slice(MDK * e, MDK * (e + 1))
                            m = pe.matmul(SB[e][:, 0:w], mqk[r, 2 + p, jt * P:(jt + 1) * P],
                                          mqk[r, p, jt * P:], start=True, stop=True)
                        m.then_inc(ml_full, 1)
                        gate(n)
                        for k in MEM_TURNS.get(n, ()):
                            mem_turn(k)
                        if n in GLA_NORMS:
                            stat_of(GLA_NORMS[n], 1)
                        if jt == 0:
                            den, num = o_bank(), o_bank()
                        pe.wait_ge(ml_done, n + 1)
                        for e in range(2):
                            h = 2 * p + e
                            pe.matmul(num[DV * e:DV * (e + 1), jt * P:], mv[:, jt, h * DV:(h + 1) * DV],
                                      sm[e][:, 0:w], start=jt == 0, stop=jt == TB - 1,
                                      skip_group_check=True)
                        for e in range(2):
                            m = pe.matmul(den[DV * e:DV * (e + 1), jt * P:],
                                          const[:, K_ONE:K_ONE + 1].to_broadcast([P, DV]),
                                          sm[e][:, 0:w], start=jt == 0, stop=jt == TB - 1,
                                          skip_group_check=True)
                        m.then_inc(o_full, 1)
                        if jt == TB - 1:
                            b = ring.next(("em", p), o_taken, 4 + 2 * p)
                            for e in range(2):
                                m = pe.matmul(b[DV * e:DV * (e + 1), :],
                                              ident[0:MH, 2 * p + e:2 * p + e + 1].to_broadcast([MH, DV]),
                                              row_e[0:MH, :], start=True, stop=True)
                            signal_tile(("em", p), m)

                    def ret_scores(n):
                        if n > 0:
                            pe.wait_ge(ret_done, n)
                        p, jt = divmod(n, TB)
                        for e in range(2):
                            t, r = head_at(2 * p + e)
                            r = slice(r, r + GDK)
                            m = pe.matmul(SB[e][:, 0:S - jt * P], rqk[r, 2 + t, jt * P:(jt + 1) * P],
                                          rqk[r, t, jt * P:], start=True, stop=True)
                        m.then_inc(ret_full, 1)

                    def ret_out(n, ob):
                        pe.wait_ge(ret_done, n + 1)
                        p, jt = divmod(n, TB)
                        for e in range(2):
                            h = 2 * p + e
                            m = pe.matmul(ob[DV * e:DV * (e + 1), jt * P:],
                                          rv[:, jt, h * DV:(h + 1) * DV],
                                          sm[2 * (n % 2) + e][:, 0:S - jt * P],
                                          start=jt == 0, stop=jt == TB - 1, skip_group_check=True)
                        m.then_inc(o_full, 1)

                    pe.wait_ge(rot_ready, 7)
                    ret_scores(0)
                    for m in range(17):
                        if m < 8:
                            chunk(C_K + m, ring.next(("kx", m), kx_ready, m + 1), memhi, memlo, cols=MEM,
                                  jobs=J_MEM if m == 0 else None)
                        elif m < 16:
                            chunk(C_K + m, ring.next(("v", m), stage_ready, m + 1), memhi, memlo, cols=MEM)
                        if m + 1 < RET_STEPS:
                            ret_scores(m + 1)
                        if m < RET_STEPS:
                            if m % TB == 0:
                                ob = o_bank()
                            ret_out(m, ob)
                        if m > 8:
                            turn(m - 1, MEM)
                        if m in POST and POST[m][1] < 2:
                            stat_of(*POST[m])

                    def project(c0, job, sem_, v0, hi_, lo_):
                        for m in range(KT):
                            chunk(c0 + m, ring.next(("proj", c0 + m), sem_, v0 + m + 1), hi_, lo_,
                                  jobs=job if m == 0 else None,
                                  order=FEAT_ORDER if c0 == C_OUT else None)

                    project(C_OUT, J_FEAT, val_ready, J_XA, xh, xl)
                    pe.wait_ge(kx_ready, KT)
                    pe.wait_ge(vtok_ready, 16)
                    assert unit_n[0] == U_XA

                    def xa_scores(n):
                        h, pair = divmod(n, 2)
                        pe.wait_ge(qx_ready, 2 * h + 2)
                        b = scores()
                        for s in range(2):
                            st = 2 * pair + s
                            for dt in range(2):
                                m = pe.matmul(b[:, s * MEM:(s + 1) * MEM],
                                              qx[:, 2 * h + dt, st * P:(st + 1) * P],
                                              kx[:, 2 * h + dt, :], start=dt == 0, stop=dt == 1)
                        m.then_inc(s_full, 1)

                    def xa_turn(n):
                        pe.wait_ge(prob_ready, 2 * n + 2)
                        b = ring.next(("pt", n), pt_ready, n + 1)
                        for mt in range(2):
                            for s in range(2):
                                m = pe.transpose(b[:, (2 * mt + s) * P:(2 * mt + s + 1) * P],
                                                 prob[n % 2][:, s, mt * P:(mt + 1) * P], ident)
                        signal_tile(("pt", n), m)

                    def xa_out(h):
                        pe.wait_ge(pt_ready, 2 * h + 2)
                        for dt in range(2):
                            b = ring.next(("att", 2 * h + dt), val_ready, J_ATT + 2 * h + dt + 1)
                            for mt in range(2):
                                m = pe.matmul(b[:], vx[:, mt, (2 * h + dt) * P:(2 * h + dt + 1) * P],
                                              pt[h][:, mt, :], start=mt == 0, stop=mt == 1)
                            signal_tile(("att", 2 * h + dt), m)

                    for kind, n in XA_STEPS:
                        if kind == "query":
                            chunk(C_Q + n, ring.next(("proj", C_Q + n), qx_ready, n + 1), ah, al,
                                  jobs=J_XA if n == 0 else None)
                            if n == 0:
                                norm_stat(2)
                        elif kind == "scores":
                            xa_scores(n)
                        elif kind == "turn":
                            xa_turn(n)
                        else:
                            xa_out(n)
                    project(C_O, J_ATT, val_ready, J_FFB, ah, al)
                    ffn(C_FFB, J_FFB, J_HB, 3, J_END)

                @block.scalar
                def _(act):
                    bank, full = rings[-1].of, rings[-1].full
                    spare = act.alloc_register("act_spare")

                    def settle():
                        act.reg_mov(spare, 0)

                    act.dma_start(w_a2[:], A["gla_w_a2"][lay]).then_inc(params_in, 16)
                    for n, name in enumerate(("ml_b_i", "ml_b_f")):
                        act.dma_start(b_if[:, n:n + 1], A[name][lay].rearrange("(h o) -> h o", o=1))\
                           .then_inc(biases_in, 16)

                    head, pieces = [0], [0] * 4

                    def ahead(count=1, n=8):
                        for _ in range(count):
                            c = head[0]
                            if c < 4:
                                act.wait_ge(w_first[c], lay * 16 + 16)
                                settle()
                            else:
                                act.wait_ge(w_loaded[c % 4], 16 * (c // 4))
                            if C_MIX <= c < C_K and len(MIX[c - C_MIX]) > 1:
                                pieces[c % 4] += len(MIX[c - C_MIX]) - 1
                                act.wait_ge(w_pieces[c % 4], 16 * pieces[c % 4])
                            if c >= 2:
                                act.wait_ge(chunk_done, c - 1)
                            act.activation(whi[c % 2][:, 0:n], raw[c % 4][:, 0:n], ACT.Copy)\
                               .then_inc(w_hi, 1)
                            head[0] += 1

                    def hi(job, dst, cols=S):
                        act.wait_ge(val_ready, job + 1)
                        act.activation(dst, T[job % 2][:, 0:cols], ACT.Copy).then_inc(hi_ready, 1)

                    def rms(i):
                        act.wait_ge(tile_full, full["stat", i])
                        act.activation(stat[:], bank["stat", i][:], ACT.Sqrt, bias=eps)\
                           .then_inc(rms_ready, 1)

                    def hi_gained(dst, k, gain):
                        act.activation(dst[:, k, :], x[:, k, :], ACT.Copy,
                                       scale=pcol[:, gain + k:gain + k + 1]).then_inc(hi_ready, 1)

                    added = [0]

                    def new_x(m, job, gain=None, dst=None):
                        act.wait_ge(val_ready, job + m + 1)
                        if gain is not None:
                            hi_gained(dst, m, gain)
                        if m >= 2:
                            act.wait_ge(sq_added, added[0] + m - 1)
                        act.activation(T[2 + m % 2][:], x[:, m, :], ACT.Square).then_inc(sq_ready, 1)
                        if m == KT - 1:
                            added[0] += KT

                    def ffn(base, hjob, i, silus, *nxt):
                        def silu(j, s):
                            act.wait_ge(a_scaled, j + (silus + 1))
                            if not isinstance(j, int):
                                settle()
                            act.activation(T[2 + s][:], T[2 + s][:], ACT.Silu).then_inc(silu_ready, 1)

                        def cut_weights(it, s):
                            q = base + s
                            act.wait_ge(w_loaded[q % 4], it * 16 + 16 * (q // 4))
                            act.wait_ge(chunk_done, it * 4 + (q - 1))
                            settle()
                            act.activation(whi[q % 2][:], raw[q % 4][:], ACT.Copy).then_inc(w_hi, 1)

                        def hidden(it, s):
                            act.wait_ge(val_ready, it * 2 + (hjob + s + 1))
                            settle()
                            act.activation(hh[:, it * 2 + s, :], T[(hjob + s) % 2][:], ACT.Copy)\
                               .then_inc(hi_ready, 1)

                        rms(i)
                        ahead()
                        silu(0, 0)
                        ahead()
                        hi(hjob, hh[:, 0, :])
                        with act.Fori(1, NJ // 2) as it:
                            cut_weights(it, 0)
                            silu(it * 2 - 1, 1)
                            cut_weights(it, 1)
                            hidden(it, -1)
                            cut_weights(it, 2)
                            silu(it * 2, 0)
                            cut_weights(it, 3)
                            hidden(it, 0)
                        d = base + FFN_UP
                        head[0] = d
                        ahead()
                        silu(NJ - 1, 1)
                        ahead(n=7)
                        hi(hjob + NJ - 1, hh[:, NJ - 1, :])
                        for m in range(KT):
                            for q in range(3):
                                if head[0] < CHUNKS:
                                    e = head[0] - d
                                    ahead(n=7 if e < FFN_DOWN and e % 3 else 8)
                            new_x(m, *nxt)

                    ahead()
                    act.wait_ge(params_up, 1)
                    for k in range(KT):
                        hi_gained(xh, k, R_FFA)
                        if k == 2:
                            ahead()
                    ffn(C_FFA, J_HA, 0, 0, J_MIX, R_MIX, xh)

                    rms(1)
                    ahead(2)
                    links = [0]

                    def link(ins):
                        links[0] += 1
                        ins.then_inc(act_link, 1)
                        act.wait_ge(act_link, links[0])

                    def softplus(buf, src, between=None):
                        link(act.activation(buf, src, ACT.Abs))
                        link(act.activation(buf, buf, ACT.Exp, scale=-1.0))
                        if between is not None:
                            between()
                        act.activation(buf, buf, ACT.Ln, bias=1.0).then_inc(ln_ready, 1)

                    act.wait_ge(row_in, 2)
                    softplus(row_m[0:MH, :], row_b[0:MH, :])
                    act.wait_ge(z_in, 2)
                    softplus(p128[:], p64[:], ahead)
                    act.wait_ge(rows_ready, 3)
                    act.activation(row_e[0:MH, :], row_e[0:MH, :], ACT.Exp, scale=-1.0)\
                       .then_inc(em_ready, 1)

                    def exps(n):
                        v, slot = X_ORDER[n], xs[n % X_SLOTS]
                        act.wait_ge(e_ready, n + 1)
                        if v <= 32:
                            act.activation(slot[:], slot[:], ACT.Exp, scale=1 / 16.0)\
                               .then_inc(exp_ready, 1)
                        else:
                            src = {64: p64, 128: p128, 256: p256}[v]
                            s = slot[:].rearrange("p t (n h v) -> p (t n) h v", h=2, v=v)
                            q = src[:].rearrange("p t (n h v) -> p (t n) h v", h=2, v=v)
                            act.activation(s[:, :, 0, :], s[:, :, 0, :], ACT.Exp, scale=1 / 16.0)
                            act.activation(s[:, :, 1, :], q[:, :, 1, :], ACT.Exp, scale=1 / 16.0)\
                               .then_inc(exp_ready, 1)

                    def conv_silu(n):
                        act.wait_ge(conv_ready, 5 * n + 5)
                        act.activation(mqk[:, n, :], mqk[:, n, :], ACT.Silu).then_inc(mqk_ready, 1)

                    ahead()
                    for n in range(3):
                        exps(n)
                        ahead()
                    ahead(2)
                    exps(3)
                    exps(4)
                    ahead()
                    exps(5)
                    ahead(2)
                    exps(6)
                    ahead(2)
                    exps(7)
                    conv_silu(0)
                    ahead(2)
                    exps(8)
                    conv_silu(1)
                    conv_silu(2)
                    ahead(2)
                    conv_silu(3)
                    ahead()
                    assert head[0] == C_GATE + 2

                    act.wait_ge(o_full, GH)
                    act.dma_start(memraw[:], mem_tok).then_inc(mem_in, 16)

                    def gate_act(n):
                        act.wait_ge(gate_copied, n + 1)
                        act.activation(gates[:, n, :], gates[:, n, :],
                                       ACT.Silu if n < 6 else ACT.Sigmoid).then_inc(gate_ready, 1)

                    def rms_of_heads(p):
                        act.wait_ge(tile_full, full["post", p])
                        if p > 3:
                            act.wait_ge(normed, p)
                        act.activation((gsq[p % 2] if p < 3 else rtmp)[:], bank["post", p][:], ACT.Sqrt, bias=eps)\
                           .then_inc(post_rms, 1)

                    for n in range(ML_STEPS):
                        p, jt = divmod(n, TB)
                        for e in range(2):
                            act.wait_ge(dlog_ready, 2 * n + e + 1)
                            b = T[2 + e][:, 0:S - jt * P]
                            act.activation(b, b, ACT.Exp).then_inc(dexp_ready, 1)
                        if n == ML_STEPS - 1:
                            for q in range(7):
                                gate_act(q)
                        if n in GLA_NORMS:
                            act.wait_ge(o_taken, GLA_NORMS[n] + 1)
                            if GLA_NORMS[n] == 1:
                                act.wait_ge(o_taken, 5)
                            elif GLA_NORMS[n] == 2:
                                act.wait_ge(normed, 1)
                            act.activation(gsq[GLA_NORMS[n] % 2][:], o_gla[:, GLA_NORMS[n], :], ACT.Square)\
                               .then_inc(post_sq, 1)
                        ahead()
                        if n == 0:
                            act.wait_ge(mem_in, 16)
                            for t in range(2):
                                link(act.activation(memsq[:], memraw[:, t, :], ACT.Square,
                                                    accum_out=memst[:, t:t + 1]))
                            act.activation(memst[:, 2:4], memst[:, 0:2], ACT.Sqrt, bias=eps,
                                           scale=1.0 / D).then_inc(mem_rms, 1)
                        for k in MEM_TURNS.get(n, ()):
                            hi(J_MEM + k, memhi[:, k, :], MEM)
                        if n in GLA_NORMS:
                            rms_of_heads(GLA_NORMS[n])
                        if jt == TB - 1:
                            act.wait_ge(o_full, GH + n + 1)
                            if p == 1:
                                act.wait_ge(normed, 2)
                            act.activation(rtmp[:], OB[1][:], ACT.Abs).then_inc(den_abs, 1)
                    gate_act(7)

                    def feature_hi(m):
                        p, step = POST.get(m, (0, 0))
                        if step:
                            hi(J_FEAT + FEAT_ORDER.index(p), xh[:, p, :])

                    for m in range(16):
                        p, step = POST.get(m, (0, 0))
                        if step == 1:
                            act.wait_ge(xc_ready, p - 2)
                            act.activation(psq[p % 2][:], o_ret[:, p - 3, :], ACT.Square)\
                               .then_inc(post_sq, 1)
                        ahead()
                        if step == 1:
                            if p == 3:
                                act.wait_ge(o_taken, 7)
                            rms_of_heads(p)
                        feature_hi(m - 1)

                    for m in range(KT):
                        ahead()
                        new_x(m, J_XA, R_XA, ah)
                    for kind, n in XA_STEPS:
                        if kind == "query":
                            if n == 0:
                                rms(2)
                            ahead()
                        elif kind == "scores":
                            act.wait_ge(max_ready, n + 1)
                            if n >= 2:
                                act.wait_ge(pt_ready, n - 1)
                            for s in range(2):
                                act.activation(prob[n % 2][:, s, :],
                                               SB[(U_XA + n) % 2][:, s * MEM:(s + 1) * MEM], ACT.Exp,
                                               bias=smx[:, n % 2, s:s + 1], scale=XDH ** -0.5,
                                               accum_out=smx[:, n % 2, 2 + s:3 + s])\
                                   .then_inc(prob_exp, 1)
                        elif kind == "out":
                            for k in (2 * n, 2 * n + 1):
                                hi(J_ATT + k, ah[:, k, :])
                    for m in range(KT):
                        ahead()
                        new_x(m, J_FFB, R_FFB, xh)
                    assert head[0] == C_FFB + 2
                    ffn(C_FFB, J_HB, 3, NJ, J_END)

                @block.vector
                def _(dve):
                    bank, full = rings[-1].of, rings[-1].full
                    links = [0]

                    def link(ins):
                        links[0] += 1
                        ins.then_inc(dve_link, 1)
                        dve.wait_ge(dve_link, links[0])

                    def lo(job, dst, hi_part, cols=S):
                        dve.wait_ge(hi_ready, cut(job))
                        dve.tensor_tensor(dst, T[job % 2][:, 0:cols], hi_part.bitcast(F32),
                                          ALU.subtract).then_inc(lo_ready, 1)

                    def free(job):
                        dve.wait_ge(lo_ready, cut(job - 2))

                    def inverse_rms(i):
                        dve.wait_ge(rms_ready, i + 1)
                        link(dve.reciprocal(stat[:], stat[:]))

                    def lo_gained(k, job, gain, hi_, lo_):
                        dve.wait_ge(hi_ready, cut(job + k))
                        dve.scalar_tensor_tensor(lo_[:, k, :], x[:, k, :],
                                                 pcol[:, gain + k:gain + k + 1],
                                                 hi_[:, k, :].bitcast(F32), ALU.mult, ALU.subtract)\
                           .then_inc(lo_ready, 1)

                    added = [0]

                    def add_square(m):
                        dve.wait_ge(sq_ready, added[0] + 1)
                        if m == 0:
                            ins = dve.tensor_copy(stat[:], T[2][:])
                        else:
                            dve.wait_ge(sq_added, added[0])
                            ins = dve.tensor_tensor(stat[:], stat[:], T[2 + m % 2][:], ALU.add)
                        ins.then_inc(sq_added, 1)
                        added[0] += 1

                    def update_x(chunk_of, name_of, factor, *parts):
                        for m in range(KT):
                            dve.wait_ge(chunk_done, chunk_of(m) + 1)
                            dve.scalar_tensor_tensor(x[:, m, :], bank[name_of(m)][:], factor,
                                                     x[:, m, :], ALU.mult, ALU.add)\
                               .then_inc(val_ready, 1)
                            if m >= 1:
                                if parts:
                                    lo_gained(m - 1, *parts)
                                add_square(m - 1)
                        if parts:
                            lo_gained(KT - 1, *parts)
                        add_square(KT - 1)

                    def ffn(base, hjob, i, silus, *parts):
                        inverse_rms(i)
                        with dve.Fori(0, NJ // 2) as it:
                            for s in range(2):
                                dve.wait_ge(lo_ready, it * 2 + (cut(hjob) + s - 2))
                                dve.wait_ge(chunk_done, it * 4 + (base + 2 * s + 1))
                                dve.tensor_tensor(T[2 + s][:], bank["up", i, 2 * s][:], stat[:],
                                                  ALU.mult).then_inc(a_scaled, 1)
                                dve.wait_ge(chunk_done, it * 4 + (base + 2 * s + 2))
                                dve.tensor_tensor(T[s][:], bank["up", i, 2 * s + 1][:], stat[:],
                                                  ALU.mult).then_inc(g_scaled, 1)
                                dve.wait_ge(g_scaled, it * 2 + (silus + s + 1))
                                dve.wait_ge(silu_ready, it * 2 + (silus + s + 1))
                                dve.tensor_tensor(T[s][:], T[s][:], T[2 + s][:],
                                                  ALU.mult).then_inc(val_ready, 1)
                                dve.wait_ge(hi_ready, it * 2 + (cut(hjob) + s))
                                dve.tensor_tensor(hl[:, it * 2 + s, :], T[s][:],
                                                  hh[:, it * 2 + s, :].bitcast(F32),
                                                  ALU.subtract).then_inc(lo_ready, 1)
                        update_x(lambda m: base + FFN_UP + 3 * m + 2, lambda m: ("down", i, m), 0.5,
                                 *parts)

                    dve.tensor_copy(pcol[:], pcols[:, bass.ds(lay * N_ROWS, N_ROWS)])\
                       .then_inc(params_up, 1)
                    dve.wait_ge(params_up, 1)
                    for k in range(KT):
                        lo_gained(k, J_FFA, R_FFA, xh, xl)
                    ffn(C_FFA, J_HA, 0, 0, J_MIX, R_MIX, xh, xl)

                    inverse_rms(1)
                    dve.wait_ge(chunk_done, C_GA + 1)
                    dve.tensor_tensor(ga_t[0:16, :], bank["ga"][0:16, :], stat[0:16, :], ALU.mult)\
                       .then_inc(ga_ready, 1)
                    dve.wait_ge(biases_in, 32)
                    for n, row in enumerate((row_u, row_b)):
                        r = slice(32 * (n + 1), 32 * (n + 1) + MH)
                        link(dve.tensor_tensor(row[0:MH, :], bank["ga"][r, :], stat[r, :], ALU.mult))
                        dve.tensor_scalar(row[0:MH, :], row[0:MH, :], b_if[:, n:n + 1],
                                          None, ALU.add).then_inc(row_in, 1)
                    for t in range(2):
                        dve.wait_ge(tile_full, full["z", t])
                        dve.tensor_scalar(p64[:, t, :], bank["z", t][:],
                                          pcol[:, R_BA + t:R_BA + t + 1], None, ALU.add)\
                           .then_inc(z_in, 1)
                    def gla_qk(n):
                        dve.wait_ge(chunk_done, C_GQK + n + 1)
                        src = bank["gqk", n]
                        if n != 1:
                            ins = dve.scalar_tensor_tensor(gq[:, n // 2, :], src[:], GDK ** -0.5,
                                                           stat[:], ALU.mult, ALU.mult)
                        if n >= 1:
                            ins = dve.tensor_tensor(gk[:, n - 1, :], src[:], stat[:], ALU.mult)
                        if n == 2:
                            link(ins)
                            ins = dve.tensor_tensor(gk[HALF:P, 1, :], src[0:HALF, :], stat[0:HALF, :],
                                                    ALU.mult)
                        ins.then_inc(gqk_ready, 1)

                    gla_qk(0)
                    u, b, mm, em = (r[0:MH, :] for r in (row_u, row_b, row_m, row_e))
                    dve.wait_ge(ln_ready, 1)
                    link(dve.scalar_tensor_tensor(b, b, 0.0, mm, ALU.min, ALU.subtract))
                    link(dve.tensor_tensor_scan(b, b, b, 0.0, ALU.add, ALU.bypass))
                    dve.tensor_tensor(u, u, b, ALU.subtract).then_inc(rows_ready, 1)
                    dve.wait_ge(rows_ready, 1)
                    dve.tensor_tensor_scan(mm, u, u, 0.0, ALU.max, ALU.bypass).then_inc(rows_ready, 1)
                    dve.wait_ge(rows_ready, 2)
                    dve.tensor_tensor(em, b, mm, ALU.add).then_inc(rows_ready, 1)
                    dve.tensor_scalar(mm, mm, -1.0, None, ALU.mult).then_inc(rows_ready, 1)
                    gla_qk(1)
                    dve.wait_ge(ln_ready, 2)
                    z = p64[:].rearrange("p t s -> p (t s)")
                    link(dve.scalar_tensor_tensor(z, z, 0.0, p128[:].rearrange("p t s -> p (t s)"),
                                                  ALU.min, ALU.subtract))
                    for n in range(16):
                        c = z[:, n * 64:(n + 1) * 64]
                        ins = dve.tensor_tensor_scan(c, c, c, 0.0, ALU.add, ALU.bypass)
                    link(ins)
                    for src, dst, v in ((p64, p128, 64), (p128, p256, 128)):
                        q = src[:].rearrange("p t (n h v) -> p (t n) h v", h=2, v=v)
                        d = dst[:].rearrange("p t (n h v) -> p (t n) h v", h=2, v=v)
                        dve.tensor_copy(d[:, :, 0, :], q[:, :, 0, :])
                        link(dve.tensor_tensor(d[:, :, 1, :], q[:, :, 1, :],
                                               q[:, :, 0, v - 1:v].to_broadcast([P, S // v, v]),
                                               ALU.add))

                    def halves(t3, v):
                        return t3[:].rearrange("p t (n h v) -> p (t n) h v", h=2, v=v)

                    def exponents(n):
                        v = X_ORDER[n]
                        q = halves({128: p128, 256: p256}.get(v, p64), v)
                        d = halves(xs[n % X_SLOTS], v)
                        mid = q[:, :, 0, v - 1:v].to_broadcast([P, S // v, v])
                        ins = dve.tensor_tensor(d[:, :, 0, :], mid, q[:, :, 0, :], ALU.subtract)
                        if v <= 32:
                            ins = dve.tensor_tensor(d[:, :, 1, :], q[:, :, 1, :], mid, ALU.subtract)
                        ins.then_inc(e_ready, 1)

                    def factors(n):
                        v = X_ORDER[n]
                        d = halves(xs[n % X_SLOTS], v)
                        dve.wait_ge(exp_ready, n + 1)
                        dve.tensor_tensor(d[:, :, 0, :], d[:, :, 0, :], halves(gk, v)[:, :, 0, :],
                                          ALU.mult)
                        dve.tensor_tensor(d[:, :, 1, :], d[:, :, 1, :], halves(gq, v)[:, :, 1, :],
                                          ALU.mult).then_inc(xs_ready, 1)

                    for n in range(3):
                        exponents(n)
                    gla_qk(2)
                    dve.wait_ge(gqk_ready, 3)
                    for n in range(3):
                        factors(n)

                    def stage(n, c):
                        dve.wait_ge(chunk_done, c + 1)
                        dve.tensor_tensor(T[2 + n % 2][:], bank["v", n][:], stat[:],
                                          ALU.mult).then_inc(stage_ready, 1)

                    def turned(n, dst, cols=S):
                        dve.wait_ge(tile_full, full["turn", n])
                        src = bank["turn", n][:, 0:cols].rearrange("p (t c) -> p t c", c=P)
                        dve.tensor_copy(dst, src).then_inc(vtok_ready, 1)

                    for n in range(4):
                        if n < 3:
                            stage(n, C_GV + n)
                        if n >= 1:
                            turned(n - 1, gv[:, :, (n - 1) * P:n * P])

                    def rot(n):
                        dve.wait_ge(chunk_done, C_ROT + n + 1)
                        dve.tensor_tensor(rqk[:, n, :], bank["rot", n][:], stat[:],
                                          ALU.mult).then_inc(rot_copied, 1)

                    def swap(n):
                        dve.wait_ge(tile_full, full["swap", n])
                        r = rqk[:, n, :]
                        if n >= 1:
                            dve.wait_ge(rot_ready, 2 * n)
                        dve.tensor_tensor(rtmp[:], sincos[:, 1, :], bank["swap", n][:],
                                          ALU.mult).then_inc(rot_ready, 1)
                        link(dve.tensor_tensor(r, r, sincos[:, 0, :], ALU.mult))
                        dve.tensor_tensor(r, r, rtmp[:], ALU.add).then_inc(rot_ready, 1)

                    def keys_moved():
                        dve.wait_ge(rot_ready, 6)
                        dve.tensor_copy(rqk[HALF:P, 3, :], rqk[0:HALF, 1, :]).then_inc(rot_ready, 1)

                    def conv(n):
                        dve.wait_ge(chunk_done, C_MQK + n + 1)
                        src, dst = bank["mqk", n], mqk[:, n, :]

                        def tap(j):
                            return pcol[:, R_CONV + 4 * j + n:R_CONV + 4 * j + n + 1]

                        dve.tensor_tensor(src[:], src[:], stat[:], ALU.mult).then_inc(conv_ready, 1)
                        dve.wait_ge(conv_ready, 5 * n + 1)
                        dve.tensor_scalar(dst, src[:], tap(3), None, ALU.mult).then_inc(conv_ready, 1)
                        for e in range(1, 4):
                            dve.wait_ge(conv_ready, 5 * n + e + 1)
                            dve.scalar_tensor_tensor(dst[:, e:], src[:, 0:S - e], tap(3 - e),
                                                     dst[:, e:], ALU.mult, ALU.add)\
                               .then_inc(conv_ready, 1)

                    def rv_of(n):
                        turned(n, rv[:, :, (n - 3) * P:(n - 2) * P])

                    def mv_of(n):
                        turned(n, mv[:, :, (n - 6) * P:(n - 5) * P])

                    fill = [
                        [lambda: rot(0), lambda: rot(1), lambda: swap(0)],
                        [lambda: rot(2), lambda: swap(1)],
                        [lambda: stage(3, C_RV), lambda: (swap(2), keys_moved(), stage(4, C_RV + 1),
                                                          rv_of(3))],
                        [lambda: stage(5, C_RV + 2), lambda: (rv_of(4), conv(0), rv_of(5))],
                        [lambda: conv(1), lambda: conv(2)],
                        [lambda: conv(3), lambda: stage(6, C_MV)],
                        [lambda: stage(7, C_MV + 1), lambda: (mv_of(6), mv_of(7))],
                    ]
                    for g in range(7):
                        for h in range(GH):
                            u_ = g * GH + h
                            dve.wait_ge(s_full, u_ + 1)
                            src = LB[u_ % 4][:].rearrange("p (t c) -> p t c", c=P)
                            if g == 0:
                                sel = ident.unsqueeze(1).to_broadcast([P, TB, P])
                                ins = dve.tensor_tensor(sdiag[:, h], src, sel, ALU.mult)
                            else:
                                dve.wait_ge(s_done, u_ - GH + 1)
                                sel = masks[:, g - 1, :].unsqueeze(1).to_broadcast([P, TB, P])
                                ins = dve.copy_predicated(sdiag[:, h], sel, src)
                            ins.then_inc(s_done, 1)
                        nxt = {1: (3, 4), 2: (5,), 3: (6,), 4: (7,), 5: (8,)}.get(g, ())
                        for n in nxt:
                            exponents(n)
                        for part in fill[g][:-1]:
                            part()
                        for n in nxt:
                            factors(n)
                        fill[g][-1]()
                    for h in range(GH):
                        for n in range(2):
                            u_ = U_OFF + 2 * h + n
                            w = S if n == 0 else 256
                            dve.wait_ge(s_full, u_ + 1)
                            if h >= 1:
                                dve.wait_ge(o_full, h)
                            dve.tensor_copy(sm[n][:, 0:w], SB[n][:, 0:w]).then_inc(s_done, 1)
                        if h % 2 == 0 and h >= 2:
                            p = h // 2 - 1
                            dve.tensor_copy(o_gla[:, p, :], OB[p % 2][:]).then_inc(o_taken, 1)
                    dve.wait_ge(o_full, GH)
                    dve.tensor_copy(o_gla[:, 2, :], OB[0][:]).then_inc(o_taken, 1)

                    dve.wait_ge(tile_full, full["ucol"])
                    dve.tensor_copy(ucol[:].rearrange("p t h -> p (t h)"), bank["ucol"][:, 0:TB * MH])\
                       .then_inc(ucol_ready, 1)
                    dve.wait_ge(ucol_ready, 1)

                    def weight_log(n):
                        p, jt = divmod(n, TB)
                        for e in range(2):
                            if jt == 0:
                                dve.wait_ge(tile_full, full["negm", 2 * p + e])
                                dve.tensor_copy(negm[e][:], bank["negm", 2 * p + e][:])\
                                   .then_inc(negm_ready, 1)
                                dve.wait_ge(negm_ready, 2 * p + e + 1)
                            dve.tensor_scalar(T[2 + e][:, 0:S - jt * P], negm[e][:, jt * P:],
                                              ucol[:, jt, 2 * p + e:2 * p + e + 1], 0.0,
                                              ALU.add, ALU.min).then_inc(dlog_ready, 1)

                    def gate(n):
                        dve.wait_ge(chunk_done, C_GATE + n + 1)
                        dve.tensor_tensor(gates[:, n, :], bank["gate", n][:], stat[:], ALU.mult)\
                           .then_inc(gate_copied, 1)

                    def mem_part(k):
                        dve.wait_ge(tile_full, full["mem", k])
                        free(J_MEM + k)
                        dve.tensor_scalar(T[(J_MEM + k) % 2][:, 0:MEM], bank["mem", k][:, 0:MEM],
                                          pcol[:, R_MEM + k:R_MEM + k + 1], None, ALU.mult)\
                           .then_inc(val_ready, 1)
                        lo(J_MEM + k, memlo[:, k, :], memhi[:, k, :], MEM)

                    def ret_weigh(n):
                        p, jt = divmod(n, TB)
                        w = S - jt * P
                        dve.wait_ge(ret_full, n + 1)
                        dve.wait_ge(o_full, GH + ML_STEPS + max(n - 1, 0))
                        for e in range(2):
                            ins = dve.tensor_tensor(sm[2 * (n % 2) + e][:, 0:w], SB[e][:, 0:w],
                                                    decay[:, 2 * p + e, 0:w], ALU.mult)
                        ins.then_inc(ret_done, 1)

                    outputs = ([o_gla[:, p, :] for p in range(3)] + [o_ret[:, p, :] for p in range(3)]
                               + [o_ml[:, p, :] for p in range(2)])

                    def norm_heads(p):
                        gain = R_GG + p if p < 3 else R_RG + p - 3
                        dve.wait_ge(post_rms, p + 1)
                        r = (gsq[p % 2] if p < 3 else rtmp)[:]
                        link(dve.reciprocal(r, r))
                        dve.scalar_tensor_tensor(outputs[p], outputs[p], pcol[:, gain:gain + 1], r, ALU.mult, ALU.mult).then_inc(normed, 1)
                        dve.wait_ge(normed, p + 1)

                    weight_log(0)
                    for n in range(ML_STEPS):
                        p, jt = divmod(n, TB)
                        w = S - jt * P
                        dve.wait_ge(ml_full, n + 1)
                        if n > 0:
                            dve.wait_ge(o_full, GH + n)
                        for e in range(2):
                            dve.wait_ge(dexp_ready, 2 * n + e + 1)
                            link(dve.scalar_tensor_tensor(sm[e][:, 0:w], SB[e][:, 0:w], MDK ** -0.5,
                                                          T[2 + e][:, 0:w], ALU.mult, ALU.mult))
                            ins = dve.tensor_tensor(sm[e][:, 0:P], sm[e][:, 0:P],
                                                    const[:, K_CAUSAL:K_CAUSAL + P], ALU.mult)
                        ins.then_inc(ml_done, 1)
                        if n + 1 < ML_STEPS and jt < TB - 1:
                            weight_log(n + 1)
                        gate(n)
                        if n - 1 in GLA_NORMS:
                            norm_heads(GLA_NORMS[n - 1])
                        if n == 1:
                            dve.wait_ge(mem_rms, 1)
                            link(dve.reciprocal(memst[:, 2:4], memst[:, 2:4]))
                            for t in range(2):
                                dve.tensor_scalar(memraw[:, t, :], memraw[:, t, :],
                                                  memst[:, 2 + t:3 + t], None, ALU.mult)\
                                   .then_inc(memn_ready, 1)
                        for k in MEM_TURNS.get(n, ()):
                            mem_part(k)
                        if jt == TB - 1:
                            if n + 1 < ML_STEPS:
                                weight_log(n + 1)
                            else:
                                ret_weigh(0)
                            dve.wait_ge(den_abs, p + 1)
                            dve.wait_ge(tile_full, full["em", p])
                            dve.tensor_tensor(rtmp[:], rtmp[:], bank["em", p][:], ALU.max)\
                               .then_inc(o_taken, 1)
                            dve.wait_ge(o_taken, 4 + 2 * p)
                            link(dve.reciprocal(rtmp[:], rtmp[:]))
                            dve.tensor_tensor(o_ml[:, p, :], rtmp[:], OB[0][:], ALU.mult)\
                               .then_inc(o_taken, 1)

                    def post(p, step):
                        if step == 0:
                            dve.wait_ge(tile_full, full["mean", p])
                            dve.tensor_tensor(outputs[p], outputs[p], bank["mean", p][:],
                                              ALU.subtract).then_inc(xc_ready, 1)
                        else:
                            if step == 1:
                                norm_heads(p)
                            gated(p, outputs[p])

                    def gated(p, o):
                        job = J_FEAT + FEAT_ORDER.index(p)
                        dve.wait_ge(gate_ready, p + 1)
                        free(job)
                        dve.tensor_tensor(T[job % 2][:], o, gates[:, p, :], ALU.mult)\
                           .then_inc(val_ready, 1)
                        lo(job, xl[:, p, :], xh[:, p, :])

                    for m in range(17):
                        if 0 < m < RET_STEPS:
                            ret_weigh(m)
                        if m % TB == 0 and 0 < m <= RET_STEPS:
                            p = m // TB - 1
                            dve.wait_ge(o_full, GH + ML_STEPS + m)
                            dve.tensor_copy(o_ret[:, p, :], OB[(7 + p) % 2][:]).then_inc(o_taken, 1)
                        if m < 8:
                            dve.wait_ge(chunk_done, C_K + m + 1)
                            dve.tensor_copy(kx[:, m, :], bank["kx", m][:, 0:MEM]).then_inc(kx_ready, 1)
                        elif m < 16:
                            dve.wait_ge(chunk_done, C_K + m + 1)
                            dve.tensor_copy(T[2 + m % 2][:, 0:MEM], bank["v", m][:, 0:MEM])\
                               .then_inc(stage_ready, 1)
                        if m > 8:
                            turned(m - 1, vx[:, :, (m - 9) * P:(m - 8) * P], MEM)
                        if m - 1 in POST:
                            post(*POST[m - 1])

                    update_x(lambda m: C_OUT + m, lambda m: ("proj", C_OUT + m), 1.0,
                             J_XA, R_XA, ah, al)

                    inverse_rms(2)
                    for kind, n in XA_STEPS:
                        if kind == "query":
                            dve.wait_ge(chunk_done, C_Q + n + 1)
                            dve.tensor_tensor(qx[:, n, :], bank["proj", C_Q + n][:], stat[:], ALU.mult)\
                               .then_inc(qx_ready, 1)
                        elif kind == "scores":
                            st = smx[:, n % 2, :]
                            dve.wait_ge(s_full, U_XA + n + 1)
                            link(dve.tensor_reduce(
                                st[:, 0:2], SB[(U_XA + n) % 2][:].rearrange("p (s m) -> p s m", s=2),
                                AX.X, ALU.max))
                            dve.tensor_scalar(st[:, 0:2], st[:, 0:2], -XDH ** -0.5, None, ALU.mult)\
                               .then_inc(max_ready, 1)
                            dve.wait_ge(prob_exp, 2 * n + 2)
                            dve.reciprocal(st[:, 2:4], st[:, 2:4]).then_inc(s_done, 1)
                            dve.wait_ge(s_done, U_XA + n + 1)
                            for s in range(2):
                                dve.tensor_scalar(prob[n % 2][:, s, :], prob[n % 2][:, s, :],
                                                  st[:, 2 + s:3 + s], None, ALU.mult)\
                                   .then_inc(prob_ready, 1)
                        elif kind == "turn":
                            h, pair = divmod(n, 2)
                            dve.wait_ge(tile_full, full["pt", n])
                            dve.tensor_copy(pt[h][:, :, pair * 256:(pair + 1) * 256],
                                            bank["pt", n][:].rearrange("p (m c) -> p m c", m=2))\
                               .then_inc(pt_ready, 1)
                        else:
                            for k in (2 * n, 2 * n + 1):
                                dve.wait_ge(tile_full, full["att", k])
                                free(J_ATT + k)
                                dve.tensor_copy(T[(J_ATT + k) % 2][:], bank["att", k][:])\
                                   .then_inc(val_ready, 1)
                                lo(J_ATT + k, al[:, k, :], ah[:, k, :])
                    update_x(lambda m: C_O + m, lambda m: ("proj", C_O + m), 1.0,
                             J_FFB, R_FFB, xh, xl)
                    ffn(C_FFB, J_HB, 3, NJ)

            for s in loop_sems:
                nc.gpsimd.sem_clear(s)
            nc.all_engine_barrier()

        with nc.Block() as block:
            @block.sync
            def _(sp):
                for t in range(TB):
                    sp.wait_ge(y_ready, 2 * KT)
                    sp.dma_start(out_tok[:, t, :], yout[:, t, :]).then_inc(y_out, 16)
                sp.wait_ge(y_out, 16 * TB)
                for w in w_first:
                    sp.wait_ge(w, 16 * (DEPTH + 1))

            @block.scalar
            def _(act):
                act.wait_ge(y_pe, 1)
                act.activation(stat[:], psum[0][:], ACT.Sqrt, bias=eps).then_inc(y_act, 1)

            @block.tensor
            def _(pe):
                pe.matmul(psum[0][:], const[:, K_MEAN:K_MEAN + 1].to_broadcast([P, P]), stat[:], start=True, stop=True)\
                  .then_inc(y_pe, 1)
                for k in range(KT):
                    pe.wait_ge(y_ready, k + 1 if k < 2 else 2 * k)
                    for t in range(TB):
                        m = pe.transpose(psum[2 + k % 6][:, t * P:(t + 1) * P],
                                         yk[k % 2][:, t * P:(t + 1) * P], ident)
                    m.then_inc(y_pe, 1)

            @block.vector
            def _(dve):
                dve.wait_ge(y_act, 1)
                dve.reciprocal(stat[:], stat[:]).then_inc(y_act, 1)
                dve.wait_ge(y_act, 2)

                def value(k):
                    dve.scalar_tensor_tensor(yk[k % 2][:], x[:, k, :],
                                             pcols[:, DEPTH * N_ROWS + k:DEPTH * N_ROWS + k + 1],
                                             stat[:], ALU.mult, ALU.mult).then_inc(y_ready, 1)

                value(0)
                value(1)
                for k in range(KT):
                    dve.wait_ge(y_pe, 2 + k)
                    dve.tensor_copy(yout[:, :, k * P:(k + 1) * P],
                                    psum[2 + k % 6][:].rearrange("p (t c) -> p t c", c=P))\
                       .then_inc(y_ready, 1)
                    if k + 2 < KT:
                        value(k + 2)


_INS = ["x", "mem", "positions", "g_ffa", "w_ffa_gu", "w_ffa_down", "g_mix", "w_in", "gla_w_a2",
        "gla_b_a", "gla_g_norm", "ret_g_norm", "ml_conv", "ml_b_i", "ml_b_f", "w_out", "g_xa",
        "g_mem", "w_xa_q", "w_xa_kv", "w_xa_o", "g_ffb", "w_ffb_gu", "w_ffb_down", "g_final"]


def kernel(**inputs):
    import numpy as _np
    import concourse.bacc as _bacc
    from concourse import mybir as _mybir
    from concourse.bass_utils import run_bass_kernel_spmd as _run

    nc = _bacc.Bacc("TRN2", target_bir_lowering=False, num_devices=1)
    c, decay, masks = constants()
    given = {n: _np.ascontiguousarray(inputs[n]) for n in _INS}
    given |= {"c_const": c, "c_decay": decay, "c_masks": masks}
    arrays, args = {}, {}
    for name, a in given.items():
        arrays[f"in_{name}_dram"] = a
        args[name] = nc.dram_tensor(f"in_{name}_dram", a.shape, _mybir.dt.from_np(a.dtype),
                                    kind="ExternalInput").ap()
    out = nc.dram_tensor("out_0_dram", (1, S, D), _mybir.dt.float32, kind="ExternalOutput").ap()
    build(nc, args, out)
    r = _run(nc, [arrays], core_ids=[0])
    return r.results[0]["out_0_dram"]
```

```python
import numpy as np
import concourse.bass as bass
from concourse import mybir
from contextlib import ExitStack

F32 = mybir.dt.float32
F32R = mybir.dt.float32r
U8 = mybir.dt.uint8
I32 = mybir.dt.int32
ALU = mybir.AluOpType
ACT = mybir.ActivationFunctionType
AX = mybir.AxisListType

P = 128
D, S, DEPTH, MEM = 1024, 512, 2, 256
KT = D // P
TB = S // P
DFF = 2816
NJ = DFF // P
EPS = 1e-6
GH, GDK, DV = 6, 32, 64
MH, MDK = 4, 64
XH, XDH = 4, 256
SIZES = [192, 192, 384, 16, 384, 192, 192, 384, 384, 256, 256, 256, 256, 4, 4]
(GQ0, GK0, GV0, GA0, GR0, RQ0, RK0, RV0, RG0, MQ0, MK0, MV0, MO0, MI0, MF0) = (
    int(v) for v in np.cumsum([0] + SIZES[:-1]))
D_IN = sum(SIZES)

FFN_UP, FFN_DOWN = 2 * NJ, 3 * KT
DOWN_PARTS = [(0, 8), (8, 15), (15, 22)]
C_FFA = 0
HALF = P // 2
MIX = ([[(0, GA0, 16), (32, MI0, 4), (64, MF0, 4)]]
       + [[(0, GQ0, P)], [(0, GK0, P)], [(0, GK0 + P, HALF), (HALF, GQ0 + P, HALF)]]
       + [[(0, GV0 + P * i, P)] for i in range(3)]
       + [[(0, RQ0, P)], [(0, RK0 + P, HALF), (HALF, RQ0 + P, HALF)], [(0, RK0, P)]]
       + [[(0, c + P * i, P)] for c, n in ((RV0, 3), (MQ0, 2), (MK0, 2), (MV0, 2), (GR0, 3), (RG0, 3),
                                           (MO0, 2)) for i in range(n)])
C_MIX = FFN_UP + FFN_DOWN
(C_GA, C_GQK, C_GV, C_ROT, C_RV, C_MQK, C_MV, C_GATE) = (
    C_MIX + i for i in (0, 1, 4, 7, 10, 13, 17, 19))
C_K = C_MIX + len(MIX)
C_V, C_OUT, C_Q, C_O = C_K + 8, C_K + 16, C_K + 24, C_K + 32
C_FFB = C_K + 40
assert DEPTH == 2
CHUNKS = C_FFB + FFN_UP + FFN_DOWN

J_FFA, J_HA, J_MIX, J_MEM, J_FEAT, J_XA, J_ATT, J_FFB, J_HB, J_END = (
    -8, 0, 22, 30, 38, 46, 54, 62, 70, 92)


def head_at(h):
    return (0, GDK * h) if h < 4 else (1, HALF + GDK * (h - 4))


def cut(job):
    return job + 1 + KT



R_FFA, R_MIX, R_XA, R_MEM, R_FFB, R_GG, R_RG, R_CONV, R_BA = 0, 8, 16, 24, 32, 40, 43, 46, 62
N_ROWS = 64
LAYER_DMAS = 10

K_ID, K_CAUSAL, K_HEAD, K_MEAN, K_ONE, K_SWAP, K_FREQ, K_EPS = (
    0, 128, 256, 384, 385, 386, 514, 515)
K_N = 516

HEAVY_LEVELS = [64, 32]
LEVELS = [16, 8, 4, 2, 1]
X_ORDER = [64, 32, 16, 8, 4, 2, 1, 256, 128]
X_SLOTS = 3
U_OFF = GH * (2 + len(LEVELS))
U_XA = U_OFF + 2 * GH
ML_STEPS, RET_STEPS = MH // 2 * TB, GH // 2 * TB
MEM_TURNS = {2: (0,), 3: (1,), 4: (2,), 5: (3,), 6: (4, 5), 7: (6, 7)}
GLA_NORMS = {1: 0, 4: 1, 5: 2}
POST = {0: (0, 2), 1: (6, 2), 2: (1, 2), 3: (7, 2), 4: (2, 2), 5: (3, 0), 7: (3, 1), 9: (4, 0),
        11: (4, 1), 13: (5, 0), 14: (5, 1)}
FEAT_ORDER = [0, 6, 1, 7, 2, 3, 4, 5]


XA_STEPS = [("query", 0), ("query", 1), ("scores", 0), ("query", 2), ("scores", 1), ("query", 3),
            ("turn", 0), ("scores", 2), ("query", 4), ("turn", 1), ("scores", 3), ("query", 5),
            ("turn", 2), ("scores", 4), ("query", 6), ("turn", 3), ("scores", 5), ("query", 7),
            ("turn", 4), ("scores", 6), ("turn", 5), ("scores", 7), ("out", 0), ("turn", 6),
            ("out", 1), ("turn", 7), ("out", 2), ("out", 3)]


def constants():
    c = np.zeros((P, K_N), np.float32)
    j, i = np.arange(P)[:, None], np.arange(P)[None, :]
    c[:, K_ID:K_ID + P] = np.eye(P)
    c[:, K_CAUSAL:K_CAUSAL + P] = j <= i
    c[:, K_HEAD:K_HEAD + P] = (j // DV == i // DV) / DV
    c[:, K_MEAN] = 1.0 / D
    c[:, K_ONE] = 1.0
    half = GDK // 2
    for h in range(P // GDK):
        for r in range(half):
            c[GDK * h + half + r, K_SWAP + GDK * h + r] = -1.0
            c[GDK * h + r, K_SWAP + GDK * h + half + r] = 1.0
    freq = (np.float32(1.0) / (np.float32(10000.0) ** np.linspace(0, 1, half, dtype=np.float32)))
    c[:, K_FREQ] = np.tile(freq.astype(np.float32), P // half)
    c[:, K_EPS] = EPS
    lg = np.log(1.0 - 2.0 ** (-5.0 - np.arange(GH)))
    rel = np.arange(S)[None, :] - np.arange(P)[:, None]
    dec = np.where(rel >= 0, np.exp(lg[:, None, None] * np.maximum(rel, 0)), 0.0) * GDK ** -0.5
    decay = np.ascontiguousarray(dec.transpose(1, 0, 2)).astype(np.float32)
    masks = np.zeros((P, 6, P), bool)
    for n, low in enumerate([HEAVY_LEVELS] + [[v] for v in LEVELS]):
        for v in low:
            masks[:, n] |= ((j // (2 * v) == i // (2 * v)) & (j % (2 * v) < v) & (i % (2 * v) >= v))
    return c, decay, masks.astype(np.float32)


class Banks:

    def __init__(self, engine, banks):
        self.engine, self.banks, self.n = engine, banks, 0
        self.freed, self.of, self.full = [None] * len(banks), {}, {}

    def next(self, name, sem, value):
        b = self.n % len(self.banks)
        if self.freed[b] is not None:
            self.engine.wait_ge(*self.freed[b])
        self.freed[b] = (sem, value)
        self.n += 1
        assert name not in self.of, name
        self.of[name] = self.banks[b]
        return self.banks[b]

    def there(self, name):
        self.full[name] = len(self.full) + 1


def build(nc, A, out):
    ctx = ExitStack()
    with ctx:
        at = [-(-nc.sbuf_base // 32) * 32]

        def place(name, shape, dt=F32, offset=None):
            size = int(np.prod(shape[1:])) * (1 if dt == U8 else 4)
            o = at[0] if offset is None else offset
            if offset is None:
                at[0] += -(-size // 32) * 32
                assert at[0] <= nc.sbuf_usable_end, (name, at[0])
            return nc.alloc_sbuf_tensor_at(name, shape, dt, offset=o)

        UNIT = S * 4
        x = place("x", [P, KT, S])
        xh = place("xh", [P, KT, S], F32R)
        xl = place("xl", [P, KT, S], F32R)
        raw = [place(f"w_raw{i}", [P, 8, P]) for i in range(4)]
        whi = [place(f"w_hi{i}", [P, 8, P], F32R) for i in range(2)]
        wlo = [place(f"w_lo{i}", [P, 8, P], F32R) for i in range(2)]
        region = at[0]
        hh = place("h_hi", [P, NJ, S], F32R)
        hl = place("h_lo", [P, NJ, S], F32R)

        def unit(name, first, shape, dt=F32):
            assert first * UNIT + int(np.prod(shape[1:])) * 4 <= 2 * NJ * UNIT
            return place(name, shape, dt, region + first * UNIT)

        gq = unit("gq", 0, [P, 2, S])
        gk = unit("gk", 2, [P, 2, S])
        p64 = unit("p64", 4, [P, 2, S])
        p128 = unit("p128", 6, [P, 2, S])
        p256 = unit("p256", 8, [P, 2, S])
        xs = [unit(f"xs{i}", 10 + 2 * i, [P, 2, S]) for i in range(X_SLOTS)]
        sdiag = unit("sdiag", 16, [P, GH, TB, P])
        gv = unit("gv", 22, [P, TB, GH * DV])
        rqk = unit("rqk", 25, [P, 4, S])
        rv = unit("rv", 29, [P, TB, GH * DV])
        mqk = unit("mqk", 32, [P, 4, S])
        mv = unit("mv", 36, [P, TB, MH * DV])
        sg = [unit(f"sg{i}", 4 + 3 * i, [P, 2, S + 256]) for i in range(2)]
        row_u = unit("row_u", 38, [P, S])
        row_b = unit("row_b", 39, [P, S])
        row_m = unit("row_m", 40, [P, S])
        row_e = unit("row_e", 41, [P, S])
        sm = [unit(f"sm{i}", 42 + i, [P, S]) for i in range(2)]
        ga_t = unit("ga_t", 10, [P, S])
        gates = unit("gates", 0, [P, 8, S])
        negm = [unit(f"negm{i}", 8 + i, [P, S]) for i in range(2)]
        gsq0 = unit("gsq0", 10, [P, S])
        sm += [unit(f"sm{i}", 11 + i, [P, S]) for i in range(2, 4)]
        o_ret = unit("o_ret", 8, [P, 3, S])
        o_ml = unit("o_ml", 11, [P, 2, S])
        memraw = unit("memraw", 13, [P, 2, D])
        memhi = unit("memhi", 17, [P, KT, MEM], F32R)
        memlo = unit("memlo", 21, [P, KT, MEM], F32R)
        psq = [unit(f"psq{i}", 40 + i, [P, S]) for i in range(2)]
        kx = unit("kx", 32, [P, KT, MEM])
        vx = unit("vx", 36, [P, 2, D])
        memsq = unit("memsq", 17, [P, D])
        ah = unit("a_hi", 0, [P, KT, S], F32R)
        al = unit("a_lo", 8, [P, KT, S], F32R)
        qx = unit("qx", 16, [P, KT, S])
        prob = [unit(f"prob{i}", 24 + i, [P, 2, MEM]) for i in range(2)]
        pt = [unit(f"pt{i}", 40 if i == 3 else 26 + 2 * i, [P, 2, S]) for i in range(XH)]
        xin = unit("xin", 0, [P, TB, D])
        prow = unit("prow", 22, [P, P])
        pfin = unit("pfin", 23, [P, P])
        xsq = unit("xsq", 24, [P, KT, S])
        posi = unit("posi", 16, [P, S], I32)
        ang = unit("ang", 17, [P, S])
        turns = unit("turns", 19, [P, S])
        masks_in = unit("masks_in", 20, [P, 6, P])
        yout = unit("yout", 0, [P, TB, D])
        yk = [unit(f"yk{i}", 16 + i, [P, S]) for i in range(2)]

        T = [place(f"tmp{i}", [P, S]) for i in range(4)]
        stat = place("stat", [P, S])
        o_gla = place("o_gla", [P, 3, S])
        rtmp = place("rtmp", [P, S])
        gsq = [gsq0, rtmp]
        hrms = [place(f"hrms{i}", [P, 2 * TB]) for i in range(2)]
        sincos = place("sincos", [P, 2, S])
        decay = place("decay", [P, GH, S])
        const = place("const", [P, K_N])
        masks = place("masks", [P, 6, P], U8)
        pcols = place("pcols", [P, DEPTH * N_ROWS + KT])
        pcol = place("pcol", [P, N_ROWS])
        w_a2 = place("w_a2", [16, GH * GDK])
        b_if = place("b_if", [MH, 2])
        ucol = place("ucol", [P, TB, MH])
        memst = place("memst", [P, 4])
        smx = place("smx", [P, 2, 4])
        ident = const[:, K_ID:K_ID + P]
        eps = const[:, K_EPS:K_EPS + 1]

        psum = [ctx.enter_context(nc.psum_tensor(f"bank{i}", [P, S], F32)) for i in range(8)]
        RB, SB, OB = psum[0:4], psum[4:6], psum[6:8]
        LB = psum[4:8]

        loop_sems = []
        rings = []

        def sem(name):
            s = ctx.enter_context(nc.semaphore(name))
            loop_sems.append(s)
            return s

        w_loaded = [sem(f"w_loaded{i}") for i in range(4)]
        w_pieces = [sem(f"w_pieces{i}") for i in range(4)]
        w_hi, w_lo, chunk_done = sem("w_hi"), sem("w_lo"), sem("chunk_done")
        val_ready, hi_ready, lo_ready = sem("val_ready"), sem("hi_ready"), sem("lo_ready")
        tile_full = sem("tile_full")
        sq_added, rms_ready, sq_ready = sem("sq_added"), sem("rms_ready"), sem("sq_ready")
        a_scaled, g_scaled = sem("a_scaled"), sem("g_scaled")
        silu_ready, params_in, params_up = sem("silu_ready"), sem("params_in"), sem("params_up")
        biases_in = sem("biases_in")
        ga_ready, row_in, z_in, ln_ready = sem("ga_ready"), sem("row_in"), sem("z_in"), sem("ln_ready")
        act_link, dve_link = sem("act_link"), sem("dve_link")
        rows_ready, em_ready = sem("rows_ready"), sem("em_ready")
        gqk_ready, stage_ready, vtok_ready = sem("gqk_ready"), sem("stage_ready"), sem("vtok_ready")
        rot_copied, rot_ready = sem("rot_copied"), sem("rot_ready")
        conv_ready, mqk_ready = sem("conv_ready"), sem("mqk_ready")
        gate_copied, gate_ready = sem("gate_copied"), sem("gate_ready")
        e_ready, exp_ready, xs_ready = sem("e_ready"), sem("exp_ready"), sem("xs_ready")
        s_full, s_done = sem("s_full"), sem("s_done")
        head_rms, normed = sem("head_rms"), sem("normed")
        ml_full, ml_done, negm_ready = sem("ml_full"), sem("ml_done"), sem("negm_ready")
        ret_full, ret_done = sem("ret_full"), sem("ret_done")
        o_full, o_taken, den_abs = sem("o_full"), sem("o_taken"), sem("den_abs")
        ucol_ready, dlog_ready, dexp_ready = sem("ucol_ready"), sem("dlog_ready"), sem("dexp_ready")
        xc_ready, post_sq, post_rms = sem("xc_ready"), sem("post_sq"), sem("post_rms")
        mem_in, mem_rms, memn_ready = sem("mem_in"), sem("mem_rms"), sem("memn_ready")
        kx_ready, qx_ready, pt_ready = sem("kx_ready"), sem("qx_ready"), sem("pt_ready")
        max_ready, prob_exp, prob_ready = sem("max_ready"), sem("prob_exp"), sem("prob_ready")

        w_first = [ctx.enter_context(nc.semaphore(f"w_first{i}")) for i in range(4)]
        once_in, angle_in, decay_in, masks_in_, params_all, once_pe, once_dve, once_act = (
            ctx.enter_context(nc.semaphore(n))
            for n in ("once_in", "angle_in", "decay_in", "masks_in", "params_all", "once_pe",
                      "once_dve", "once_act"))
        x_in = [ctx.enter_context(nc.semaphore(f"x_in{t}")) for t in range(TB)]
        angle_step, angle_ready, angle_abs, x_squares = (
            ctx.enter_context(nc.semaphore(n))
            for n in ("angle_step", "angle_ready", "angle_abs", "x_squares"))
        y_pe, y_ready, y_out, y_act, y_gained = (
            ctx.enter_context(nc.semaphore(n)) for n in ("y_pe", "y_ready", "y_out", "y_act",
                                                         "y_gained"))

        x_tok = A["x"].rearrange("b (t p) d -> p (b t) d", p=P)
        mem_tok = A["mem"].rearrange("b (t p) d -> p (b t) d", p=P)
        out_tok = out.rearrange("b (t p) d -> p (b t) d", p=P)

        gu = [A[n].rearrange("l (k p) (h j c) -> l h j p k c", p=P, h=2, c=P)
              for n in ("w_ffa_gu", "w_ffb_gu")]

        def load_first(sp, layer):
            for c in range(4):
                if layer > 0:
                    last = CHUNKS - 1 - (CHUNKS - 1 - c) % 4
                    sp.wait_ge(w_hi, last + 1)
                    sp.wait_ge(w_lo, last + 1)
                sp.dma_start(raw[c][:], gu[0][layer, c % 2, c // 2]).then_inc(w_first[c], 16)

        with nc.Block() as block:
            def layer_params(engine, l):
                def rows(r, src, n):
                    r += l * N_ROWS
                    engine.dma_start(prow[r:r + n, :], src).then_inc(params_all, 16)

                for r, n in ((R_FFA, "g_ffa"), (R_MIX, "g_mix"), (R_XA, "g_xa"), (R_MEM, "g_mem"),
                             (R_FFB, "g_ffb")):
                    rows(r, A[n][l].rearrange("(k p) -> k p", p=P), KT)
                rows(R_GG, A["gla_g_norm"][l].rearrange("(k p) -> k p", p=P), 3)
                rows(R_RG, A["ret_g_norm"][l].rearrange("(k p) -> k p", p=P), 3)
                rows(R_CONV, A["ml_conv"][l].rearrange("j (t p) -> (j t) p", p=P), 16)
                b_a = A["gla_b_a"].rearrange("l (o c) -> l o c", o=1)
                for t in range(2):
                    rows(R_BA + t, b_a[l, :, t * HALF:t * HALF + P], 1)

            @block.sync
            def _(sp):
                for t in range(TB):
                    sp.dma_start(xin[:, t, :], x_tok[:, t, :]).then_inc(x_in[t], 16)
                load_first(sp, 0)
                layer_params(sp, 1)
                sp.dma_start(decay[:], A["c_decay"]).then_inc(decay_in, 16)
                sp.wait_ge(decay_in, 16)

            @block.scalar
            def _(act):
                act.dma_start(posi[:], A["positions"].to_broadcast([P, S])).then_inc(angle_in, 16)
                act.dma_start(const[:], A["c_const"]).then_inc(once_in, 16)
                layer_params(act, 0)
                act.dma_start(pfin[0:KT, :], A["g_final"].rearrange("(k p) -> k p", p=P))\
                   .then_inc(params_all, 16)
                act.dma_start(masks_in[:], A["c_masks"]).then_inc(masks_in_, 16)
                act.wait_ge(angle_ready, 1)
                act.activation(sincos[:, 1, :], ang[:], ACT.Sin)
                act.activation(turns[:], ang[:], ACT.Abs).then_inc(angle_abs, 1)
                act.wait_ge(angle_ready, 2)
                act.activation(sincos[:, 0, :], turns[:], ACT.Sin)
                for k in range(KT):
                    act.wait_ge(once_dve, k + 1)
                    act.activation(xsq[:, k, :], x[:, k, :], ACT.Square).then_inc(once_act, 1)

            @block.tensor
            def _(pe):
                pe.wait_ge(once_in, 16)
                for t in range(TB):
                    pe.wait_ge(x_in[t], 16)
                    for k in range(KT):
                        m = pe.transpose(psum[k][:, t * P:(t + 1) * P],
                                         xin[:, t, k * P:(k + 1) * P], ident)
                        if t == TB - 1:
                            m.then_inc(once_pe, 1)
                pe.wait_ge(params_all, 16 * (2 * LAYER_DMAS + 1))
                pe.wait_ge(once_dve, 1)
                pe.transpose(psum[0][:, 0:P], prow[:], ident)
                pe.transpose(psum[0][:, P:P + KT], pfin[0:KT, :], ident[0:KT, 0:KT])\
                  .then_inc(once_pe, 1)

            @block.vector
            def _(dve):
                two_pi = 2.0 * np.pi
                c1 = 6.28125
                c2 = float(np.float32(np.floor((two_pi - c1) * 2 ** 21) / 2 ** 21))
                c3 = float(two_pi - c1 - c2)
                steps = [0]

                def step(ins):
                    steps[0] += 1
                    ins.then_inc(angle_step, 1)
                    dve.wait_ge(angle_step, steps[0])

                dve.wait_ge(angle_in, 16)
                step(dve.tensor_copy(turns[:], posi[:]))
                dve.wait_ge(once_in, 16)
                step(dve.tensor_scalar(ang[:], turns[:], const[:, K_FREQ:K_FREQ + 1],
                                       None, ALU.mult))
                step(dve.tensor_scalar(turns[:], ang[:], 1.0 / two_pi, 12582912.0,
                                       ALU.mult, ALU.add))
                step(dve.tensor_scalar(turns[:], turns[:], 12582912.0, None, ALU.subtract))
                for c in (c1, c2, c3):
                    step(dve.scalar_tensor_tensor(ang[:], turns[:], -c, ang[:],
                                                  ALU.mult, ALU.add))
                dve.tensor_scalar(ang[:], ang[:], 3.1415925, -3.1415925,
                                  ALU.min, ALU.max).then_inc(angle_ready, 1)

                def add_square(k):
                    dve.wait_ge(once_act, k + 1)
                    if k > 1:
                        dve.wait_ge(x_squares, k - 1)
                    dve.tensor_tensor(stat[:], xsq[:, 0, :] if k == 1 else stat[:], xsq[:, k, :],
                                      ALU.add).then_inc(x_squares, 1)

                for k in range(KT):
                    dve.wait_ge(once_pe, k + 1)
                    dve.tensor_copy(x[:, k, :], psum[k][:]).then_inc(once_dve, 1)
                    if k == 1:
                        dve.wait_ge(angle_abs, 1)
                        dve.tensor_scalar(turns[:], turns[:], -1.0, float(np.pi / 2),
                                          ALU.mult, ALU.add).then_inc(angle_ready, 1)
                    if k >= 4:
                        add_square(k - 3)
                for k in range(KT - 3, KT):
                    add_square(k)
                dve.wait_ge(once_pe, KT + 1)
                dve.tensor_copy(pcols[:], psum[0][:, 0:DEPTH * N_ROWS + KT])
                dve.wait_ge(masks_in_, 16)
                dve.tensor_copy(masks[:], masks_in[:])

        w_in = A["w_in"].rearrange("l (k p) c -> l p k c", p=P)
        down = [A[n].rearrange("l (k p) (m c) -> l m p k c", p=P, c=P)
                for n in ("w_ffa_down", "w_ffb_down")]
        w_kv = A["w_xa_kv"].rearrange("l (k p) c -> l p k c", p=P)
        square = {n: A[n].rearrange("l (k p) c -> l p k c", p=P) for n in ("w_out", "w_xa_q", "w_xa_o")}

        with nc.Fori(0, DEPTH) as lay:
            with nc.Block() as block:

                @block.sync
                def _(sp):
                    def slot_free(c):
                        sp.wait_ge(w_hi, c - 3)
                        sp.wait_ge(w_lo, c - 3)

                    def load(c, src):
                        slot_free(c)
                        n, w = src.shape[-2], src.shape[-1]
                        sp.dma_start(raw[c % 4][:, 0:n, 0:w], src).then_inc(w_loaded[c % 4], 16)

                    def ffn(base, w_up, w_down):
                        for c in range(4 if base > 0 else 0):
                            load(base + c, w_up[lay, c % 2, c // 2])
                        with sp.Fori(1, NJ // 2) as it:
                            for s in range(4):
                                slot_free(it * 4 + (base + s))
                                sp.dma_start(raw[(base + s) % 4][:], w_up[lay, s % 2, it * 2 + s // 2])\
                                  .then_inc(w_loaded[(base + s) % 4], 16)
                        for m in range(KT):
                            for i, (k0, k1) in enumerate(DOWN_PARTS):
                                load(base + FFN_UP + 3 * m + i, w_down[lay, m, :, k0:k1, :])

                    ffn(C_FFA, gu[0], down[0])
                    for i, pieces in enumerate(MIX):
                        c = C_MIX + i
                        slot_free(c)
                        for n, (at_, c0, w) in enumerate(pieces):
                            sp.dma_start(raw[c % 4][:, :, at_:at_ + w], w_in[lay, :, :, c0:c0 + w])\
                              .then_inc(w_loaded[c % 4] if n == 0 else w_pieces[c % 4], 16)
                    for m in range(16):
                        load(C_K + m, w_kv[lay, :, :, m * P:(m + 1) * P])
                    for c0, n in ((C_OUT, "w_out"), (C_Q, "w_xa_q"), (C_O, "w_xa_o")):
                        for m in range(KT):
                            load(c0 + m, square[n][lay, :, :, m * P:(m + 1) * P])
                    ffn(C_FFB, gu[1], down[1])
                    load_first(sp, DEPTH - 1)

                @block.gpsimd
                def _(pool):
                    def lo(c, parity, n=8):
                        pool.wait_ge(w_hi, c + 1)
                        r = raw[parity % 4]
                        pool.tensor_tensor(wlo[parity % 2][:, 0:n], r[:, 0:n],
                                           whi[parity % 2][:, 0:n].bitcast(F32),
                                           ALU.subtract).then_inc(w_lo, 1)

                    def ffn(base):
                        with pool.Fori(0, NJ // 2) as it:
                            for s in range(4):
                                lo(it * 4 + (base + s), base + s)
                        for m in range(KT):
                            for i, (k0, k1) in enumerate(DOWN_PARTS):
                                c = base + FFN_UP + 3 * m + i
                                lo(c, c, k1 - k0)

                    ffn(C_FFA)
                    for c in range(C_MIX, C_FFB):
                        lo(c, c)
                    ffn(C_FFB)

                @block.tensor
                def _(pe):
                    ring = Banks(pe, RB)
                    rings.append(ring)

                    def signal_tile(name, m):
                        ring.there(name)
                        m.then_inc(tile_full, 1)

                    def chunk(c, bank, rhs_hi, rhs_lo, k0=0, k1=8, jobs=None, start=True,
                              stop=True, parity=None, cols=S, order=None):
                        q = c if parity is None else parity
                        pe.wait_ge(w_lo, c + 1)
                        o, wh, wl = bank[:, 0:cols], whi[q % 2], wlo[q % 2]
                        for n, k in enumerate(order or range(k0, k1)):
                            if jobs is not None:
                                pe.wait_ge(lo_ready, cut(jobs + n))
                            pe.matmul(o, wl[:, k - k0, :], rhs_hi[:, k, :],
                                      start=start and n == 0, stop=False)
                            pe.matmul(o, wh[:, k - k0, :], rhs_lo[:, k, :], start=False, stop=False)
                        for k in range(k0, k1):
                            m = pe.matmul(o, wh[:, k - k0, :], rhs_hi[:, k, :], start=False,
                                          stop=stop and k == k1 - 1)
                        m.then_inc(chunk_done, 1)

                    def norm_stat(i):
                        if i > 0:
                            pe.wait_ge(sq_added, KT * i)
                        ring.of["stat", i] = SB[0]
                        signal_tile(("stat", i), pe.matmul(
                            SB[0][:], const[:, K_MEAN:K_MEAN + 1].to_broadcast([P, P]), stat[:],
                            start=True, stop=True))

                    def ffn(base, job, hjob, i, nxt):
                        n0 = ring.n

                        def up(it, first):
                            for s in range(4):
                                j = it * 2 + s // 2
                                b = RB[(n0 + s) % 4]
                                if first:
                                    b = ring.next(("up", i, s), val_ready, hjob + s // 2 + 1)
                                else:
                                    pe.wait_ge(val_ready, j + (hjob - 1))
                                chunk(it * 4 + (base + s), b, xh, xl, parity=base + s,
                                      jobs=job if first and s == 0 else None)
                                if first and s == 0:
                                    norm_stat(i)

                        up(0, True)
                        with pe.Fori(1, NJ // 2) as it:
                            up(it, False)
                        for s in range(4):
                            ring.freed[(n0 + s) % 4] = (val_ready, hjob + NJ - 1 + s // 2)
                        for m in range(KT):
                            b = ring.next(("down", i, m), val_ready, nxt + m + 1)
                            for q, (k0, k1) in enumerate(DOWN_PARTS):
                                chunk(base + FFN_UP + 3 * m + q, b, hh, hl, k0, k1,
                                      jobs=hjob + k0 if m == 0 else None, start=q == 0, stop=q == 2)

                    ffn(C_FFA, J_FFA, J_HA, 0, J_MIX)

                    def turn(n, cols=S):
                        pe.wait_ge(stage_ready, n + 1)
                        b = ring.next(("turn", n), vtok_ready, n + 1)
                        for t in range(cols // P):
                            m = pe.transpose(b[:, t * P:(t + 1) * P], T[2 + n % 2][:, t * P:(t + 1) * P],
                                             ident)
                        signal_tile(("turn", n), m)

                    chunk(C_GA, ring.next("ga", row_in, 2), xh, xl, jobs=J_MIX)
                    norm_stat(1)
                    for n in range(3):
                        chunk(C_GQK + n, ring.next(("gqk", n), gqk_ready, n + 1), xh, xl)
                        if n == 0:
                            pe.wait_ge(ga_ready, 1)
                            pe.wait_ge(params_in, 16)
                            for t in range(2):
                                b = ring.next(("z", t), z_in, t + 1)
                                signal_tile(("z", t), pe.matmul(b[:], w_a2[:, t * HALF:t * HALF + P],
                                                                ga_t[0:16, :], start=True, stop=True))
                    for n in range(4):
                        if n < 3:
                            chunk(C_GV + n, ring.next(("v", n), stage_ready, n + 1), xh, xl)
                        if n >= 1:
                            turn(n - 1)

                    unit_n = [0]

                    def scores():
                        u = unit_n[0]
                        unit_n[0] += 1
                        if u < U_OFF:
                            if u >= 4:
                                pe.wait_ge(s_done, u - 3)
                            return LB[u % 4]
                        pe.wait_ge(s_done, u - 1)
                        return SB[u % 2]

                    def rot(n):
                        chunk(C_ROT + n, ring.next(("rot", n), rot_copied, n + 1), xh, xl)

                    def swap(n):
                        pe.wait_ge(rot_copied, n + 1)
                        b = ring.next(("swap", n), rot_ready, 2 * n + 1)
                        signal_tile(("swap", n), pe.matmul(b[:], const[:, K_SWAP:K_SWAP + P],
                                                           rqk[:, n, :], start=True, stop=True))

                    def vchunk(c, n):
                        chunk(c, ring.next(("v", n), stage_ready, n + 1), xh, xl)

                    def qk_chunk(n):
                        chunk(C_MQK + n, ring.next(("mqk", n), conv_ready, 5 * n + 5), xh, xl)

                    fill = [
                        lambda: (rot(0), rot(1), swap(0)),
                        lambda: (rot(2), swap(1)),
                        lambda: (vchunk(C_RV, 3), swap(2), vchunk(C_RV + 1, 4), turn(3)),
                        lambda: (vchunk(C_RV + 2, 5), turn(4), qk_chunk(0), turn(5)),
                        lambda: (qk_chunk(1), qk_chunk(2)),
                        lambda: (qk_chunk(3), vchunk(C_MV, 6)),
                        lambda: vchunk(C_MV + 1, 7),
                    ]

                    def head_rows(t3, h):
                        t, r = head_at(h)
                        return t3[r:r + GDK, t, :]

                    pe.wait_ge(gqk_ready, 3)
                    for h in range(0, GH, 2):
                        pair = [(h, scores()), (h + 1, scores())]
                        for t in range(TB):
                            c = slice(t * P, (t + 1) * P)
                            for hd, b in pair:
                                m = pe.matmul(b[:, c], head_rows(gk, hd)[:, c],
                                              head_rows(gq, hd)[:, c], start=True, stop=True)
                                if t == TB - 1:
                                    m.then_inc(s_full, 1)
                    fill[0]()
                    pe.wait_ge(xs_ready, 2)
                    for h in range(GH):
                        b = scores()
                        for t in range(TB):
                            for n, v in enumerate(HEAVY_LEVELS):
                                r = head_rows(xs[n], h)
                                for g in range(P // (2 * v)):
                                    k0 = 2 * v * g
                                    m = pe.matmul(b[k0:k0 + v, t * P + k0 + v:t * P + k0 + 2 * v],
                                                  r[:, t * P + k0:t * P + k0 + v],
                                                  r[:, t * P + k0 + v:t * P + k0 + 2 * v],
                                                  start=True, stop=True)
                        m.then_inc(s_full, 1)
                    fill[1]()
                    for n, v in enumerate(LEVELS):
                        pe.wait_ge(xs_ready, 3 + n)
                        for h in range(0, GH, 2):
                            pair = [(head_rows(xs[(2 + n) % X_SLOTS], h + e), scores())
                                    for e in range(2)]
                            for t in range(TB):
                                c = slice(t * P, (t + 1) * P)
                                for r, b in pair:
                                    m = pe.matmul(b[:, c], r[:, c], r[:, c], start=True, stop=True)
                                    if t == TB - 1:
                                        m.then_inc(s_full, 1)
                        fill[2 + n]()

                    o_n = [0]

                    def o_bank():
                        q = o_n[0]
                        if q >= 2:
                            pe.wait_ge(o_taken, q - 1)
                        o_n[0] += 1
                        return OB[q % 2]

                    def gate(n):
                        chunk(C_GATE + n, ring.next(("gate", n), gate_copied, n + 1), xh, xl)

                    pe.wait_ge(xs_ready, 9)
                    x256, x128 = xs[7 % X_SLOTS], xs[8 % X_SLOTS]
                    pe.wait_ge(vtok_ready, 3)

                    def gla_off(p):
                        banks = [ring.next(("off", u), s_done, U_OFF + u + 1)
                                 for u in range(4 * p, 4 * p + 4)]
                        unit_n[0] += 4
                        for jt in range(2):
                            for e in range(2):
                                r = head_rows(x256, 2 * p + e)
                                m = pe.matmul(banks[e][:, jt * 256:(jt + 1) * 256],
                                              r[:, jt * P:(jt + 1) * P], r[:, 256:512],
                                              start=True, stop=True)
                                if jt == 1:
                                    m.then_inc(s_full, 1)
                        for n in range(2):
                            for e in range(2):
                                r = head_rows(x128, 2 * p + e)
                                m = pe.matmul(banks[2 + e][:, n * P:(n + 1) * P],
                                              r[:, n * 256:n * 256 + P],
                                              r[:, n * 256 + P:n * 256 + 256], start=True, stop=True)
                                if n == 1:
                                    m.then_inc(s_full, 1)

                    def gla_pv(p):
                        ob = o_bank()
                        pe.wait_ge(s_done, U_OFF + 4 * p + 4)
                        pieces = [(jt, lambda e, jt=jt: sdiag[:, 2 * p + e, jt, :], jt * P)
                                  for jt in range(TB)]
                        pieces += [(jt, lambda e, jt=jt: sg[p % 2][:, e, jt * 256:(jt + 1) * 256], 256)
                                   for jt in range(2)]
                        pieces += [(2 * n, lambda e, n=n: sg[p % 2][:, e, S + n * P:S + (n + 1) * P],
                                    n * 256 + P) for n in range(2)]
                        for n, (jt, scores_of, i0) in enumerate(pieces):
                            for e in range(2):
                                s, h = scores_of(e), 2 * p + e
                                m = pe.matmul(ob[DV * e:DV * (e + 1), i0:i0 + s.shape[-1]],
                                              gv[:, jt, h * DV:(h + 1) * DV], s, start=n == 0,
                                              stop=n == len(pieces) - 1, skip_group_check=True)
                                if n == len(pieces) - 1:
                                    m.then_inc(o_full, 1)

                    gla_off(0)
                    turn(6)
                    turn(7)
                    gla_off(1)
                    gla_pv(0)
                    gla_off(2)
                    gla_pv(1)
                    gla_pv(2)

                    pe.wait_ge(rows_ready, 4)
                    b = ring.next("ucol", ucol_ready, 1)
                    for t in range(TB):
                        m = pe.transpose(b[:, t * MH:(t + 1) * MH], row_u[0:MH, t * P:(t + 1) * P],
                                         ident[0:MH, 0:MH])
                    signal_tile("ucol", m)
                    pe.wait_ge(mqk_ready, 4)
                    pe.wait_ge(vtok_ready, 8)
                    pe.wait_ge(em_ready, 1)

                    def mem_turn(k):
                        if k == 0:
                            pe.wait_ge(memn_ready, 2)
                        b = ring.next(("mem", k), val_ready, J_MEM + k + 1)
                        for t in range(2):
                            m = pe.transpose(b[:, t * P:(t + 1) * P], memraw[:, t, k * P:(k + 1) * P],
                                             ident)
                        signal_tile(("mem", k), m)

                    def stat_of(p, step):
                        if step == 0:
                            pe.wait_ge(o_taken, 7 + p - 3 + 1)
                            b = ring.next(("mean", p), xc_ready, p - 3 + 1)
                            signal_tile(("mean", p), pe.matmul(
                                b[:], const[:, K_HEAD:K_HEAD + P], o_ret[:, p - 3, :],
                                start=True, stop=True))
                        else:
                            pe.wait_ge(post_sq, p + 1)
                            b = ring.next(("post", p), post_rms, p + 1)
                            src = (gsq if p < 3 else psq)[p % 2]
                            for t in range(TB):
                                m = pe.matmul(b[:, 2 * t:2 * t + 2], src[:, t * P:(t + 1) * P],
                                              const[:, K_HEAD:K_HEAD + P:DV], start=True, stop=True)
                            signal_tile(("post", p), m)

                    def spread(p):
                        pe.wait_ge(head_rms, p + 1)
                        b = ring.next(("spread", p), normed, p + 1)
                        for t in range(TB):
                            for e in range(2):
                                r = hrms[p % 2][:, 2 * t + e:2 * t + e + 1].to_broadcast([P, DV])
                                m = pe.matmul(b[DV * e:DV * (e + 1), t * P:(t + 1) * P], r, ident,
                                              start=True, stop=True)
                        signal_tile(("spread", p), m)

                    for n in range(ML_STEPS):
                        p, jt = divmod(n, TB)
                        w = S - jt * P
                        if jt == 0:
                            for h in (2 * p, 2 * p + 1):
                                b = ring.next(("negm", h), negm_ready, h + 1)
                                signal_tile(("negm", h), pe.matmul(
                                    b[:], ident[0:MH, h:h + 1].to_broadcast([MH, P]),
                                    row_m[0:MH, :], start=True, stop=True))
                        for e in range(2):
                            r = slice(MDK * e, MDK * (e + 1))
                            m = pe.matmul(SB[e][:, 0:w], mqk[r, 2 + p, jt * P:(jt + 1) * P],
                                          mqk[r, p, jt * P:], start=True, stop=True)
                        m.then_inc(ml_full, 1)
                        gate(n)
                        for k in MEM_TURNS.get(n, ()):
                            mem_turn(k)
                        if n - 1 in GLA_NORMS:
                            spread(GLA_NORMS[n - 1])
                        if n in GLA_NORMS:
                            stat_of(GLA_NORMS[n], 1)
                        if jt == 0:
                            den, num = o_bank(), o_bank()
                        pe.wait_ge(ml_done, n + 1)
                        for e in range(2):
                            h = 2 * p + e
                            pe.matmul(num[DV * e:DV * (e + 1), jt * P:], mv[:, jt, h * DV:(h + 1) * DV],
                                      sm[e][:, 0:w], start=jt == 0, stop=jt == TB - 1,
                                      skip_group_check=True)
                        for e in range(2):
                            m = pe.matmul(den[DV * e:DV * (e + 1), jt * P:],
                                          const[:, K_ONE:K_ONE + 1].to_broadcast([P, DV]),
                                          sm[e][:, 0:w], start=jt == 0, stop=jt == TB - 1,
                                          skip_group_check=True)
                        m.then_inc(o_full, 1)
                        if jt == TB - 1:
                            b = ring.next(("em", p), o_taken, 4 + 2 * p)
                            for e in range(2):
                                m = pe.matmul(b[DV * e:DV * (e + 1), :],
                                              ident[0:MH, 2 * p + e:2 * p + e + 1].to_broadcast([MH, DV]),
                                              row_e[0:MH, :], start=True, stop=True)
                            signal_tile(("em", p), m)

                    def ret_scores(n):
                        if n > 0:
                            pe.wait_ge(ret_done, n)
                        p, jt = divmod(n, TB)
                        for e in range(2):
                            t, r = head_at(2 * p + e)
                            r = slice(r, r + GDK)
                            m = pe.matmul(SB[e][:, 0:S - jt * P], rqk[r, 2 + t, jt * P:(jt + 1) * P],
                                          rqk[r, t, jt * P:], start=True, stop=True)
                        m.then_inc(ret_full, 1)

                    def ret_out(n, ob):
                        pe.wait_ge(ret_done, n + 1)
                        p, jt = divmod(n, TB)
                        for e in range(2):
                            h = 2 * p + e
                            m = pe.matmul(ob[DV * e:DV * (e + 1), jt * P:],
                                          rv[:, jt, h * DV:(h + 1) * DV],
                                          sm[2 * (n % 2) + e][:, 0:S - jt * P],
                                          start=jt == 0, stop=jt == TB - 1, skip_group_check=True)
                        m.then_inc(o_full, 1)

                    pe.wait_ge(rot_ready, 7)
                    ret_scores(0)
                    for m in range(17):
                        if m < 8:
                            chunk(C_K + m, ring.next(("kx", m), kx_ready, m + 1), memhi, memlo, cols=MEM,
                                  jobs=J_MEM if m == 0 else None)
                        elif m < 16:
                            chunk(C_K + m, ring.next(("v", m), stage_ready, m + 1), memhi, memlo, cols=MEM)
                        if m + 1 < RET_STEPS:
                            ret_scores(m + 1)
                        if m < RET_STEPS:
                            if m % TB == 0:
                                ob = o_bank()
                            ret_out(m, ob)
                        if POST.get(m - 1, (0, 0))[1] == 1:
                            spread(POST[m - 1][0])
                        if m > 8:
                            turn(m - 1, MEM)
                        if m in POST and POST[m][1] < 2:
                            stat_of(*POST[m])

                    def project(c0, job, sem_, v0, hi_, lo_):
                        for m in range(KT):
                            chunk(c0 + m, ring.next(("proj", c0 + m), sem_, v0 + m + 1), hi_, lo_,
                                  jobs=job if m == 0 else None,
                                  order=FEAT_ORDER if c0 == C_OUT else None)

                    project(C_OUT, J_FEAT, val_ready, J_XA, xh, xl)
                    pe.wait_ge(kx_ready, KT)
                    pe.wait_ge(vtok_ready, 16)
                    assert unit_n[0] == U_XA

                    def xa_scores(n):
                        h, pair = divmod(n, 2)
                        pe.wait_ge(qx_ready, 2 * h + 2)
                        b = scores()
                        for s in range(2):
                            st = 2 * pair + s
                            for dt in range(2):
                                m = pe.matmul(b[:, s * MEM:(s + 1) * MEM],
                                              qx[:, 2 * h + dt, st * P:(st + 1) * P],
                                              kx[:, 2 * h + dt, :], start=dt == 0, stop=dt == 1)
                        m.then_inc(s_full, 1)

                    def xa_turn(n):
                        pe.wait_ge(prob_ready, 2 * n + 2)
                        b = ring.next(("pt", n), pt_ready, n + 1)
                        for mt in range(2):
                            for s in range(2):
                                m = pe.transpose(b[:, (2 * mt + s) * P:(2 * mt + s + 1) * P],
                                                 prob[n % 2][:, s, mt * P:(mt + 1) * P], ident)
                        signal_tile(("pt", n), m)

                    def xa_out(h):
                        pe.wait_ge(pt_ready, 2 * h + 2)
                        for dt in range(2):
                            b = ring.next(("att", 2 * h + dt), val_ready, J_ATT + 2 * h + dt + 1)
                            for mt in range(2):
                                m = pe.matmul(b[:], vx[:, mt, (2 * h + dt) * P:(2 * h + dt + 1) * P],
                                              pt[h][:, mt, :], start=mt == 0, stop=mt == 1)
                            signal_tile(("att", 2 * h + dt), m)

                    for kind, n in XA_STEPS:
                        if kind == "query":
                            chunk(C_Q + n, ring.next(("proj", C_Q + n), qx_ready, n + 1), ah, al,
                                  jobs=J_XA if n == 0 else None)
                            if n == 0:
                                norm_stat(2)
                        elif kind == "scores":
                            xa_scores(n)
                        elif kind == "turn":
                            xa_turn(n)
                        else:
                            xa_out(n)
                    project(C_O, J_ATT, val_ready, J_FFB, ah, al)
                    ffn(C_FFB, J_FFB, J_HB, 3, J_END)

                @block.scalar
                def _(act):
                    bank, full = rings[-1].of, rings[-1].full
                    spare = act.alloc_register("act_spare")

                    def settle():
                        act.reg_mov(spare, 0)

                    act.dma_start(w_a2[:], A["gla_w_a2"][lay]).then_inc(params_in, 16)
                    for n, name in enumerate(("ml_b_i", "ml_b_f")):
                        act.dma_start(b_if[:, n:n + 1], A[name][lay].rearrange("(h o) -> h o", o=1))\
                           .then_inc(biases_in, 16)

                    head, pieces = [0], [0] * 4

                    def ahead(count=1, n=8):
                        for _ in range(count):
                            c = head[0]
                            if c < 4:
                                act.wait_ge(w_first[c], lay * 16 + 16)
                                settle()
                            else:
                                act.wait_ge(w_loaded[c % 4], 16 * (c // 4))
                            if C_MIX <= c < C_K and len(MIX[c - C_MIX]) > 1:
                                pieces[c % 4] += len(MIX[c - C_MIX]) - 1
                                act.wait_ge(w_pieces[c % 4], 16 * pieces[c % 4])
                            if c >= 2:
                                act.wait_ge(chunk_done, c - 1)
                            act.activation(whi[c % 2][:, 0:n], raw[c % 4][:, 0:n], ACT.Copy)\
                               .then_inc(w_hi, 1)
                            head[0] += 1

                    def hi(job, dst, cols=S):
                        act.wait_ge(val_ready, job + 1)
                        act.activation(dst, T[job % 2][:, 0:cols], ACT.Copy).then_inc(hi_ready, 1)

                    def rms(i):
                        act.wait_ge(tile_full, full["stat", i])
                        act.activation(stat[:], bank["stat", i][:], ACT.Sqrt, bias=eps)\
                           .then_inc(rms_ready, 1)

                    def hi_gained(dst, k, gain):
                        act.activation(dst[:, k, :], x[:, k, :], ACT.Copy,
                                       scale=pcol[:, gain + k:gain + k + 1]).then_inc(hi_ready, 1)

                    added = [0]

                    def new_x(m, job, gain=None, dst=None):
                        act.wait_ge(val_ready, job + m + 1)
                        if gain is not None:
                            hi_gained(dst, m, gain)
                        if m >= 2:
                            act.wait_ge(sq_added, added[0] + m - 1)
                        act.activation(T[2 + m % 2][:], x[:, m, :], ACT.Square).then_inc(sq_ready, 1)
                        if m == KT - 1:
                            added[0] += KT

                    def ffn(base, hjob, i, silus, *nxt):
                        def silu(j, s):
                            act.wait_ge(a_scaled, j + (silus + 1))
                            if not isinstance(j, int):
                                settle()
                            act.activation(T[2 + s][:], T[2 + s][:], ACT.Silu).then_inc(silu_ready, 1)

                        def cut_weights(it, s):
                            q = base + s
                            act.wait_ge(w_loaded[q % 4], it * 16 + 16 * (q // 4))
                            act.wait_ge(chunk_done, it * 4 + (q - 1))
                            settle()
                            act.activation(whi[q % 2][:], raw[q % 4][:], ACT.Copy).then_inc(w_hi, 1)

                        def hidden(it, s):
                            act.wait_ge(val_ready, it * 2 + (hjob + s + 1))
                            settle()
                            act.activation(hh[:, it * 2 + s, :], T[(hjob + s) % 2][:], ACT.Copy)\
                               .then_inc(hi_ready, 1)

                        rms(i)
                        ahead()
                        silu(0, 0)
                        ahead()
                        hi(hjob, hh[:, 0, :])
                        with act.Fori(1, NJ // 2) as it:
                            cut_weights(it, 0)
                            silu(it * 2 - 1, 1)
                            cut_weights(it, 1)
                            hidden(it, -1)
                            cut_weights(it, 2)
                            silu(it * 2, 0)
                            cut_weights(it, 3)
                            hidden(it, 0)
                        d = base + FFN_UP
                        head[0] = d
                        ahead()
                        silu(NJ - 1, 1)
                        ahead(n=7)
                        hi(hjob + NJ - 1, hh[:, NJ - 1, :])
                        for m in range(KT):
                            for q in range(3):
                                if head[0] < CHUNKS:
                                    e = head[0] - d
                                    ahead(n=7 if e < FFN_DOWN and e % 3 else 8)
                            new_x(m, *nxt)

                    ahead()
                    act.wait_ge(params_up, 1)
                    for k in range(KT):
                        hi_gained(xh, k, R_FFA)
                        if k == 2:
                            ahead()
                    ffn(C_FFA, J_HA, 0, 0, J_MIX, R_MIX, xh)

                    rms(1)
                    ahead(2)
                    links = [0]

                    def link(ins):
                        links[0] += 1
                        ins.then_inc(act_link, 1)
                        act.wait_ge(act_link, links[0])

                    def softplus(buf, src, between=None):
                        link(act.activation(buf, src, ACT.Abs))
                        link(act.activation(buf, buf, ACT.Exp, scale=-1.0))
                        if between is not None:
                            between()
                        act.activation(buf, buf, ACT.Ln, bias=1.0).then_inc(ln_ready, 1)

                    act.wait_ge(row_in, 2)
                    softplus(row_m[0:MH, :], row_b[0:MH, :])
                    act.wait_ge(z_in, 2)
                    softplus(p128[:], p64[:], ahead)
                    act.wait_ge(rows_ready, 3)
                    act.activation(row_e[0:MH, :], row_e[0:MH, :], ACT.Exp, scale=-1.0)\
                       .then_inc(em_ready, 1)

                    def exps(n):
                        v, slot = X_ORDER[n], xs[n % X_SLOTS]
                        act.wait_ge(e_ready, n + 1)
                        if v <= 32:
                            act.activation(slot[:], slot[:], ACT.Exp, scale=1 / 16.0)\
                               .then_inc(exp_ready, 1)
                        else:
                            src = {64: p64, 128: p128, 256: p256}[v]
                            s = slot[:].rearrange("p t (n h v) -> p (t n) h v", h=2, v=v)
                            q = src[:].rearrange("p t (n h v) -> p (t n) h v", h=2, v=v)
                            act.activation(s[:, :, 0, :], s[:, :, 0, :], ACT.Exp, scale=1 / 16.0)
                            act.activation(s[:, :, 1, :], q[:, :, 1, :], ACT.Exp, scale=1 / 16.0)\
                               .then_inc(exp_ready, 1)

                    def conv_silu(n):
                        act.wait_ge(conv_ready, 5 * n + 5)
                        act.activation(mqk[:, n, :], mqk[:, n, :], ACT.Silu).then_inc(mqk_ready, 1)

                    ahead()
                    for n in range(3):
                        exps(n)
                        ahead()
                    ahead(2)
                    exps(3)
                    exps(4)
                    ahead()
                    exps(5)
                    ahead(2)
                    exps(6)
                    ahead(2)
                    exps(7)
                    conv_silu(0)
                    ahead(2)
                    exps(8)
                    conv_silu(1)
                    conv_silu(2)
                    ahead(2)
                    conv_silu(3)
                    ahead()
                    assert head[0] == C_GATE + 2

                    act.wait_ge(o_full, GH)
                    act.dma_start(memraw[:], mem_tok).then_inc(mem_in, 16)

                    def gate_act(n):
                        act.wait_ge(gate_copied, n + 1)
                        act.activation(gates[:, n, :], gates[:, n, :],
                                       ACT.Silu if n < 6 else ACT.Sigmoid).then_inc(gate_ready, 1)

                    def rms_of_heads(p):
                        act.wait_ge(tile_full, full["post", p])
                        if p >= 2:
                            act.wait_ge(normed, p - 1)
                        act.activation(hrms[p % 2][:], bank["post", p][:, 0:2 * TB], ACT.Sqrt,
                                       bias=eps).then_inc(post_rms, 1)

                    for n in range(ML_STEPS):
                        p, jt = divmod(n, TB)
                        for e in range(2):
                            act.wait_ge(dlog_ready, 2 * n + e + 1)
                            b = T[2 + e][:, 0:S - jt * P]
                            act.activation(b, b, ACT.Exp).then_inc(dexp_ready, 1)
                        if n == ML_STEPS - 1:
                            for q in range(7):
                                gate_act(q)
                        if n in GLA_NORMS:
                            act.wait_ge(o_taken, GLA_NORMS[n] + 1)
                            if GLA_NORMS[n] == 1:
                                act.wait_ge(o_taken, 5)
                            act.activation(gsq[GLA_NORMS[n] % 2][:], o_gla[:, GLA_NORMS[n], :],
                                           ACT.Square)\
                               .then_inc(post_sq, 1)
                        ahead()
                        if n == 0:
                            act.wait_ge(mem_in, 16)
                            for t in range(2):
                                link(act.activation(memsq[:], memraw[:, t, :], ACT.Square,
                                                    accum_out=memst[:, t:t + 1]))
                            act.activation(memst[:, 2:4], memst[:, 0:2], ACT.Sqrt, bias=eps,
                                           scale=1.0 / D).then_inc(mem_rms, 1)
                        for k in MEM_TURNS.get(n, ()):
                            hi(J_MEM + k, memhi[:, k, :], MEM)
                        if n in GLA_NORMS:
                            rms_of_heads(GLA_NORMS[n])
                        if jt == TB - 1:
                            act.wait_ge(o_full, GH + n + 1)
                            act.activation(rtmp[:], OB[1][:], ACT.Abs).then_inc(den_abs, 1)
                    gate_act(7)

                    def feature_hi(m):
                        p, step = POST.get(m, (0, 0))
                        if step:
                            hi(J_FEAT + FEAT_ORDER.index(p), xh[:, p, :])

                    for m in range(16):
                        p, step = POST.get(m, (0, 0))
                        if step == 1:
                            act.wait_ge(xc_ready, p - 2)
                            act.activation(psq[p % 2][:], o_ret[:, p - 3, :], ACT.Square)\
                               .then_inc(post_sq, 1)
                        ahead()
                        if step == 1:
                            rms_of_heads(p)
                        feature_hi(m - 1)

                    for m in range(KT):
                        ahead()
                        new_x(m, J_XA, R_XA, ah)
                    for kind, n in XA_STEPS:
                        if kind == "query":
                            if n == 0:
                                rms(2)
                            ahead()
                        elif kind == "scores":
                            act.wait_ge(max_ready, n + 1)
                            if n >= 2:
                                act.wait_ge(pt_ready, n - 1)
                            for s in range(2):
                                act.activation(prob[n % 2][:, s, :],
                                               SB[(U_XA + n) % 2][:, s * MEM:(s + 1) * MEM], ACT.Exp,
                                               bias=smx[:, n % 2, s:s + 1], scale=XDH ** -0.5,
                                               accum_out=smx[:, n % 2, 2 + s:3 + s])\
                                   .then_inc(prob_exp, 1)
                        elif kind == "out":
                            for k in (2 * n, 2 * n + 1):
                                hi(J_ATT + k, ah[:, k, :])
                    for m in range(KT):
                        ahead()
                        new_x(m, J_FFB, R_FFB, xh)
                    assert head[0] == C_FFB + 2
                    ffn(C_FFB, J_HB, 3, NJ, J_END)

                @block.vector
                def _(dve):
                    bank, full = rings[-1].of, rings[-1].full
                    links = [0]

                    def link(ins):
                        links[0] += 1
                        ins.then_inc(dve_link, 1)
                        dve.wait_ge(dve_link, links[0])

                    def lo(job, dst, hi_part, cols=S):
                        dve.wait_ge(hi_ready, cut(job))
                        dve.tensor_tensor(dst, T[job % 2][:, 0:cols], hi_part.bitcast(F32),
                                          ALU.subtract).then_inc(lo_ready, 1)

                    def free(job):
                        dve.wait_ge(lo_ready, cut(job - 2))

                    def inverse_rms(i):
                        dve.wait_ge(rms_ready, i + 1)
                        link(dve.reciprocal(stat[:], stat[:]))

                    def lo_gained(k, job, gain, hi_, lo_):
                        dve.wait_ge(hi_ready, cut(job + k))
                        dve.scalar_tensor_tensor(lo_[:, k, :], x[:, k, :],
                                                 pcol[:, gain + k:gain + k + 1],
                                                 hi_[:, k, :].bitcast(F32), ALU.mult, ALU.subtract)\
                           .then_inc(lo_ready, 1)

                    added = [0]

                    def add_square(m):
                        dve.wait_ge(sq_ready, added[0] + 1)
                        if m == 0:
                            ins = dve.tensor_copy(stat[:], T[2][:])
                        else:
                            dve.wait_ge(sq_added, added[0])
                            ins = dve.tensor_tensor(stat[:], stat[:], T[2 + m % 2][:], ALU.add)
                        ins.then_inc(sq_added, 1)
                        added[0] += 1

                    def update_x(chunk_of, name_of, factor, *parts):
                        for m in range(KT):
                            dve.wait_ge(chunk_done, chunk_of(m) + 1)
                            dve.scalar_tensor_tensor(x[:, m, :], bank[name_of(m)][:], factor,
                                                     x[:, m, :], ALU.mult, ALU.add)\
                               .then_inc(val_ready, 1)
                            if m >= 1:
                                if parts:
                                    lo_gained(m - 1, *parts)
                                add_square(m - 1)
                        if parts:
                            lo_gained(KT - 1, *parts)
                        add_square(KT - 1)

                    def ffn(base, hjob, i, silus, *parts):
                        inverse_rms(i)
                        with dve.Fori(0, NJ // 2) as it:
                            for s in range(2):
                                dve.wait_ge(lo_ready, it * 2 + (cut(hjob) + s - 2))
                                dve.wait_ge(chunk_done, it * 4 + (base + 2 * s + 1))
                                dve.tensor_tensor(T[2 + s][:], bank["up", i, 2 * s][:], stat[:],
                                                  ALU.mult).then_inc(a_scaled, 1)
                                dve.wait_ge(chunk_done, it * 4 + (base + 2 * s + 2))
                                dve.tensor_tensor(T[s][:], bank["up", i, 2 * s + 1][:], stat[:],
                                                  ALU.mult).then_inc(g_scaled, 1)
                                dve.wait_ge(g_scaled, it * 2 + (silus + s + 1))
                                dve.wait_ge(silu_ready, it * 2 + (silus + s + 1))
                                dve.tensor_tensor(T[s][:], T[s][:], T[2 + s][:],
                                                  ALU.mult).then_inc(val_ready, 1)
                                dve.wait_ge(hi_ready, it * 2 + (cut(hjob) + s))
                                dve.tensor_tensor(hl[:, it * 2 + s, :], T[s][:],
                                                  hh[:, it * 2 + s, :].bitcast(F32),
                                                  ALU.subtract).then_inc(lo_ready, 1)
                        update_x(lambda m: base + FFN_UP + 3 * m + 2, lambda m: ("down", i, m), 0.5,
                                 *parts)

                    dve.tensor_copy(pcol[:], pcols[:, bass.ds(lay * N_ROWS, N_ROWS)])\
                       .then_inc(params_up, 1)
                    dve.wait_ge(params_up, 1)
                    for k in range(KT):
                        lo_gained(k, J_FFA, R_FFA, xh, xl)
                    ffn(C_FFA, J_HA, 0, 0, J_MIX, R_MIX, xh, xl)

                    inverse_rms(1)
                    dve.wait_ge(chunk_done, C_GA + 1)
                    dve.tensor_tensor(ga_t[0:16, :], bank["ga"][0:16, :], stat[0:16, :], ALU.mult)\
                       .then_inc(ga_ready, 1)
                    dve.wait_ge(biases_in, 32)
                    for n, row in enumerate((row_u, row_b)):
                        r = slice(32 * (n + 1), 32 * (n + 1) + MH)
                        link(dve.tensor_tensor(row[0:MH, :], bank["ga"][r, :], stat[r, :], ALU.mult))
                        dve.tensor_scalar(row[0:MH, :], row[0:MH, :], b_if[:, n:n + 1],
                                          None, ALU.add).then_inc(row_in, 1)
                    for t in range(2):
                        dve.wait_ge(tile_full, full["z", t])
                        dve.tensor_scalar(p64[:, t, :], bank["z", t][:],
                                          pcol[:, R_BA + t:R_BA + t + 1], None, ALU.add)\
                           .then_inc(z_in, 1)
                    def gla_qk(n):
                        dve.wait_ge(chunk_done, C_GQK + n + 1)
                        src = bank["gqk", n]
                        if n != 1:
                            ins = dve.scalar_tensor_tensor(gq[:, n // 2, :], src[:], GDK ** -0.5,
                                                           stat[:], ALU.mult, ALU.mult)
                        if n >= 1:
                            ins = dve.tensor_tensor(gk[:, n - 1, :], src[:], stat[:], ALU.mult)
                        if n == 2:
                            link(ins)
                            ins = dve.tensor_tensor(gk[HALF:P, 1, :], src[0:HALF, :], stat[0:HALF, :],
                                                    ALU.mult)
                        ins.then_inc(gqk_ready, 1)

                    gla_qk(0)
                    u, b, mm, em = (r[0:MH, :] for r in (row_u, row_b, row_m, row_e))
                    dve.wait_ge(ln_ready, 1)
                    link(dve.scalar_tensor_tensor(b, b, 0.0, mm, ALU.min, ALU.subtract))
                    link(dve.tensor_tensor_scan(b, b, b, 0.0, ALU.add, ALU.bypass))
                    dve.tensor_tensor(u, u, b, ALU.subtract).then_inc(rows_ready, 1)
                    dve.wait_ge(rows_ready, 1)
                    dve.tensor_tensor_scan(mm, u, u, 0.0, ALU.max, ALU.bypass).then_inc(rows_ready, 1)
                    dve.wait_ge(rows_ready, 2)
                    dve.tensor_tensor(em, b, mm, ALU.add).then_inc(rows_ready, 1)
                    dve.tensor_scalar(mm, mm, -1.0, None, ALU.mult).then_inc(rows_ready, 1)
                    gla_qk(1)
                    dve.wait_ge(ln_ready, 2)
                    z = p64[:].rearrange("p t s -> p (t s)")
                    link(dve.scalar_tensor_tensor(z, z, 0.0, p128[:].rearrange("p t s -> p (t s)"),
                                                  ALU.min, ALU.subtract))
                    for n in range(16):
                        c = z[:, n * 64:(n + 1) * 64]
                        ins = dve.tensor_tensor_scan(c, c, c, 0.0, ALU.add, ALU.bypass)
                    link(ins)
                    for src, dst, v in ((p64, p128, 64), (p128, p256, 128)):
                        q = src[:].rearrange("p t (n h v) -> p (t n) h v", h=2, v=v)
                        d = dst[:].rearrange("p t (n h v) -> p (t n) h v", h=2, v=v)
                        dve.tensor_copy(d[:, :, 0, :], q[:, :, 0, :])
                        link(dve.tensor_tensor(d[:, :, 1, :], q[:, :, 1, :],
                                               q[:, :, 0, v - 1:v].to_broadcast([P, S // v, v]),
                                               ALU.add))

                    def halves(t3, v):
                        return t3[:].rearrange("p t (n h v) -> p (t n) h v", h=2, v=v)

                    def exponents(n):
                        v = X_ORDER[n]
                        q = halves({128: p128, 256: p256}.get(v, p64), v)
                        d = halves(xs[n % X_SLOTS], v)
                        mid = q[:, :, 0, v - 1:v].to_broadcast([P, S // v, v])
                        ins = dve.tensor_tensor(d[:, :, 0, :], mid, q[:, :, 0, :], ALU.subtract)
                        if v <= 32:
                            ins = dve.tensor_tensor(d[:, :, 1, :], q[:, :, 1, :], mid, ALU.subtract)
                        ins.then_inc(e_ready, 1)

                    def factors(n):
                        v = X_ORDER[n]
                        d = halves(xs[n % X_SLOTS], v)
                        dve.wait_ge(exp_ready, n + 1)
                        dve.tensor_tensor(d[:, :, 0, :], d[:, :, 0, :], halves(gk, v)[:, :, 0, :],
                                          ALU.mult)
                        dve.tensor_tensor(d[:, :, 1, :], d[:, :, 1, :], halves(gq, v)[:, :, 1, :],
                                          ALU.mult).then_inc(xs_ready, 1)

                    for n in range(3):
                        exponents(n)
                    gla_qk(2)
                    dve.wait_ge(gqk_ready, 3)

                    def stage(n, c):
                        dve.wait_ge(chunk_done, c + 1)
                        dve.tensor_tensor(T[2 + n % 2][:], bank["v", n][:], stat[:],
                                          ALU.mult).then_inc(stage_ready, 1)

                    def turned(n, dst, cols=S):
                        dve.wait_ge(tile_full, full["turn", n])
                        src = bank["turn", n][:, 0:cols].rearrange("p (t c) -> p t c", c=P)
                        dve.tensor_copy(dst, src).then_inc(vtok_ready, 1)

                    for n in range(4):
                        if n < 3:
                            stage(n, C_GV + n)
                        if n >= 1:
                            turned(n - 1, gv[:, :, (n - 1) * P:n * P])
                        if n < 3:
                            factors(n)

                    def rot(n):
                        dve.wait_ge(chunk_done, C_ROT + n + 1)
                        dve.tensor_tensor(rqk[:, n, :], bank["rot", n][:], stat[:],
                                          ALU.mult).then_inc(rot_copied, 1)

                    def swap(n):
                        dve.wait_ge(tile_full, full["swap", n])
                        r = rqk[:, n, :]
                        if n >= 1:
                            dve.wait_ge(rot_ready, 2 * n)
                        dve.tensor_tensor(rtmp[:], sincos[:, 1, :], bank["swap", n][:],
                                          ALU.mult).then_inc(rot_ready, 1)
                        link(dve.tensor_tensor(r, r, sincos[:, 0, :], ALU.mult))
                        dve.tensor_tensor(r, r, rtmp[:], ALU.add).then_inc(rot_ready, 1)

                    def keys_moved():
                        dve.wait_ge(rot_ready, 6)
                        dve.tensor_copy(rqk[HALF:P, 3, :], rqk[0:HALF, 1, :]).then_inc(rot_ready, 1)

                    def conv(n):
                        dve.wait_ge(chunk_done, C_MQK + n + 1)
                        src, dst = bank["mqk", n], mqk[:, n, :]

                        def tap(j):
                            return pcol[:, R_CONV + 4 * j + n:R_CONV + 4 * j + n + 1]

                        dve.tensor_tensor(src[:], src[:], stat[:], ALU.mult).then_inc(conv_ready, 1)
                        dve.wait_ge(conv_ready, 5 * n + 1)
                        dve.tensor_scalar(dst, src[:], tap(3), None, ALU.mult).then_inc(conv_ready, 1)
                        for e in range(1, 4):
                            dve.wait_ge(conv_ready, 5 * n + e + 1)
                            dve.scalar_tensor_tensor(dst[:, e:], src[:, 0:S - e], tap(3 - e),
                                                     dst[:, e:], ALU.mult, ALU.add)\
                               .then_inc(conv_ready, 1)

                    def rv_of(n):
                        turned(n, rv[:, :, (n - 3) * P:(n - 2) * P])

                    def mv_of(n):
                        turned(n, mv[:, :, (n - 6) * P:(n - 5) * P])

                    fill = [
                        [lambda: rot(0), lambda: rot(1), lambda: swap(0)],
                        [lambda: rot(2), lambda: swap(1)],
                        [lambda: stage(3, C_RV), lambda: (swap(2), keys_moved(), stage(4, C_RV + 1),
                                                          rv_of(3))],
                        [lambda: stage(5, C_RV + 2), lambda: (rv_of(4), conv(0), rv_of(5))],
                        [lambda: conv(1), lambda: conv(2)],
                        [lambda: conv(3), lambda: stage(6, C_MV)],
                        [lambda: stage(7, C_MV + 1)],
                    ]
                    for g in range(7):
                        for h in range(GH):
                            u_ = g * GH + h
                            dve.wait_ge(s_full, u_ + 1)
                            src = LB[u_ % 4][:].rearrange("p (t c) -> p t c", c=P)
                            if g == 0:
                                sel = ident.unsqueeze(1).to_broadcast([P, TB, P])
                                ins = dve.tensor_tensor(sdiag[:, h], src, sel, ALU.mult)
                            else:
                                dve.wait_ge(s_done, u_ - GH + 1)
                                sel = masks[:, g - 1, :].unsqueeze(1).to_broadcast([P, TB, P])
                                ins = dve.copy_predicated(sdiag[:, h], sel, src)
                            ins.then_inc(s_done, 1)
                            if g > 0 and h == 3:
                                fill[g - 1][-1]()
                        nxt = {1: (3, 4), 2: (5,), 3: (6,), 4: (7,), 5: (8,)}.get(g, ())
                        for n in nxt:
                            exponents(n)
                        for part in fill[g][:-1]:
                            part()
                        for n in nxt:
                            factors(n)
                    fill[6][-1]()
                    def gla_off(p):
                        for q in range(4):
                            n, e = divmod(q, 2)
                            dve.wait_ge(s_full, U_OFF + 4 * p + q + 1)
                            if p == 2:
                                dve.wait_ge(o_full, 2)
                            c = slice(0, S) if n == 0 else slice(S, S + 256)
                            dve.tensor_copy(sg[p % 2][:, e, c],
                                            bank["off", 4 * p + q][:, 0:c.stop - c.start])\
                               .then_inc(s_done, 1)

                    def gla_out(p):
                        dve.wait_ge(o_full, 2 * p + 2)
                        dve.tensor_copy(o_gla[:, p, :], OB[p % 2][:]).then_inc(o_taken, 1)

                    gla_off(0)
                    mv_of(6)
                    mv_of(7)
                    gla_off(1)
                    gla_off(2)
                    for p in range(3):
                        gla_out(p)

                    dve.wait_ge(tile_full, full["ucol"])
                    dve.tensor_copy(ucol[:].rearrange("p t h -> p (t h)"), bank["ucol"][:, 0:TB * MH])\
                       .then_inc(ucol_ready, 1)
                    dve.wait_ge(ucol_ready, 1)

                    def weight_log(n):
                        p, jt = divmod(n, TB)
                        for e in range(2):
                            if jt == 0:
                                dve.wait_ge(tile_full, full["negm", 2 * p + e])
                                dve.tensor_copy(negm[e][:], bank["negm", 2 * p + e][:])\
                                   .then_inc(negm_ready, 1)
                                dve.wait_ge(negm_ready, 2 * p + e + 1)
                            dve.tensor_scalar(T[2 + e][:, 0:S - jt * P], negm[e][:, jt * P:],
                                              ucol[:, jt, 2 * p + e:2 * p + e + 1], 0.0,
                                              ALU.add, ALU.min).then_inc(dlog_ready, 1)

                    def gate(n):
                        dve.wait_ge(chunk_done, C_GATE + n + 1)
                        dve.tensor_tensor(gates[:, n, :], bank["gate", n][:], stat[:], ALU.mult)\
                           .then_inc(gate_copied, 1)

                    def mem_part(k):
                        dve.wait_ge(tile_full, full["mem", k])
                        free(J_MEM + k)
                        dve.tensor_scalar(T[(J_MEM + k) % 2][:, 0:MEM], bank["mem", k][:, 0:MEM],
                                          pcol[:, R_MEM + k:R_MEM + k + 1], None, ALU.mult)\
                           .then_inc(val_ready, 1)
                        lo(J_MEM + k, memlo[:, k, :], memhi[:, k, :], MEM)

                    def ret_weigh(n):
                        p, jt = divmod(n, TB)
                        w = S - jt * P
                        dve.wait_ge(ret_full, n + 1)
                        dve.wait_ge(o_full, GH + ML_STEPS + max(n - 1, 0))
                        for e in range(2):
                            ins = dve.tensor_tensor(sm[2 * (n % 2) + e][:, 0:w], SB[e][:, 0:w],
                                                    decay[:, 2 * p + e, 0:w], ALU.mult)
                        ins.then_inc(ret_done, 1)

                    outputs = ([o_gla[:, p, :] for p in range(3)] + [o_ret[:, p, :] for p in range(3)]
                               + [o_ml[:, p, :] for p in range(2)])

                    def inverse_head_rms(p):
                        dve.wait_ge(post_rms, p + 1)
                        dve.reciprocal(hrms[p % 2][:], hrms[p % 2][:]).then_inc(head_rms, 1)

                    def norm_heads(p):
                        gain = R_GG + p if p < 3 else R_RG + p - 3
                        dve.wait_ge(tile_full, full["spread", p])
                        dve.scalar_tensor_tensor(outputs[p], outputs[p], pcol[:, gain:gain + 1],
                                                 bank["spread", p][:], ALU.mult, ALU.mult)\
                           .then_inc(normed, 1)
                        dve.wait_ge(normed, p + 1)

                    weight_log(0)
                    for n in range(ML_STEPS):
                        p, jt = divmod(n, TB)
                        w = S - jt * P
                        dve.wait_ge(ml_full, n + 1)
                        if n > 0:
                            dve.wait_ge(o_full, GH + n)
                        for e in range(2):
                            dve.wait_ge(dexp_ready, 2 * n + e + 1)
                            link(dve.scalar_tensor_tensor(sm[e][:, 0:w], SB[e][:, 0:w], MDK ** -0.5,
                                                          T[2 + e][:, 0:w], ALU.mult, ALU.mult))
                            ins = dve.tensor_tensor(sm[e][:, 0:P], sm[e][:, 0:P],
                                                    const[:, K_CAUSAL:K_CAUSAL + P], ALU.mult)
                        ins.then_inc(ml_done, 1)
                        if n - 1 in GLA_NORMS:
                            inverse_head_rms(GLA_NORMS[n - 1])
                        if n + 1 < ML_STEPS and jt < TB - 1:
                            weight_log(n + 1)
                        gate(n)
                        if n - 1 in GLA_NORMS:
                            norm_heads(GLA_NORMS[n - 1])
                        if n == 1:
                            dve.wait_ge(mem_rms, 1)
                            link(dve.reciprocal(memst[:, 2:4], memst[:, 2:4]))
                            for t in range(2):
                                dve.tensor_scalar(memraw[:, t, :], memraw[:, t, :],
                                                  memst[:, 2 + t:3 + t], None, ALU.mult)\
                                   .then_inc(memn_ready, 1)
                        for k in MEM_TURNS.get(n, ()):
                            mem_part(k)
                        if jt == TB - 1:
                            if n + 1 < ML_STEPS:
                                weight_log(n + 1)
                            else:
                                ret_weigh(0)
                            dve.wait_ge(den_abs, p + 1)
                            dve.wait_ge(tile_full, full["em", p])
                            dve.tensor_tensor(rtmp[:], rtmp[:], bank["em", p][:], ALU.max)\
                               .then_inc(o_taken, 1)
                            dve.wait_ge(o_taken, 4 + 2 * p)
                            link(dve.reciprocal(rtmp[:], rtmp[:]))
                            dve.tensor_tensor(o_ml[:, p, :], rtmp[:], OB[0][:], ALU.mult)\
                               .then_inc(o_taken, 1)

                    def post(p, step):
                        if step == 0:
                            dve.wait_ge(tile_full, full["mean", p])
                            dve.tensor_tensor(outputs[p], outputs[p], bank["mean", p][:],
                                              ALU.subtract).then_inc(xc_ready, 1)
                        else:
                            if step == 1:
                                norm_heads(p)
                            gated(p, outputs[p])

                    def gated(p, o):
                        job = J_FEAT + FEAT_ORDER.index(p)
                        dve.wait_ge(gate_ready, p + 1)
                        free(job)
                        dve.tensor_tensor(T[job % 2][:], o, gates[:, p, :], ALU.mult)\
                           .then_inc(val_ready, 1)
                        lo(job, xl[:, p, :], xh[:, p, :])

                    for m in range(17):
                        if POST.get(m - 1, (0, 0))[1] == 1:
                            inverse_head_rms(POST[m - 1][0])
                        if m % TB == 0 and 0 < m <= RET_STEPS:
                            p = m // TB - 1
                            dve.wait_ge(o_full, GH + ML_STEPS + m)
                            dve.tensor_copy(o_ret[:, p, :], OB[(7 + p) % 2][:]).then_inc(o_taken, 1)
                        if m < 8:
                            dve.wait_ge(chunk_done, C_K + m + 1)
                            dve.tensor_copy(kx[:, m, :], bank["kx", m][:, 0:MEM]).then_inc(kx_ready, 1)
                        elif m < 16:
                            dve.wait_ge(chunk_done, C_K + m + 1)
                            dve.tensor_copy(T[2 + m % 2][:, 0:MEM], bank["v", m][:, 0:MEM])\
                               .then_inc(stage_ready, 1)
                        if m + 1 < RET_STEPS:
                            ret_weigh(m + 1)
                        if m > 8:
                            turned(m - 1, vx[:, :, (m - 9) * P:(m - 8) * P], MEM)
                        if m - 1 in POST:
                            post(*POST[m - 1])

                    update_x(lambda m: C_OUT + m, lambda m: ("proj", C_OUT + m), 1.0,
                             J_XA, R_XA, ah, al)

                    inverse_rms(2)
                    for kind, n in XA_STEPS:
                        if kind == "query":
                            dve.wait_ge(chunk_done, C_Q + n + 1)
                            dve.tensor_tensor(qx[:, n, :], bank["proj", C_Q + n][:], stat[:], ALU.mult)\
                               .then_inc(qx_ready, 1)
                        elif kind == "scores":
                            st = smx[:, n % 2, :]
                            dve.wait_ge(s_full, U_XA + n + 1)
                            link(dve.tensor_reduce(
                                st[:, 0:2], SB[(U_XA + n) % 2][:].rearrange("p (s m) -> p s m", s=2),
                                AX.X, ALU.max))
                            dve.tensor_scalar(st[:, 0:2], st[:, 0:2], -XDH ** -0.5, None, ALU.mult)\
                               .then_inc(max_ready, 1)
                            dve.wait_ge(prob_exp, 2 * n + 2)
                            dve.reciprocal(st[:, 2:4], st[:, 2:4]).then_inc(s_done, 1)
                            dve.wait_ge(s_done, U_XA + n + 1)
                            for s in range(2):
                                dve.tensor_scalar(prob[n % 2][:, s, :], prob[n % 2][:, s, :],
                                                  st[:, 2 + s:3 + s], None, ALU.mult)\
                                   .then_inc(prob_ready, 1)
                        elif kind == "turn":
                            h, pair = divmod(n, 2)
                            dve.wait_ge(tile_full, full["pt", n])
                            dve.tensor_copy(pt[h][:, :, pair * 256:(pair + 1) * 256],
                                            bank["pt", n][:].rearrange("p (m c) -> p m c", m=2))\
                               .then_inc(pt_ready, 1)
                        else:
                            for k in (2 * n, 2 * n + 1):
                                dve.wait_ge(tile_full, full["att", k])
                                free(J_ATT + k)
                                dve.tensor_copy(T[(J_ATT + k) % 2][:], bank["att", k][:])\
                                   .then_inc(val_ready, 1)
                                lo(J_ATT + k, al[:, k, :], ah[:, k, :])
                    update_x(lambda m: C_O + m, lambda m: ("proj", C_O + m), 1.0,
                             J_FFB, R_FFB, xh, xl)
                    ffn(C_FFB, J_HB, 3, NJ)

            for s in loop_sems:
                nc.gpsimd.sem_clear(s)
            nc.all_engine_barrier()

        with nc.Block() as block:
            @block.sync
            def _(sp):
                for q in range(4):
                    sp.wait_ge(y_ready, (q + 1) * KT // 4)
                    c = slice(q * D // 4, (q + 1) * D // 4)
                    sp.dma_start(out_tok[:, :, c], yout[:, :, c]).then_inc(y_out, 16)
                sp.wait_ge(y_out, 64)
                for w in w_first:
                    sp.wait_ge(w, 16 * (DEPTH + 1))

            @block.scalar
            def _(act):
                def gained(k):
                    if k >= 2:
                        act.wait_ge(y_pe, k)
                    g = DEPTH * N_ROWS + k
                    act.activation(yk[k % 2][:], x[:, k, :], ACT.Copy, scale=pcols[:, g:g + 1])\
                       .then_inc(y_gained, 1)

                gained(0)
                act.wait_ge(y_pe, 1)
                act.activation(memst[:], psum[0][:, 0:TB], ACT.Sqrt, bias=eps).then_inc(y_act, 1)
                for k in range(1, KT):
                    gained(k)

            @block.tensor
            def _(pe):
                for t in range(TB):
                    m = pe.matmul(psum[0][:, t:t + 1], stat[:, t * P:(t + 1) * P],
                                  const[:, K_MEAN:K_MEAN + 1], start=True, stop=True)
                m.then_inc(y_pe, 1)
                for k in range(KT):
                    pe.wait_ge(y_gained, k + 1)
                    if k >= 7:
                        pe.wait_ge(y_ready, k - 6)
                    for t in range(TB):
                        m = pe.transpose(psum[1 + k % 7][:, t * P:(t + 1) * P],
                                         yk[k % 2][:, t * P:(t + 1) * P], ident)
                    m.then_inc(y_pe, 1)

            @block.vector
            def _(dve):
                dve.wait_ge(y_act, 1)
                dve.reciprocal(memst[:], memst[:]).then_inc(y_act, 1)
                dve.wait_ge(y_act, 2)
                for k in range(KT):
                    dve.wait_ge(y_pe, 2 + k)
                    dve.tensor_tensor(yout[:, :, k * P:(k + 1) * P],
                                      psum[1 + k % 7][:].rearrange("p (t c) -> p t c", c=P),
                                      memst[:].unsqueeze(2).to_broadcast([P, TB, P]), ALU.mult)\
                       .then_inc(y_ready, 1)


_INS = ["x", "mem", "positions", "g_ffa", "w_ffa_gu", "w_ffa_down", "g_mix", "w_in", "gla_w_a2",
        "gla_b_a", "gla_g_norm", "ret_g_norm", "ml_conv", "ml_b_i", "ml_b_f", "w_out", "g_xa",
        "g_mem", "w_xa_q", "w_xa_kv", "w_xa_o", "g_ffb", "w_ffb_gu", "w_ffb_down", "g_final"]


def kernel(**inputs):
    import numpy as _np
    import concourse.bacc as _bacc
    from concourse import mybir as _mybir
    from concourse.bass_utils import run_bass_kernel_spmd as _run

    nc = _bacc.Bacc("TRN2", target_bir_lowering=False, num_devices=1)
    c, decay, masks = constants()
    given = {n: _np.ascontiguousarray(inputs[n]) for n in _INS}
    given |= {"c_const": c, "c_decay": decay, "c_masks": masks}
    arrays, args = {}, {}
    for name, a in given.items():
        arrays[f"in_{name}_dram"] = a
        args[name] = nc.dram_tensor(f"in_{name}_dram", a.shape, _mybir.dt.from_np(a.dtype),
                                    kind="ExternalInput").ap()
    out = nc.dram_tensor("out_0_dram", (1, S, D), _mybir.dt.float32, kind="ExternalOutput").ap()
    build(nc, args, out)
    r = _run(nc, [arrays], core_ids=[0])
    return r.results[0]["out_0_dram"]
```
